# Optimizing a Trainium2 kernel written in Bass

```python
import math
import jax
import jax.numpy as jnp
from jax import lax
import numpy as np
import jax, jax.numpy as jnp

D_MODEL = 1024
BATCH = 1
SEQ = 512
DEPTH = 2

Q_BLOCK = 128
LN_EPS = 1e-5
RMS_EPS = 1e-5
N_BUCKETS = 32
MAX_DISTANCE = 2048
N_BIAS_COLS = 16
A_HEADS = 4
A_QK = 64
A_V = 128
B_PAIRS = ((128, 1), (512, 4), (2048, 16))
B_HEADS = 4
B_DIM = 64
C_HEADS = 8
C_KV_GROUPS = 2
C_DIM = 64
CMP_LEN = 32
CMP_STRIDE = 16
CMP_HIDDEN = 256
SLC_BLOCK = 64
SLC_TOP_N = 16
SLC_Q_CHUNK = 32
WIN_SIZE = 512
D_HEADS = 8
D_Q_LORA = 384
D_KV_LORA = 256
D_NOPE = 64
D_ROPE = 32
D_V = 64
ROPE_THETA = 10000.0
D_FF = 2816
CONV_W = 3

EVEN_SPLITS = (2 * A_HEADS * A_QK, 2 * A_HEADS * A_QK, A_HEADS * A_V, len(B_PAIRS) * 3 * B_HEADS * B_DIM)
EVEN_IN = sum(EVEN_SPLITS)
EVEN_OUT = A_HEADS * A_V + B_HEADS * B_DIM
ODD_SPLITS = (C_HEADS * C_DIM, 3 * 2 * C_KV_GROUPS * C_DIM, 3 * C_HEADS, D_Q_LORA, D_KV_LORA, D_ROPE)
ODD_IN = sum(ODD_SPLITS)
ODD_OUT = C_HEADS * C_DIM + D_HEADS * D_V


def split_cols(h, sizes):
    outs, off = [], 0
    for s in sizes:
        outs.append(h[..., off:off + s])
        off += s
    return outs

def layer_norm(x, g, b):
    xf = x.astype(jnp.float32)
    mu = jnp.mean(xf, -1, keepdims=True)
    var = jnp.mean(jnp.square(xf - mu), -1, keepdims=True)
    return ((xf - mu) * lax.rsqrt(var + LN_EPS) * g + b).astype(x.dtype)

def rms_norm(x, g):
    xf = x.astype(jnp.float32)
    return (xf * lax.rsqrt(jnp.mean(xf * xf, -1, keepdims=True) + RMS_EPS) * g).astype(x.dtype)

def t5_bucket(dist):
    max_exact = N_BUCKETS // 2
    n = jnp.maximum(dist, 0)
    nf = jnp.maximum(n, 1).astype(jnp.float32)
    large = max_exact + (jnp.log(nf / max_exact) / math.log(MAX_DISTANCE / max_exact) * (N_BUCKETS - max_exact)).astype(jnp.int32)
    return jnp.where(n < max_exact, n, jnp.minimum(large, N_BUCKETS - 1))

def rope(x, pos):
    half = x.shape[-1] // 2
    inv = ROPE_THETA ** (-jnp.arange(half, dtype=jnp.float32) / half)
    ang = pos.astype(jnp.float32)[:, None] * inv
    ang = ang.reshape(ang.shape[:1] + (1,) * (x.ndim - 3) + (half,))
    cos, sin = jnp.cos(ang), jnp.sin(ang)
    xf = x.astype(jnp.float32)
    x1, x2 = xf[..., :half], xf[..., half:]
    return jnp.concatenate([x1 * cos - x2 * sin, x1 * sin + x2 * cos], -1).astype(x.dtype)

def banded_attention(q, k, v, max_dist, bias_tbl, dist_scale):
    N, L, G, Hg, D = q.shape
    blk = Q_BLOCK
    n_prev = -(-max_dist // blk)
    nb = -(-L // blk)
    pad = nb * blk - L
    qb = jnp.pad(q, ((0, 0), (0, pad), (0, 0), (0, 0), (0, 0))).reshape(N, nb, blk, G, Hg, D)
    kv_pad = ((0, 0), (n_prev * blk, pad), (0, 0), (0, 0))
    kb = jnp.pad(k, kv_pad).reshape(N, nb + n_prev, blk, G, D)
    vb = jnp.pad(v, kv_pad).reshape(N, nb + n_prev, blk, G, v.shape[-1])
    kw = jnp.concatenate([kb[:, j:j + nb] for j in range(n_prev + 1)], axis=2)
    vw = jnp.concatenate([vb[:, j:j + nb] for j in range(n_prev + 1)], axis=2)
    n_keys = (n_prev + 1) * blk
    kj = jnp.arange(n_keys)
    dist = jnp.arange(blk)[:, None] + n_prev * blk - kj[None, :]
    kpos = (jnp.arange(nb) * blk)[:, None, None] - n_prev * blk + kj[None, None, :]
    valid = (dist >= 0) & (dist <= max_dist) & (kpos >= 0)
    bias = bias_tbl[t5_bucket(dist * dist_scale)].transpose(2, 3, 0, 1)
    s = jnp.einsum('nbqghd,nbkgd->nbghqk', qb, kw).astype(jnp.float32) * (D ** -0.5) + bias
    s = jnp.where(valid[:, None, None], s, -jnp.inf)
    m = jnp.max(s, -1, keepdims=True)
    p = jnp.exp(s - m)
    den = jnp.sum(p, -1, keepdims=True)
    o = jnp.einsum('nbghqk,nbkgd->nbqghd', (p / den).astype(v.dtype), vw)
    lse = (m + jnp.log(den))[..., 0].transpose(0, 1, 4, 2, 3)
    o = o.reshape(N, nb * blk, G, Hg, v.shape[-1])[:, :L]
    lse = lse.reshape(N, nb * blk, G, Hg)[:, :L]
    return o, lse

def diff_attention(q, k, v, lam, bias_tbl):
    B, S, _, H, Dk = q.shape
    nb = S // Q_BLOCK
    kpos = jnp.arange(S)
    qb = q.reshape(B, nb, Q_BLOCK, 2, H, Dk).swapaxes(0, 1)

    def step(args):
        qi, start = args
        dist = (start + jnp.arange(Q_BLOCK))[:, None] - kpos[None, :]
        bias = bias_tbl[t5_bucket(dist)].transpose(2, 0, 1)
        s = jnp.einsum('bqmhd,bkmhd->bmhqk', qi, k).astype(jnp.float32) * (Dk ** -0.5) + bias
        s = jnp.where(dist >= 0, s, -jnp.inf)
        p = jax.nn.softmax(s, axis=-1)
        w = p[:, 0] - lam * p[:, 1]
        return jnp.einsum('bhqk,bkhd->bqhd', w.astype(v.dtype), v)

    o = lax.map(step, (qb, jnp.arange(nb) * Q_BLOCK))
    return o.swapaxes(0, 1).reshape(B, S, H, v.shape[-1])

def to_residue(t, d):
    B, S, H, D = t.shape
    return t.reshape(B, S // d, d, H, D).transpose(0, 2, 1, 3, 4).reshape(B * d, S // d, H, D)

def dilated_mixture(hb, bias_table):
    B, S = hb.shape[:2]
    outs, lses = [], []
    for i, (window, d) in enumerate(B_PAIRS):
        M = S // d
        col = A_HEADS + i * B_HEADS
        tbl = bias_table[:, col:col + B_HEADS][:, :, None]
        o, lse = banded_attention(to_residue(hb[:, :, i, 0], d)[:, :, :, None], to_residue(hb[:, :, i, 1], d),
                                  to_residue(hb[:, :, i, 2], d), window // d, tbl, d)
        outs.append(o.reshape(B, d, M, B_HEADS, B_DIM).transpose(0, 2, 1, 3, 4).reshape(B, S, B_HEADS, B_DIM))
        lses.append(lse.reshape(B, d, M, B_HEADS).transpose(0, 2, 1, 3).reshape(B, S, B_HEADS))
    wts = jax.nn.softmax(jnp.stack(lses), axis=0)
    return jnp.einsum('pbsh,pbshd->bshd', wts.astype(outs[0].dtype), jnp.stack(outs))

def nsa_compress(t, pe, w1, w2):
    B, S, G, D = t.shape
    ch = t.reshape(B, S // CMP_STRIDE, CMP_STRIDE, G, D)
    blocks = jnp.concatenate([ch[:, :-1], ch[:, 1:]], axis=2)
    blocks = blocks + pe[:, None, :]
    flat = blocks.transpose(0, 1, 3, 2, 4).reshape(B, blocks.shape[1], G, CMP_LEN * D)
    return jax.nn.gelu(flat @ w1) @ w2

def nsa_compressed(q, k, v, pe, w1, w2, tbl):
    B, S, G, Hg, D = q.shape
    kc = nsa_compress(k, pe[0], w1[0], w2[0])
    vc = nsa_compress(v, pe[1], w1[1], w2[1])
    ncb = kc.shape[1]
    kend = jnp.arange(ncb) * CMP_STRIDE + CMP_LEN - 1
    dist = jnp.arange(S)[:, None] - kend[None, :]
    bias = tbl[t5_bucket(dist)].transpose(2, 3, 0, 1)
    s = jnp.einsum('bqghd,bcgd->bghqc', q, kc).astype(jnp.float32) * (D ** -0.5) + bias
    s = jnp.where(dist >= 0, s, -jnp.inf)
    m = jnp.max(s, -1, keepdims=True)
    p = jnp.exp(s - jnp.where(jnp.isfinite(m), m, 0.0))
    den = jnp.sum(p, -1, keepdims=True)
    p = p / jnp.where(den > 0, den, 1.0)
    o = jnp.einsum('bghqc,bcgd->bqghd', p.astype(v.dtype), vc)
    n_sel = S // SLC_BLOCK
    r = SLC_BLOCK // CMP_STRIDE
    pg = jnp.sum(p, axis=2)
    pp = jnp.pad(pg, ((0, 0), (0, 0), (0, 0), (1, r * (n_sel + 1) - 1 - ncb))).reshape(B, G, S, n_sel + 1, r)
    score = 0.5 * pp[..., :-1, 0] + jnp.sum(pp[..., :-1, 1:], -1) + 0.5 * pp[..., 1:, 0]
    return o, score

def nsa_selected(q, k, v, slc_score, tbl):
    B, S, G, Hg, D = q.shape
    n_sel = S // SLC_BLOCK
    top_n = min(SLC_TOP_N, n_sel)
    qblk = jnp.arange(S) // SLC_BLOCK
    jb = jnp.arange(n_sel)[None, :]
    allowed = jb <= qblk[:, None]
    forced = (jb == 0) | (jb == qblk[:, None]) | (jb == qblk[:, None] - 1)
    score = jnp.where(forced, jnp.inf, jnp.where(allowed, slc_score.astype(jnp.float32), -jnp.inf))
    _, idx = lax.top_k(score, top_n)
    kb = k.reshape(B, n_sel, SLC_BLOCK, G, D).transpose(0, 3, 1, 2, 4)
    vb = v.reshape(B, n_sel, SLC_BLOCK, G, v.shape[-1]).transpose(0, 3, 1, 2, 4)
    nq = S // SLC_Q_CHUNK
    idx_c = idx.transpose(0, 2, 1, 3).reshape(B, nq, SLC_Q_CHUNK, G, top_n).swapaxes(0, 1)
    q_c = q.reshape(B, nq, SLC_Q_CHUNK, G, Hg, D).swapaxes(0, 1)
    bi = jnp.arange(B)[:, None, None, None]
    gi = jnp.arange(G)[None, None, :, None]
    tok = jnp.arange(SLC_BLOCK)

    def step(args):
        qi, ii, start = args
        kg = kb[bi, gi, ii]
        vg = vb[bi, gi, ii]
        qp = start + jnp.arange(SLC_Q_CHUNK)
        dist = qp[None, :, None, None, None] - (ii[..., None] * SLC_BLOCK + tok)
        bias = tbl[t5_bucket(dist), gi[..., None]]
        s = jnp.einsum('bqghd,bqgnkd->bqghnk', qi, kg).astype(jnp.float32) * (D ** -0.5) + jnp.moveaxis(bias, -1, 3)
        s = jnp.where((dist >= 0)[:, :, :, None], s, -jnp.inf)
        p = jax.nn.softmax(s.reshape(s.shape[:4] + (-1,)), axis=-1).astype(v.dtype)
        return jnp.einsum('bqghk,bqgkd->bqghd', p, vg.reshape(vg.shape[:3] + (-1, vg.shape[-1])))

    o = lax.map(step, (q_c, idx_c, jnp.arange(nq) * SLC_Q_CHUNK))
    return o.swapaxes(0, 1).reshape(B, S, G, Hg, v.shape[-1])

def mla_attention(q_nope, q_rope, k_nope, k_rope, v):
    B, S, H, _ = q_nope.shape
    nb = S // Q_BLOCK
    kpos = jnp.arange(S)
    scale = (D_NOPE + D_ROPE) ** -0.5

    def blocks(t):
        return t.reshape((B, nb, Q_BLOCK) + t.shape[2:]).swapaxes(0, 1)

    def step(args):
        qn, qr, start = args
        s = (jnp.einsum('bqhd,bkhd->bhqk', qn, k_nope) + jnp.einsum('bqhr,bkr->bhqk', qr, k_rope)).astype(jnp.float32) * scale
        s = jnp.where((start + jnp.arange(Q_BLOCK))[:, None] >= kpos[None, :], s, -jnp.inf)
        p = jax.nn.softmax(s, axis=-1).astype(v.dtype)
        return jnp.einsum('bhqk,bkhd->bqhd', p, v)

    o = lax.map(step, (blocks(q_nope), blocks(q_rope), jnp.arange(nb) * Q_BLOCK))
    return o.swapaxes(0, 1).reshape(B, S, H, v.shape[-1])

def even_mixer(x, w_in, w_out, lam_p, subln_g, bias_table, layer_idx):
    B, S, _ = x.shape
    qa, ka, va, hb = split_cols(x @ w_in, EVEN_SPLITS)
    qa = qa.reshape(B, S, 2, A_HEADS, A_QK)
    ka = ka.reshape(B, S, 2, A_HEADS, A_QK)
    va = va.reshape(B, S, A_HEADS, A_V)
    lam_init = 0.8 - 0.6 * math.exp(-0.3 * layer_idx)
    lp = lam_p.astype(jnp.float32)
    lam = jnp.exp(jnp.sum(lp[0] * lp[1])) - jnp.exp(jnp.sum(lp[2] * lp[3])) + lam_init
    o_a = diff_attention(qa, ka, va, lam, bias_table[:, :A_HEADS])
    o_a = rms_norm(o_a, subln_g) * (1.0 - lam_init)
    o_b = dilated_mixture(hb.reshape(B, S, len(B_PAIRS), 3, B_HEADS, B_DIM), bias_table)
    y = jnp.concatenate([o_a.reshape(B, S, -1), o_b.reshape(B, S, -1)], axis=-1)
    return y @ w_out

def odd_mixer(x, w_in, w_out, cmp_pe, cmp_w1, cmp_w2, q_norm_g, kv_norm_g, w_uq, w_uk, w_uv, bias_table):
    B, S, _ = x.shape
    G, Hg = C_KV_GROUPS, C_HEADS // C_KV_GROUPS
    q_c, kv_c, gate_c, cq, ckv, k_rope = split_cols(x @ w_in, ODD_SPLITS)
    q = q_c.reshape(B, S, G, Hg, C_DIM)
    kv = kv_c.reshape(B, S, 3, 2, G, C_DIM)
    gates = jax.nn.sigmoid(gate_c.astype(jnp.float32)).reshape(B, S, 3, G, Hg, 1).astype(x.dtype)
    tbl_c = bias_table[:, :C_HEADS].reshape(N_BUCKETS, G, Hg)
    o_cmp, slc_score = nsa_compressed(q, kv[:, :, 0, 0], kv[:, :, 0, 1], cmp_pe, cmp_w1, cmp_w2, tbl_c)
    o_slc = nsa_selected(q, kv[:, :, 1, 0], kv[:, :, 1, 1], slc_score, tbl_c)
    o_win, _ = banded_attention(q, kv[:, :, 2, 0], kv[:, :, 2, 1], WIN_SIZE - 1, tbl_c, 1)
    o_c = gates[:, :, 0] * o_cmp + gates[:, :, 1] * o_slc + gates[:, :, 2] * o_win
    pos = jnp.arange(S)
    qd = (rms_norm(cq, q_norm_g) @ w_uq).reshape(B, S, D_HEADS, D_NOPE + D_ROPE)
    c = rms_norm(ckv, kv_norm_g)
    k_nope = (c @ w_uk).reshape(B, S, D_HEADS, D_NOPE)
    v = (c @ w_uv).reshape(B, S, D_HEADS, D_V)
    o_d = mla_attention(qd[..., :D_NOPE], rope(qd[..., D_NOPE:], pos), k_nope, rope(k_rope, pos), v)
    y = jnp.concatenate([o_c.reshape(B, S, -1), o_d.reshape(B, S, -1)], axis=-1)
    return y @ w_out

def conv_ffn(x, w_up, conv_w, conv_b, w_down):
    a, g = jnp.split(x @ w_up, 2, axis=-1)
    g = lax.conv_general_dilated(g, conv_w[:, None, :].astype(g.dtype), window_strides=(1,),
                                 padding=((CONV_W - 1, 0),), dimension_numbers=('NWC', 'WIO', 'NWC'),
                                 feature_group_count=D_FF) + conv_b
    return (jax.nn.gelu(g) * a) @ w_down

def first_inputs(seed: int = 0) -> dict:
    key = jax.random.key(seed)
    ks = jax.random.split(key, 22)
    f32 = jnp.float32
    n_ev, n_od = (DEPTH + 1) // 2, DEPTH // 2
    beta = (8 * DEPTH) ** -0.25

    def w(k, shape, fan_in, gain=1.0):
        return jax.random.normal(k, shape, f32) * (gain * fan_in ** -0.5)

    def near_one(k, shape):
        return 1.0 + 0.02 * jax.random.normal(k, shape, f32)

    def small(k, shape, std):
        return std * jax.random.normal(k, shape, f32)

    return {
        'x': jax.random.normal(ks[0], (BATCH, SEQ, D_MODEL), f32),
        'rel_bias': small(ks[1], (N_BUCKETS, N_BIAS_COLS), 0.2),
        'ev_w_in': w(ks[2], (n_ev, D_MODEL, EVEN_IN), D_MODEL),
        'ev_w_out': w(ks[3], (n_ev, EVEN_OUT, D_MODEL), EVEN_OUT, beta),
        'ev_lambda': small(ks[4], (n_ev, 4, A_QK), 0.1),
        'ev_subln': near_one(ks[5], (n_ev, A_V)),
        'od_w_in': w(ks[6], (n_od, D_MODEL, ODD_IN), D_MODEL),
        'od_w_out': w(ks[7], (n_od, ODD_OUT, D_MODEL), ODD_OUT, beta),
        'od_cmp_pe': small(ks[8], (n_od, 2, CMP_LEN, C_DIM), 0.1),
        'od_cmp_w1': w(ks[9], (n_od, 2, CMP_LEN * C_DIM, CMP_HIDDEN), CMP_LEN * C_DIM),
        'od_cmp_w2': w(ks[10], (n_od, 2, CMP_HIDDEN, C_DIM), CMP_HIDDEN),
        'od_q_norm': near_one(ks[11], (n_od, D_Q_LORA)),
        'od_kv_norm': near_one(ks[12], (n_od, D_KV_LORA)),
        'od_w_uq': w(ks[13], (n_od, D_Q_LORA, D_HEADS * (D_NOPE + D_ROPE)), D_Q_LORA),
        'od_w_uk': w(ks[14], (n_od, D_KV_LORA, D_HEADS * D_NOPE), D_KV_LORA),
        'od_w_uv': w(ks[15], (n_od, D_KV_LORA, D_HEADS * D_V), D_KV_LORA),
        'ffn_w_up': w(ks[16], (DEPTH, D_MODEL, 2 * D_FF), D_MODEL),
        'ffn_conv_w': w(ks[17], (DEPTH, CONV_W, D_FF), CONV_W),
        'ffn_conv_b': small(ks[18], (DEPTH, D_FF), 0.02),
        'ffn_w_down': w(ks[19], (DEPTH, D_FF, D_MODEL), D_FF, beta),
        'ln_g': near_one(ks[20], (DEPTH, 2, D_MODEL)),
        'ln_b': small(ks[21], (DEPTH, 2, D_MODEL), 0.02),
    }

def first_block(x, rel_bias, ev_w_in, ev_w_out, ev_lambda, ev_subln, od_w_in, od_w_out, od_cmp_pe, od_cmp_w1,
              od_cmp_w2, od_q_norm, od_kv_norm, od_w_uq, od_w_uk, od_w_uv, ffn_w_up, ffn_conv_w, ffn_conv_b,
              ffn_w_down, ln_g, ln_b):
    alpha = (2 * DEPTH) ** 0.25
    for l in range(DEPTH):
        i = l // 2
        if l % 2 == 0:
            y = even_mixer(x, ev_w_in[i], ev_w_out[i], ev_lambda[i], ev_subln[i], rel_bias, l)
        else:
            y = odd_mixer(x, od_w_in[i], od_w_out[i], od_cmp_pe[i], od_cmp_w1[i], od_cmp_w2[i], od_q_norm[i],
                          od_kv_norm[i], od_w_uq[i], od_w_uk[i], od_w_uv[i], rel_bias)
        x = layer_norm(alpha * x + y, ln_g[l, 0], ln_b[l, 0])
        y = conv_ffn(x, ffn_w_up[l], ffn_conv_w[l], ffn_conv_b[l], ffn_w_down[l])
        x = layer_norm(alpha * x + y, ln_g[l, 1], ln_b[l, 1])
    return x


N_MIXERS = 2
N_LRU = (DEPTH + 1) // 2
N_RET = DEPTH // 2

D_RNN = 3 * D_MODEL // 2
N_GATE_BLOCKS = 16
BLOCK_W = D_RNN // N_GATE_BLOCKS
CONV_W_2 = 4
C_RG = 8.0

RET_HEADS = D_MODEL // 256
QK_HEAD = 256
V_HEAD = 2 * QK_HEAD
QK_DIM = RET_HEADS * QK_HEAD
V_DIM = RET_HEADS * V_HEAD
CHUNK = 128
ROPE_BASE = 10000.0

RMS_EPS_2 = 1e-6
GN_EPS = 1e-5


def rms_norm_2(x, g):
    xf = x.astype(jnp.float32)
    y = xf * lax.rsqrt(jnp.mean(xf * xf, axis=-1, keepdims=True) + RMS_EPS_2)
    return (y * g.astype(jnp.float32)).astype(x.dtype)

def causal_depthwise_conv(x, w, b):
    s = x.shape[1]
    xp = jnp.pad(x, ((0, 0), (CONV_W_2 - 1, 0), (0, 0)))
    y = b
    for k in range(CONV_W_2):
        y = y + xp[:, k:k + s] * w[k]
    return y

def _lin_rec_combine(e1, e2):
    a1, b1 = e1
    a2, b2 = e2
    return a1 * a2, a2 * b1 + b2

def rglru_mixer(h, w_in, conv_w, conv_b, w_a, b_a, w_x, b_x, lam, w_out):
    bsz, s, _ = h.shape
    u = h @ w_in
    xb, gate = u[..., :D_RNN], u[..., D_RNN:]
    xb = causal_depthwise_conv(xb, conv_w, conv_b)
    xblk = xb.reshape(bsz, s, N_GATE_BLOCKS, BLOCK_W)
    r = jax.nn.sigmoid(jnp.einsum('bsnc,ncd->bsnd', xblk, w_a).reshape(bsz, s, D_RNN) + b_a)
    i = jax.nn.sigmoid(jnp.einsum('bsnc,ncd->bsnd', xblk, w_x).reshape(bsz, s, D_RNN) + b_x)
    log_a = -C_RG * r.astype(jnp.float32) * jax.nn.softplus(-lam.astype(jnp.float32))
    a = jnp.exp(log_a)
    bt = jnp.sqrt(-jnp.expm1(2.0 * log_a)) * (i * xb).astype(jnp.float32)
    _, hseq = lax.associative_scan(_lin_rec_combine, (a, bt), axis=1)
    y = hseq.astype(h.dtype) * jax.nn.silu(gate)
    return y @ w_out

def apply_rotary(x, cos, sin):
    half = x.shape[-1] // 2
    x1, x2 = x[..., :half], x[..., half:]
    c = cos[None, :, None, :]
    s_ = sin[None, :, None, :]
    return jnp.concatenate([x1 * c - x2 * s_, x2 * c + x1 * s_], axis=-1)

def retention_mixer(h, w_in, w_out, cos, sin):
    bsz, s, _ = h.shape
    n_chunks = s // CHUNK
    u = h @ w_in
    q = u[..., :QK_DIM].reshape(bsz, s, RET_HEADS, QK_HEAD).astype(jnp.float32)
    k = u[..., QK_DIM:2 * QK_DIM].reshape(bsz, s, RET_HEADS, QK_HEAD).astype(jnp.float32)
    v = u[..., 2 * QK_DIM:2 * QK_DIM + V_DIM].reshape(bsz, s, RET_HEADS, V_HEAD).astype(jnp.float32)
    gate = u[..., 2 * QK_DIM + V_DIM:]
    q = apply_rotary(q, cos, sin)
    k = apply_rotary(k, cos, sin) * (QK_HEAD ** -0.5)

    def to_chunks(t):
        return t.reshape(bsz, n_chunks, CHUNK, RET_HEADS, t.shape[-1]).transpose(1, 0, 3, 2, 4)

    qc, kc, vc = to_chunks(q), to_chunks(k), to_chunks(v)

    log_g = jnp.log(1.0 - jnp.exp2(-5.0 - jnp.arange(RET_HEADS, dtype=jnp.float32)))
    idx = jnp.arange(CHUNK, dtype=jnp.float32)
    diff = idx[:, None] - idx[None, :]
    dmask = jnp.where(diff[None] >= 0, jnp.exp(jnp.maximum(diff, 0.0)[None] * log_g[:, None, None]), 0.0)
    q_decay = jnp.exp((idx[None, :] + 1.0) * log_g[:, None])[..., None]
    k_decay = jnp.exp((CHUNK - 1.0 - idx[None, :]) * log_g[:, None])[..., None]
    chunk_decay = jnp.exp(CHUNK * log_g)[:, None, None]

    def step(state, inp):
        qi, ki, vi = inp
        scores = jnp.einsum('bhqd,bhkd->bhqk', qi, ki) * dmask
        inner = jnp.einsum('bhqk,bhke->bhqe', scores, vi)
        cross = jnp.einsum('bhqd,bhde->bhqe', qi * q_decay, state)
        new_state = state * chunk_decay + jnp.einsum('bhkd,bhke->bhde', ki * k_decay, vi)
        return new_state, inner + cross

    state0 = jnp.zeros((bsz, RET_HEADS, QK_HEAD, V_HEAD), jnp.float32)
    _, out = lax.scan(step, state0, (qc, kc, vc))
    out = out.transpose(1, 0, 3, 2, 4).reshape(bsz, s, RET_HEADS, V_HEAD)
    mu = jnp.mean(out, axis=-1, keepdims=True)
    var = jnp.mean(jnp.square(out - mu), axis=-1, keepdims=True)
    out = ((out - mu) * lax.rsqrt(var + GN_EPS)).reshape(bsz, s, V_DIM).astype(h.dtype)
    y = out * jax.nn.silu(gate)
    return y @ w_out

def second_inputs(seed: int = 0) -> dict:
    key = jax.random.key(seed)
    ks = jax.random.split(key, 16)
    f32 = jnp.float32

    def nrm(k, shape, fan_in):
        return jax.random.normal(k, shape, f32) * (fan_in ** -0.5)

    x = jax.random.normal(ks[0], (BATCH, SEQ, D_MODEL), f32)
    norm_pre = 1.0 + 0.05 * jax.random.normal(ks[1], (DEPTH, D_MODEL), f32)
    norm_post = 1.0 + 0.05 * jax.random.normal(ks[2], (DEPTH, D_MODEL), f32)
    lru_w_in = nrm(ks[3], (N_LRU, D_MODEL, 2 * D_RNN), D_MODEL)
    lru_conv_w = nrm(ks[4], (N_LRU, CONV_W_2, D_RNN), CONV_W_2)
    lru_conv_b = 0.02 * jax.random.normal(ks[5], (N_LRU, D_RNN), f32)
    lru_w_a = nrm(ks[6], (N_LRU, N_GATE_BLOCKS, BLOCK_W, BLOCK_W), BLOCK_W)
    lru_b_a = 0.02 * jax.random.normal(ks[7], (N_LRU, D_RNN), f32)
    lru_w_x = nrm(ks[8], (N_LRU, N_GATE_BLOCKS, BLOCK_W, BLOCK_W), BLOCK_W)
    lru_b_x = 0.02 * jax.random.normal(ks[9], (N_LRU, D_RNN), f32)
    a_c = jax.random.uniform(ks[10], (N_LRU, D_RNN), f32, minval=0.9, maxval=0.999)
    sig = a_c ** (1.0 / C_RG)
    lru_lambda = jnp.log(sig) - jnp.log1p(-sig)
    lru_w_out = nrm(ks[11], (N_LRU, D_RNN, D_MODEL), D_RNN)
    ret_w_in = nrm(ks[12], (N_RET, D_MODEL, 2 * QK_DIM + 2 * V_DIM), D_MODEL)
    ret_w_out = nrm(ks[13], (N_RET, V_DIM, D_MODEL), V_DIM)
    return {"x": x, "norm_pre": norm_pre, "norm_post": norm_post,
            "lru_w_in": lru_w_in, "lru_conv_w": lru_conv_w, "lru_conv_b": lru_conv_b,
            "lru_w_a": lru_w_a, "lru_b_a": lru_b_a, "lru_w_x": lru_w_x, "lru_b_x": lru_b_x,
            "lru_lambda": lru_lambda, "lru_w_out": lru_w_out,
            "ret_w_in": ret_w_in, "ret_w_out": ret_w_out}

def second_block(x, norm_pre, norm_post, lru_w_in, lru_conv_w, lru_conv_b, lru_w_a, lru_b_a,
              lru_w_x, lru_b_x, lru_lambda, lru_w_out, ret_w_in, ret_w_out):
    s = x.shape[1]
    pos = jnp.arange(s, dtype=jnp.float32)
    inv_freq = ROPE_BASE ** (-jnp.arange(0, QK_HEAD, 2, dtype=jnp.float32) / QK_HEAD)
    ang = pos[:, None] * inv_freq[None, :]
    cos, sin = jnp.cos(ang), jnp.sin(ang)
    for layer in range(DEPTH):
        h = rms_norm_2(x, norm_pre[layer])
        j = layer // N_MIXERS
        if layer % N_MIXERS == 0:
            o = rglru_mixer(h, lru_w_in[j], lru_conv_w[j], lru_conv_b[j], lru_w_a[j], lru_b_a[j],
                            lru_w_x[j], lru_b_x[j], lru_lambda[j], lru_w_out[j])
        else:
            o = retention_mixer(h, ret_w_in[j], ret_w_out[j], cos, sin)
        x = x + rms_norm_2(o, norm_post[layer])
    return x


def setup_inputs(seed=0):
    out = dict(first_inputs(seed))
    for name, value in second_inputs(seed + 1).items():
        if name != "x":
            out[name + "_2"] = value
    return out


def reference(
    x, rel_bias, ev_w_in, ev_w_out, ev_lambda, ev_subln, od_w_in, od_w_out, od_cmp_pe,
    od_cmp_w1, od_cmp_w2, od_q_norm, od_kv_norm, od_w_uq, od_w_uk, od_w_uv, ffn_w_up,
    ffn_conv_w, ffn_conv_b, ffn_w_down, ln_g, ln_b, norm_pre_2, norm_post_2, lru_w_in_2,
    lru_conv_w_2, lru_conv_b_2, lru_w_a_2, lru_b_a_2, lru_w_x_2, lru_b_x_2, lru_lambda_2,
    lru_w_out_2, ret_w_in_2, ret_w_out_2,
):
    x = first_block(
        x, rel_bias, ev_w_in, ev_w_out, ev_lambda, ev_subln, od_w_in, od_w_out, od_cmp_pe,
        od_cmp_w1, od_cmp_w2, od_q_norm, od_kv_norm, od_w_uq, od_w_uk, od_w_uv, ffn_w_up,
        ffn_conv_w, ffn_conv_b, ffn_w_down, ln_g, ln_b,
    )
    return second_block(
        x, norm_pre_2, norm_post_2, lru_w_in_2, lru_conv_w_2, lru_conv_b_2, lru_w_a_2,
        lru_b_a_2, lru_w_x_2, lru_b_x_2, lru_lambda_2, lru_w_out_2, ret_w_in_2, ret_w_out_2,
    )


_drawn_inputs = setup_inputs


def setup_inputs(seed=0):
    import zlib

    import numpy as np

    out = dict(_drawn_inputs(seed))
    spreads = {}
    factors = {'ev_lambda': 6.4,
     'ev_subln': 3.508,
     'od_q_norm': 8.0,
     'od_kv_norm': 8.0,
     'ffn_conv_b': 5.13,
     'lru_b_a_2': 8.0,
     'lru_b_x_2': 7.3,
     'od_cmp_pe': 5.679}
    for name, (base, spread) in spreads.items():
        noise = np.random.default_rng([zlib.crc32(name.encode()), seed]).standard_normal(out[name].shape)
        drawn = base * np.exp(spread * noise) if base else spread * noise
        out[name] = jnp.asarray(drawn.astype(out[name].dtype))
    for name, factor in factors.items():
        out[name] = (out[name] * factor).astype(out[name].dtype)
    return out
```

```python
import math
from contextlib import ExitStack

import concourse.bass as bass
from concourse import mybir

F32 = mybir.dt.float32
ALU = mybir.AluOpType
ACT = mybir.ActivationFunctionType
AX_X = mybir.AxisListType.X

P = 128
D = 1024
S = 512
NT = S // P
CH = D // P
RING = 4
SLOT = 2048
NEG = -1.0e30
LN_EPS = 1e-5
RMS_EPS = 1e-5
RMS_EPS_2 = 1e-6
GN_EPS = 1e-5
DEPTH = 2
ALPHA = (2 * DEPTH) ** 0.25
LAM_INIT = 0.8 - 0.6 * math.exp(-0.3 * 0)

A_HEADS, A_QK, A_V = 4, 64, 128
B_HEADS, B_DIM, N_PAIRS = 4, 64, 3
C_HEADS, C_DIM, C_GROUPS = 8, 64, 2
CMP_BLOCKS, CMP_LEN, CMP_STRIDE, CMP_HIDDEN = 31, 32, 16, 256
D_HEADS, D_NOPE, D_ROPE, D_V = 8, 64, 32, 64
D_Q_LORA, D_KV_LORA = 384, 256
D_FF = 2816
FF_CH = D_FF // P
D_RNN = 1536
GATES, BW = 16, 96
C_RG = 8.0
R_HEADS, R_QK, R_V = 4, 256, 512

TOE = 640
STD, WIN, DIL4, DIL16 = range(4)
KINDS = 4
TCOLS = 17
CB_SPAN = 55
FWD_OFF = 511
FWD_LEN = FWD_OFF + 24 * CMP_STRIDE - 31 + P


class Stream:

    def __init__(self, nc, ctx):
        self.ring = ctx.enter_context(nc.sbuf_tensor("weight_ring", [P, RING, SLOT], F32))
        self.loaded = [ctx.enter_context(nc.semaphore(f"weights_loaded_{s}")) for s in range(RING)]
        self.used = ctx.enter_context(nc.semaphore("weights_used"))
        self.tiles = 0
        self.count = [0] * RING
        self.segments = []

    def segment(self, count, pieces, load):
        seg = {"start": self.tiles, "count": count, "pieces": pieces, "load": load, "base": list(self.count)}
        for t in range(count):
            self.count[(self.tiles + t) % RING] += 16 * pieces
        self.tiles += count
        self.segments.append(seg)
        return seg

    def issue(self, sp, seg, t, turn=None):
        n = seg["start"] + t
        slot = n % RING
        t_now = t if turn is None else turn * RING + t
        if n >= RING:
            sp.wait_ge(self.used, seg["start"] - RING + 1 + t_now)
        for dst, src in seg["load"](t_now, self.ring[:, slot, :]):
            sp.dma_start(dst, src).then_inc(self.loaded[slot], 16)

    def rest(self, sp, seg):
        turns = (seg["count"] - RING) // RING
        if turns > 1:
            with sp.Fori(0, turns) as turn:
                for t in range(RING, 2 * RING):
                    self.issue(sp, seg, t, turn)
        else:
            turns = 0
        for t in range(RING * (turns + 1), seg["count"]):
            self.issue(sp, seg, t)

    def first(self, sp, seg):
        for t in range(min(RING, seg["count"])):
            self.issue(sp, seg, t)

    def feed(self, sp, seg):
        self.rest(sp, seg)
        k = self.segments.index(seg)
        if k + 1 < len(self.segments):
            self.first(sp, self.segments[k + 1])

    def wait(self, pe, seg, t, turn=None):
        slot = (seg["start"] + t) % RING
        k = t // RING
        level = seg["base"][slot] + 16 * seg["pieces"] * (k + 1)
        pe.wait_ge(self.loaded[slot], level if turn is None else turn * (16 * seg["pieces"]) + level)
        return self.ring[:, slot, :]


def loop_tiles(eng, count, first, body):
    for t in range(first):
        body(t, None)
    turns = (count - first - 1) // RING
    if turns > 1:
        with eng.Fori(0, turns) as turn:
            for t in range(first, first + RING):
                body(t, turn)
    else:
        turns = 0
    for t in range(first + turns * RING, count):
        body(t, None)


def at(turn, step, t):
    return step * t if turn is None else turn * (step * RING) + step * t


class Program:
    def __init__(self, nc, ctx, a):
        self.nc, self.a = nc, a
        sb = lambda name, shape: ctx.enter_context(nc.sbuf_tensor(name, shape, F32))
        self.x = sb("residual", [P, CH, S])
        self.h = sb("mixer_in", [P, CH, S])
        self.ident = sb("ident", [P, P])
        self.mean_w = sb("mean_weights", [P, P])
        self.ln_g = sb("ln_gain", [P, 2 * DEPTH, CH])
        self.ln_b = sb("ln_shift", [P, 2 * DEPTH, CH])
        self.norm_pre = sb("norm_pre", [P, DEPTH, CH])
        self.norm_post = sb("norm_post", [P, DEPTH, CH])
        self.ps = ctx.enter_context(nc.psum_tensor("banks", [P, 8, S], F32))
        self.st = Stream(nc, ctx)
        self.rev = nc.dram_tensor("distance_rows", [KINDS, TCOLS, TOE], F32, kind="Internal")

    def plan(self):
        st, a = self.st, self.a

        def cols(w, col_of, width):
            w_v = w.rearrange("(c p) n -> p c n", p=P)
            chunks = w_v.shape[1]
            def load(t, slot):
                view = slot[:, 0:chunks * width].rearrange("p (c n) -> p c n", c=chunks)
                return [(view, w_v[:, :, bass.ds(col_of(t), width)])]
            return load

        def rows(w, kp):
            w_v = w.rearrange("(t c p) n -> p t c n", p=kp, c=2)
            def load(t, slot):
                view = slot[0:kp, :].rearrange("p (c n) -> p c n", c=2)
                return [(view, w_v[:, bass.ds(t, 1), :, :].rearrange("p t c n -> p (t c) n"))]
            return load

        def ffn_up(l):
            w_v = a["ffn_w_up"][l].rearrange("(c p) (s n) -> p c s n", p=P, s=2)
            def load(t, slot):
                view = slot.rearrange("p (c s n) -> p c s n", c=CH, s=2)
                return [(view[:, :, s, :], w_v[:, :, s, bass.ds(t * P, P)]) for s in range(2)]
            return load

        ev = a["ev_w_in"][0]
        self.seg_a = st.segment(6, 1, cols(ev, lambda t: t * 256, 256))
        self.seg_b = st.segment(9, 1, cols(ev, lambda t: (t + 6) * 256, 256))
        self.seg_ev_out = st.segment(3, 1, rows(a["ev_w_out"][0], P))
        self.seg_up, self.seg_down = [None, None], [None, None]
        self.seg_up[0] = st.segment(FF_CH, 2, ffn_up(0))
        self.seg_down[0] = st.segment(FF_CH // 2, 1, rows(a["ffn_w_down"][0], P))
        od = a["od_w_in"][0].rearrange("(c p) n -> p c n", p=P)
        C0 = 2 * 512 + 3 * 2 * 2 * 64 - 512
        gate0, cq0 = C0, C0 + 24
        ckv0 = cq0 + D_Q_LORA
        kr0 = ckv0 + D_KV_LORA
        self.od_tiles = [(0, 256), (256, 256), (512, 256), (768, 256), (1024, 256), (gate0, 24), (kr0, 32),
                         (cq0, 256), (cq0 + 256, 256), (cq0 + 512, 128)]
        def load_od(t, slot):
            c, w = self.od_tiles[t]
            return [(slot[:, 0:CH * w].rearrange("p (c n) -> p c n", c=CH), od[:, :, c:c + w])]
        self.seg_od = st.segment(len(self.od_tiles), 1, load_od)
        w1 = a["od_cmp_w1"][0].rearrange("s (u c p) n -> s u p c n", p=P, u=2)
        def load_w1(t, slot):
            return [(slot.rearrange("p (c n) -> p c n", c=8), w1[t // 2, t % 2])]
        self.seg_cmp = st.segment(4, 1, load_w1)
        uq = a["od_w_uq"][0].rearrange("(c p) n -> p c n", p=P)
        def load_mla(t, slot):
            if t < 2:
                return [(slot[:, 0:3 * 384].rearrange("p (c n) -> p c n", c=3), uq[:, :, 384 * t:384 * (t + 1)])]
            w = a["od_w_uk" if t == 2 else "od_w_uv"][0]
            return [(slot[:, 0:1024].rearrange("p (c n) -> p c n", c=2), w.rearrange("(c p) n -> p c n", p=P))]
        self.seg_mla = st.segment(4, 1, load_mla)
        self.seg_od_out = st.segment(4, 1, rows(a["od_w_out"][0], P))
        self.seg_up[1] = st.segment(FF_CH, 2, ffn_up(1))
        self.seg_down[1] = st.segment(FF_CH // 2, 1, rows(a["ffn_w_down"][1], P))
        lru = a["lru_w_in_2"][0].rearrange("(c p) (s n) -> p c s n", p=P, s=2)
        def load_lru(t, slot):
            view = slot[:, 0:CH * 2 * BW].rearrange("p (c s n) -> p c s n", c=CH, s=2)
            gates = [(slot[0:BW, CH * 2 * BW + s * BW:CH * 2 * BW + (s + 1) * BW],
                      a[n][0, bass.ds(t, 1)].rearrange("t p n -> p (t n)")) for s, n in enumerate(("lru_w_a_2", "lru_w_x_2"))]
            return [(view[:, :, s, :], lru[:, :, s, bass.ds(t * BW, BW)]) for s in range(2)] + gates
        self.seg_lru = st.segment(GATES, 4, load_lru)
        self.seg_lru_out = st.segment(GATES // 2, 1, rows(a["lru_w_out_2"][0], BW))
        ret = a["ret_w_in_2"][0]
        def ret_col(t):
            h, k = divmod(t, 6)
            return [256 * h, 1024 + 256 * h, 2048 + 512 * h, 2048 + 512 * h + 256,
                    4096 + 512 * h, 4096 + 512 * h + 256][k]
        self.seg_ret = [st.segment(6, 1, cols(ret, lambda t, h=h: ret_col(6 * h + t), 256)) for h in range(R_HEADS)]
        self.seg_ret_out = st.segment(R_HEADS * 2, 1, rows(a["ret_w_out_2"][0], P))


def start(g):
    nc, a, ps = g.nc, g.a, g.ps
    with ExitStack() as ctx:
        sb = lambda n, s: ctx.enter_context(nc.sbuf_tensor(n, s, F32))
        sem = lambda n: nc.alloc_semaphore(n)
        xt = sb("x_tokens", [P, NT, D])
        onehot = sb("onehot", [33, KINDS, TOE])
        tbl = sb("bias_table", [33, TCOLS])
        rows = sb("distance_rows_sb", [TCOLS, KINDS, TOE])
        x_in, small_in, const_in = sem("x_in"), sem("small_in"), sem("const_in")
        turned, kept, rows_done, rows_kept, rows_out, cleared = (
            sem("x_turned"), sem("x_kept"), sem("rows_done"), sem("rows_kept"), sem("rows_out"), sem("table_cleared"))
        block = ctx.enter_context(nc.Block())

        @block.sync
        def _(sp):
            sp.dma_start(xt[:], a["x"].rearrange("b (t p) d -> p (b t) d", p=P)).then_inc(x_in, 16)
            sp.dma_start(g.ident[:], a["c_ident"]).then_inc(x_in, 16)
            sp.dma_start(onehot[:], a["c_onehot"].rearrange("k b m -> b k m")).then_inc(const_in, 16)
            sp.wait_ge(cleared, 2)
            sp.dma_start(tbl[0:32, 0:16], a["rel_bias"]).then_inc(const_in, 16)
            g.st.first(sp, g.seg_a)
            for dst, src in ((g.ln_g, "f_ln_g"), (g.ln_b, "f_ln_b"), (g.norm_pre, "f_norm_pre"), (g.norm_post, "f_norm_post")):
                sp.dma_start(dst[:], a[src]).then_inc(small_in, 16)
            sp.wait_ge(rows_kept, 2 * KINDS)
            sp.dma_start(g.rev.rearrange("k h m -> h k m"), rows[:]).then_inc(rows_out, 16)
            sp.wait_ge(rows_out, 16)
            sp.wait_ge(small_in, 16 * 4)

        @block.gpsimd
        def _(pool):
            pool.memset(g.mean_w[:], 1.0)
            pool.memset(tbl[:], 0.0).then_inc(cleared, 1)
            pool.wait_ge(cleared, 1)
            pool.memset(tbl[32:33, :], NEG).then_inc(cleared, 1)

        @block.tensor
        def _(pe):
            pe.wait_ge(x_in, 32)
            for c in range(CH):
                for t in range(NT):
                    last = nc.tensor.transpose(ps[:, c % 4, t * P:(t + 1) * P], xt[:, t, c * P:(c + 1) * P], g.ident[:])
                    if t == 0 and c >= 4:
                        pass
                last.then_inc(turned, 1)
                if c >= 3 and c < CH - 1:
                    pe.wait_ge(kept, c - 2)
            pe.wait_ge(const_in, 32)
            pe.wait_ge(cleared, 2)
            for k in range(KINDS):
                for half in range(2):
                    lo = half * (TOE // 2)
                    nc.tensor.matmul(ps[0:TCOLS, 4 + (2 * k + half) % 4, 0:TOE // 2], tbl[:], onehot[:, k, lo:lo + TOE // 2],
                                     start=True, stop=True).then_inc(rows_done, 1)
                    if 2 * k + half >= 3 and 2 * k + half < 2 * KINDS - 1:
                        pe.wait_ge(rows_kept, 2 * k + half - 2)

        @block.vector
        def _(dve):
            for c in range(CH):
                dve.wait_ge(turned, c + 1)
                nc.vector.tensor_copy(g.x[:, c, :], ps[:, c % 4, :]).then_inc(kept, 1)

        @block.scalar
        def _(act):
            for u in range(2 * KINDS):
                act.wait_ge(rows_done, u + 1)
                lo = (u % 2) * (TOE // 2)
                nc.scalar.copy(rows[:, u // 2, lo:lo + TOE // 2], ps[0:TCOLS, 4 + u % 4, 0:TOE // 2]).then_inc(rows_kept, 1)


def project(g, name, seg, plan):
    nc, ps, st = g.nc, g.ps, g.st
    units = []
    for t, tile in enumerate(plan):
        for item in tile:
            if item["kind"] == "F":
                units.append((t, item, None))
            else:
                units += [(t, item, q) for q in range(NT)]
    with ExitStack() as ctx:
        sem = lambda n: nc.alloc_semaphore(n)
        done = sem(f"{name}_tile_done")
        kept = [sem(f"{name}_kept_by_scalar"), sem(f"{name}_kept_by_vector")]
        block = ctx.enter_context(nc.Block())

        @block.sync
        def _(sp):
            st.feed(sp, seg)

        last_of = [u + 1 == len(units) or units[u + 1][0] != units[u][0] for u in range(len(units))]

        def wait_product(eng, u):
            if last_of[u]:
                eng.wait_ge(st.used, seg["start"] + units[u][0] + 1)
            else:
                eng.wait_ge(done, last_of[:u + 1].count(False))

        @block.tensor
        def _(pe):
            now = -1
            for u, (t, item, q) in enumerate(units):
                if t != now:
                    slot = st.wait(pe, seg, t)
                    now = t
                if u >= 8:
                    pe.wait_ge(kept[u % 2], (u - 8) // 2 + 1)
                x = item["x"]
                chunks, width = x.shape[1], item["tile"]
                w = slot[:, 0:chunks * width].rearrange("p (c n) -> p c n", c=chunks)
                col, n = item["col"], item["n"]
                for c in range(chunks):
                    if q is None:
                        last = nc.tensor.matmul(ps[0:n, u % 8, :], w[:, c, col:col + n], x[:, c, :],
                                                start=(c == 0), stop=(c == chunks - 1))
                    else:
                        last = nc.tensor.matmul(ps[:, u % 8, 0:n], x[:, c, q * P:(q + 1) * P], w[:, c, col:col + n],
                                                start=(c == 0), stop=(c == chunks - 1))
                last.then_inc(st.used if last_of[u] else done, 1)

        def keep(eng, parity):
            for u, (t, item, q) in enumerate(units):
                if u % 2 != parity:
                    continue
                wait_product(eng, u)
                if q is None:
                    outs = [(dst, ps[lo:hi, u % 8, c0:c0 + dst.shape[-1]], scale) for dst, lo, hi, scale, c0 in item["out"]]
                else:
                    outs = [(item["out"](q), ps[:, u % 8, 0:item["n"]], 1.0)]
                for dst, bank, scale in outs:
                    if parity == 0:
                        last = nc.scalar.mul(dst, bank, scale)
                    else:
                        last = nc.vector.tensor_scalar(dst, bank, scale, None, ALU.mult)
                last.then_inc(kept[parity], 1)

        @block.scalar
        def _(act):
            keep(act, 0)

        @block.vector
        def _(dve):
            keep(dve, 1)


def features(col, n, tile, x, out):
    return {"kind": "F", "col": col, "n": n, "tile": tile, "x": x, "out": out}


def tokens(col, n, tile, x, out):
    return {"kind": "T", "col": col, "n": n, "tile": tile, "x": x, "out": out}


def attention(g, name, heads, shared, tables, out_of, gate_of=None, next_seg=None):
    nc, ps, st = g.nc, g.ps, g.st
    NH = len(heads)
    U = max(len(u) for u in heads)
    width = lambda u, i: len(u["blocks"](i)) * u["klen"]
    cap = max(sum(width(u, i) for u in us for i in range(NT)) for us in heads)

    def packs(u):
        where, bank, col = {}, 0, 0
        for kb in sorted({kb for i in range(NT) for kb in u["blocks"](i)}):
            ts = [i for i in range(NT) if kb in u["blocks"](i)]
            if col + len(ts) * P > S:
                bank, col = bank + 1, 0
            where[kb] = (bank, col, ts[0], len(ts))
            col += len(ts) * P
        return where, bank + 1

    flat = [(h, k, u) for h in range(NH) for k, u in enumerate(heads[h])]
    first_of = [0]
    for us in heads:
        first_of.append(first_of[-1] + len(us))
    banks_before = [0]
    for h, k, u in flat:
        banks_before.append(banks_before[-1] + packs(u)[1])

    with ExitStack() as ctx:
        sb = lambda n, s: ctx.enter_context(nc.sbuf_tensor(n, s, F32))
        sem = lambda n: nc.alloc_semaphore(n)
        sc = sb(f"{name}_scores", [P, 2, cap])
        pt = sb(f"{name}_weights_t", [P, 2, 3 * S])
        stat = sb(f"{name}_stats", [P, 2, 6, U, NT])
        s_ready, s_kept, negmax, exped, normed = (sem(f"{name}_{n}") for n in
            ("scores_ready", "scores_kept", "negmax_ready", "exp_done", "weights_ready"))
        t_ready, t_kept, pv_done, o_kept, dve_step = (sem(f"{name}_{n}") for n in
            ("turned", "turned_kept", "values_done", "out_kept", "vector_step"))
        table_in = [sem(f"{name}_table_in_{s}") for s in range(2)]
        block = ctx.enter_context(nc.Block())

        def place(h, k, i):
            o = 0
            for kk, u in enumerate(heads[h]):
                for ii in range(NT):
                    w = width(u, ii)
                    if (kk, ii) == (k, i):
                        return o, w
                    o += w

        @block.sync
        def _(sp):
            if next_seg is not None:
                st.first(sp, next_seg)
            for h in range(NH):
                if h >= 2:
                    sp.wait_ge(s_kept, NT * first_of[h - 1])
                for dst, src in tables(h, h % 2):
                    sp.dma_start(dst, src).then_inc(table_in[h % 2], 16)

        @block.tensor
        def _(pe):
            def scores(h):
                for k, u in enumerate(heads[h]):
                    n = first_of[h] + k
                    for i in range(NT):
                        if n:
                            pe.wait_ge(s_kept, NT * (n - 1) + i + 1)
                        kb = u["blocks"](i)
                        nc.tensor.matmul(ps[:, i, 0:width(u, i)], u["q"][:, i * P:(i + 1) * P],
                                         u["k"](kb[0], width(u, i)), start=True, stop=True).then_inc(s_ready, 1)

            def values(h):
                dv0, dv = out_of(h)[1:3]
                o = ps[dv0:dv0 + dv, 7, :]
                total = sum(len(packs(u)[0]) for u in heads[h])
                done = 0
                for k, u in enumerate(heads[h]):
                    n = first_of[h] + k
                    where, nb = packs(u)
                    for b in range(nb):
                        if n:
                            pe.wait_ge(t_kept, banks_before[n])
                        for kb in sorted(where):
                            bank, col, i0, cnt = where[kb]
                            if bank != b:
                                continue
                            for i in range(i0, i0 + cnt):
                                pe.wait_ge(normed, NT * n + i + 1)
                                off, w = place(h, k, i)
                                j = u["blocks"](i).index(kb) * u["klen"]
                                last = nc.tensor.transpose(ps[0:u["klen"], 4 + bank, col + (i - i0) * P:col + (i - i0 + 1) * P],
                                                           sc[:, h % 2, off + j:off + j + u["klen"]], g.ident[:])
                        last.then_inc(t_ready, 1)
                    for kb in sorted(where):
                        bank, col, i0, cnt = where[kb]
                        pe.wait_ge(t_kept, banks_before[n] + bank + 1)
                        if done == 0 and h:
                            pe.wait_ge(o_kept, h)
                        last = nc.tensor.matmul(o[:, i0 * P:(i0 + cnt) * P], u["v"](kb),
                                                pt[0:u["klen"], n % 2, bank * S + col:bank * S + col + cnt * P],
                                                start=(done == 0), stop=(done == total - 1), skip_group_check=True)
                        done += 1
                    last.then_inc(pv_done, 1)

            scores(0)
            for h in range(NH):
                if h + 1 < NH:
                    scores(h + 1)
                values(h)

        @block.vector
        def _(dve):
            steps = [0]

            def step(ins):
                steps[0] += 1
                ins.then_inc(dve_step, 1)
                dve.wait_ge(dve_step, steps[0])

            def masked(h):
                slot = h % 2
                dve.wait_ge(table_in[slot], 16 * sum(len(tables(hh, hh % 2)) for hh in range(slot, h + 1, 2)))
                if h >= 2:
                    dve.wait_ge(t_ready, banks_before[first_of[h - 1]])
                for k, u in enumerate(heads[h]):
                    n = first_of[h] + k
                    for i in range(NT):
                        off, w = place(h, k, i)
                        dve.wait_ge(s_ready, NT * n + i + 1)
                        nc.vector.tensor_tensor_reduce(sc[:, slot, off:off + w], ps[:, i, 0:w], u["bias"](i), 1.0, 3 * NEG,
                                                       ALU.add, ALU.max, stat[:, slot, 0, k, i:i + 1]).then_inc(s_kept, 1)
                nu = len(heads[h])
                dve.wait_ge(s_kept, NT * first_of[h + 1])
                if shared:
                    step(nc.vector.tensor_reduce(stat[:, slot, 5, 0, :], stat[:, slot, 0, :, :].rearrange("p u i -> p i u"),
                                                 AX_X, ALU.max))
                    nc.vector.tensor_scalar(stat[:, slot, 1, 0, :], stat[:, slot, 5, 0, :], -1.0, None, ALU.mult).then_inc(negmax, 1)
                else:
                    for k, u in enumerate(heads[h]):
                        ins = nc.vector.tensor_scalar(stat[:, slot, 1, k, :], stat[:, slot, 0, k, :],
                                                      NEG * 1e-8 if u.get("guard") else 3 * NEG, -1.0, ALU.max, ALU.mult)
                    ins.then_inc(negmax, 1)

            def normal(h):
                slot = h % 2
                nu = len(heads[h])
                dve.wait_ge(exped, NT * first_of[h + 1])
                if shared:
                    step(nc.vector.tensor_reduce(stat[:, slot, 5, 0, :], stat[:, slot, 2, :, :].rearrange("p u i -> p i u"),
                                                 AX_X, ALU.add))
                    step(nc.vector.reciprocal(stat[:, slot, 4, 0, :], stat[:, slot, 5, 0, :]))
                else:
                    step(nc.vector.tensor_scalar(stat[:, slot, 5, 0:nu, :], stat[:, slot, 2, 0:nu, :], 1e-30, None, ALU.max))
                    step(nc.vector.reciprocal(stat[:, slot, 4, 0:nu, :], stat[:, slot, 5, 0:nu, :]))
                    if gate_of is not None:
                        for k in range(nu):
                            if gate_of(h, k) is not None:
                                ins = nc.vector.tensor_tensor(stat[:, slot, 4, k, :], stat[:, slot, 4, k, :], gate_of(h, k), ALU.mult)
                        step(ins)
                for k, u in enumerate(heads[h]):
                    for i in range(NT):
                        off, w = place(h, k, i)
                        kk = 0 if shared else k
                        nc.vector.tensor_scalar(sc[:, slot, off:off + w], sc[:, slot, off:off + w],
                                                stat[:, slot, 4, kk, i:i + 1], None, ALU.mult).then_inc(normed, 1)

            masked(0)
            for h in range(NH):
                if h + 1 < NH:
                    masked(h + 1)
                normal(h)

        @block.scalar
        def _(act):
            def exps(h):
                act.wait_ge(negmax, h + 1)
                if h >= 2:
                    act.wait_ge(normed, NT * first_of[h - 1])
                for k, u in enumerate(heads[h]):
                    for i in range(NT):
                        off, w = place(h, k, i)
                        kk = 0 if shared else k
                        nc.scalar.activation(sc[:, h % 2, off:off + w], sc[:, h % 2, off:off + w], ACT.Exp,
                                             bias=stat[:, h % 2, 1, kk, i:i + 1], scale=1.0,
                                             accum_out=stat[:, h % 2, 2, k, i:i + 1]).then_inc(exped, 1)

            exps(0)
            for h in range(NH):
                if h + 1 < NH:
                    exps(h + 1)
                for k, u in enumerate(heads[h]):
                    n = first_of[h] + k
                    where, nb = packs(u)
                    for b in range(nb):
                        act.wait_ge(t_ready, banks_before[n] + b + 1)
                        if n >= 2:
                            act.wait_ge(pv_done, n - 1)
                        cols = max(col + cnt * P for bank, col, _, cnt in where.values() if bank == b)
                        nc.scalar.copy(pt[0:u["klen"], n % 2, b * S:b * S + cols], ps[0:u["klen"], 4 + b, 0:cols]).then_inc(t_kept, 1)
                act.wait_ge(pv_done, first_of[h + 1])
                dst, dv0, dv = out_of(h)
                nc.scalar.copy(dst, ps[dv0:dv0 + dv, 7, :]).then_inc(o_kept, 1)


def down(g, name, seg, src, kp, kind, l, src_chunks, col=None):
    nc, ps, st = g.nc, g.ps, g.st
    ntile = src_chunks // 2
    with ExitStack() as ctx:
        sb = lambda n, s: ctx.enter_context(nc.sbuf_tensor(n, s, F32))
        sem = lambda n: nc.alloc_semaphore(n)
        sq = sb(f"{name}_squares", [P, CH, S])
        y = sb(f"{name}_y", [P, CH, S]) if kind == "rms" else g.x
        rs = sb(f"{name}_rstd", [P, 3, S])
        y_kept, mean_done, centred, squared, sq_done, v_step, rstd, scaled = (sem(f"{name}_{n}") for n in
            ("y_kept", "mean_done", "centred", "squared", "squares_summed", "vector_step", "root_ready", "scaled"))
        block = ctx.enter_context(nc.Block())

        @block.sync
        def _(sp):
            st.feed(sp, seg)

        @block.tensor
        def _(pe):
            def tile(t, turn):
                slot = st.wait(pe, seg, t, turn)
                w = slot[0:kp, :].rearrange("p (c n) -> p c n", c=2)
                for j in range(2):
                    for b in range(8):
                        if turn is None:
                            rhs = src[0:kp, 2 * t + j, :]
                        else:
                            rhs = src[0:kp, bass.ds(turn * (2 * RING) + (2 * t + j), 1), :].rearrange("p c n -> p (c n)")
                        last = nc.tensor.matmul(ps[:, b, :], w[:, j, b * P:(b + 1) * P], rhs,
                                                start=(turn is None and t == 0 and j == 0),
                                                stop=(turn is None and t == ntile - 1 and j == 1), skip_group_check=True)
                last.then_inc(st.used, 1)
            loop_tiles(pe, ntile, 1, tile)
            if kind == "ln":
                pe.wait_ge(y_kept, 1)
                for c in range(CH):
                    pe.wait_ge(y_kept, c + 1)
                    last = nc.tensor.matmul(ps[:, 0, :], g.mean_w[:], y[:, c, :], start=(c == 0), stop=(c == CH - 1))
                last.then_inc(mean_done, 1)
            else:
                pe.wait_ge(y_kept, 2)
            for c in range(CH):
                pe.wait_ge(squared, c + 1)
                last = nc.tensor.matmul(ps[:, 1, :], g.mean_w[:], sq[:, c, :], start=(c == 0), stop=(c == CH - 1))
            last.then_inc(sq_done, 1)

        @block.vector
        def _(dve):
            steps = [0]

            def step(ins):
                steps[0] += 1
                ins.then_inc(v_step, 1)
                dve.wait_ge(v_step, steps[0])

            dve.wait_ge(st.used, seg["start"] + ntile)
            if kind == "ln":
                for c in range(CH):
                    nc.vector.scalar_tensor_tensor(out=g.x[:, c, :], in0=g.x[:, c, :], scalar=ALPHA, in1=ps[:, c, :],
                                                   op0=ALU.mult, op1=ALU.add).then_inc(y_kept, 1)
                dve.wait_ge(mean_done, 1)
                step(nc.vector.tensor_scalar(rs[:, 0, :], ps[:, 0, :], 1.0 / D, None, ALU.mult))
                for c in range(CH):
                    nc.vector.tensor_tensor(g.x[:, c, :], g.x[:, c, :], rs[:, 0, :], ALU.subtract).then_inc(centred, 1)
            else:
                for c in range(CH):
                    nc.vector.tensor_copy(y[:, c, :], ps[:, c, :]).then_inc(y_kept, 1)
            dve.wait_ge(sq_done, 1)
            step(nc.vector.tensor_scalar(rs[:, 1, :], ps[:, 1, :], 1.0 / D, LN_EPS if kind == "ln" else RMS_EPS_2, ALU.mult, ALU.add))
            nc.vector.reciprocal(rs[:, 2, :], rs[:, 1, :]).then_inc(rstd, 1)
            dve.wait_ge(rstd, 2)
            for c in range(CH):
                if kind == "ln":
                    nc.vector.scalar_tensor_tensor(out=g.x[:, c, :], in0=g.x[:, c, :], scalar=g.ln_g[:, l, c:c + 1],
                                                   in1=rs[:, 0, :], op0=ALU.mult, op1=ALU.mult).then_inc(scaled, 1)
                else:
                    nc.vector.scalar_tensor_tensor(out=y[:, c, :], in0=y[:, c, :], scalar=g.norm_post[:, l, c:c + 1],
                                                   in1=rs[:, 0, :], op0=ALU.mult, op1=ALU.mult).then_inc(scaled, 1)
            if kind == "rms":
                for c in range(CH):
                    dve.wait_ge(scaled, c + 1)
                    nc.vector.tensor_tensor(g.x[:, c, :], g.x[:, c, :], y[:, c, :], ALU.add)

        @block.scalar
        def _(act):
            for c in range(CH):
                act.wait_ge(centred if kind == "ln" else y_kept, c + 1)
                nc.scalar.activation(sq[:, c, :], y[:, c, :], ACT.Square).then_inc(squared, 1)
            act.wait_ge(rstd, 1)
            nc.scalar.activation(rs[:, 0, :], rs[:, 2, :], ACT.Sqrt).then_inc(rstd, 1)
            if kind == "ln":
                for c in range(CH):
                    act.wait_ge(scaled, c + 1)
                    nc.scalar.activation(g.x[:, c, :], g.x[:, c, :], ACT.Identity, bias=g.ln_b[:, l, c:c + 1], scale=1.0)


def ffn_up(g, l, act_t, cw):
    nc, ps, st, seg = g.nc, g.ps, g.st, g.seg_up[l]
    with ExitStack() as ctx:
        sb = lambda n, s: ctx.enter_context(nc.sbuf_tensor(n, s, F32))
        sem = lambda n: nc.alloc_semaphore(n)
        conv = sb(f"ffn{l}_conv", [P, RING, S + 2])
        gel = sb(f"ffn{l}_gelu", [P, RING, S])
        n_ = f"ffn{l}_"
        par_in, done, zeroed, g_kept, t1, t2, t3, gelu_done, act_done = (sem(n_ + n) for n in
            ("params_in", "tile_done", "margins_zero", "gate_copied", "tap_1", "tap_2", "tap_3", "gelu_done", "act_done"))
        block = ctx.enter_context(nc.Block())

        @block.sync
        def _(sp):
            sp.dma_start(cw[:], g.a["f_ffn_conv"][l]).then_inc(par_in, 16)
            st.feed(sp, seg)

        @block.tensor
        def _(pe):
            def tile(t, turn):
                slot = st.wait(pe, seg, t, turn)
                w = slot.rearrange("p (c s n) -> p c s n", c=CH, s=2)
                if turn is not None or t >= RING:
                    pe.wait_ge(act_done, at(turn, 1, t) - (RING - 1))
                for s in (1, 0):
                    for c in range(CH):
                        last = nc.tensor.matmul(ps[:, 2 * (t % RING) + s, :], w[:, c, s, :], g.x[:, c, :],
                                                start=(c == 0), stop=(c == CH - 1))
                    last.then_inc(done if s else st.used, 1)
            loop_tiles(pe, FF_CH, RING, tile)

        @block.gpsimd
        def _(pool):
            pool.memset(conv[:, :, 0:2], 0.0).then_inc(zeroed, 1)

        @block.scalar
        def _(act):
            act.wait_ge(par_in, 16)

            def tile(t, turn):
                act.wait_ge(done, at(turn, 1, t) + 1)
                if turn is not None or t >= RING:
                    act.wait_ge(t3, at(turn, 1, t) - (RING - 1))
                nc.scalar.copy(conv[:, t % RING, 2:S + 2], ps[:, 2 * (t % RING) + 1, :]).then_inc(g_kept, 1)
                act.wait_ge(t3, at(turn, 1, t) + 1)
                nc.scalar.activation(gel[:, t % RING, :], gel[:, t % RING, :], ACT.Gelu_apprx_tanh).then_inc(gelu_done, 1)
            loop_tiles(act, FF_CH, RING, tile)

        @block.vector
        def _(dve):
            dve.wait_ge(par_in, 16)
            dve.wait_ge(zeroed, 1)

            def tile(t, turn):
                f = bass.ds(at(turn, 1, t), 1)
                r = t % RING
                tap = lambda k: cw[:, k, f]
                dve.wait_ge(g_kept, at(turn, 1, t) + 1)
                nc.vector.tensor_scalar(gel[:, r, :], conv[:, r, 2:S + 2], tap(2), tap(3), ALU.mult, ALU.add).then_inc(t1, 1)
                dve.wait_ge(t1, at(turn, 1, t) + 1)
                nc.vector.scalar_tensor_tensor(out=gel[:, r, :], in0=conv[:, r, 1:S + 1], scalar=tap(1), in1=gel[:, r, :],
                                               op0=ALU.mult, op1=ALU.add).then_inc(t2, 1)
                dve.wait_ge(t2, at(turn, 1, t) + 1)
                nc.vector.scalar_tensor_tensor(out=gel[:, r, :], in0=conv[:, r, 0:S], scalar=tap(0), in1=gel[:, r, :],
                                               op0=ALU.mult, op1=ALU.add).then_inc(t3, 1)
                dve.wait_ge(gelu_done, at(turn, 1, t) + 1)
                dve.wait_ge(st.used, at(turn, 1, t) + (seg["start"] + 1))
                dst = act_t[:, t, :] if turn is None else act_t[:, f, :].rearrange("p c n -> p (c n)")
                nc.vector.tensor_tensor(dst, gel[:, r, :], ps[:, 2 * r, :], ALU.mult).then_inc(act_done, 1)
            loop_tiles(dve, FF_CH, RING, tile)


def rms(g, name, groups):
    nc, ps = g.nc, g.ps
    flat = [(k, c) for k, gr in enumerate(groups) for c in range(len(gr["src"]))]
    with ExitStack() as ctx:
        sb = lambda n, s: ctx.enter_context(nc.sbuf_tensor(n, s, F32))
        sem = lambda n: nc.alloc_semaphore(n)
        G = len(groups)
        sq = sb(f"{name}_squares", [P, len(flat), S])
        rs = sb(f"{name}_rstd", [P, 3, G, S])
        squared, summed, ms_done, inv_done, root = (sem(f"{name}_{n}") for n in
            ("squared", "squares_summed", "mean_square", "inverse", "root_ready"))
        block = ctx.enter_context(nc.Block())

        @block.scalar
        def _(act):
            for n, (k, c) in enumerate(flat):
                nc.scalar.activation(sq[:, n, :], groups[k]["src"][c], ACT.Square).then_inc(squared, 1)
            for k in range(G):
                act.wait_ge(inv_done, k + 1)
                nc.scalar.activation(rs[:, 2, k, :], rs[:, 1, k, :], ACT.Sqrt).then_inc(root, 1)

        @block.tensor
        def _(pe):
            for n, (k, c) in enumerate(flat):
                pe.wait_ge(squared, n + 1)
                last_c = c == len(groups[k]["src"]) - 1
                mm = nc.tensor.matmul(ps[:, k, :], g.mean_w[:], sq[:, n, :], start=(c == 0), stop=last_c)
                if last_c:
                    mm.then_inc(summed, 1)

        @block.vector
        def _(dve):
            for k, gr in enumerate(groups):
                m2 = gr.get("mult", 1.0) ** 2
                dve.wait_ge(summed, k + 1)
                nc.vector.tensor_scalar(rs[:, 0, k, :], ps[:, k, :], 1.0 / (gr["n"] * m2), gr["eps"] / m2,
                                        ALU.mult, ALU.add).then_inc(ms_done, 1)
                dve.wait_ge(ms_done, k + 1)
                nc.vector.reciprocal(rs[:, 1, k, :], rs[:, 0, k, :]).then_inc(inv_done, 1)
            for k, gr in enumerate(groups):
                dve.wait_ge(root, k + 1)
                for c, src in enumerate(gr["src"]):
                    nc.vector.scalar_tensor_tensor(out=gr["dst"][c], in0=src, scalar=gr["gain"][c], in1=rs[:, 2, k, :],
                                                   op0=ALU.mult, op1=ALU.mult)


def toeplitz(g, kind, col):
    base = g.rev[kind, col, :]
    return bass.AP(tensor=base.tensor, offset=base.offset, ap=[[1, P], [1, S]])


def biases(table, i, first_block=0):
    top = P * (i - first_block + 1) - 1
    return table[:, top::-1]


def causal(i):
    return list(range(i + 1))


def banded(i):
    return list(range(max(0, i - 1), i + 1))


def lambda_stage(g, neg_lam):
    nc, a = g.nc, g.a
    with ExitStack() as ctx:
        sb = lambda n, s: ctx.enter_context(nc.sbuf_tensor(n, s, F32))
        sem = lambda n: nc.alloc_semaphore(n)
        lp = sb("lambda_params", [P, 4, A_QK])
        prod = sb("lambda_products", [P, 2, A_QK])
        dots, ex = sb("lambda_dots", [P, 2]), sb("lambda_exps", [P, 2])
        lp_in, v, e = sem("lambda_in"), sem("lambda_vector"), sem("lambda_exp")
        block = ctx.enter_context(nc.Block())

        @block.sync
        def _(sp):
            sp.dma_start(lp[:], a["ev_lambda"][0].partition_broadcast(P)).then_inc(lp_in, 16)

        @block.vector
        def _(dve):
            dve.wait_ge(lp_in, 16)
            pairs = lp[:].rearrange("p (k two) d -> p two k d", two=2)
            nc.vector.tensor_tensor(prod[:], pairs[:, 0], pairs[:, 1], ALU.mult).then_inc(v, 1)
            dve.wait_ge(v, 1)
            nc.vector.tensor_reduce(dots[:], prod[:], AX_X, ALU.add).then_inc(v, 1)
            dve.wait_ge(e, 1)
            nc.vector.tensor_tensor(dots[:, 0:1], ex[:, 1:2], ex[:, 0:1], ALU.subtract).then_inc(v, 1)
            dve.wait_ge(v, 3)
            for i in range(NT):
                nc.vector.tensor_scalar(neg_lam[:, i:i + 1], dots[:, 0:1], -LAM_INIT, None, ALU.add)

        @block.scalar
        def _(act):
            act.wait_ge(v, 2)
            nc.scalar.activation(ex[:], dots[:], ACT.Exp).then_inc(e, 1)


def even_mixer(g, o):
    nc, a = g.nc, g.a
    with ExitStack() as ctx:
        sb = lambda n, s: ctx.enter_context(nc.sbuf_tensor(n, s, F32))
        neg_lam, sub_g = sb("neg_lambda", [P, NT]), sb("subln_gain", [P, 1])
        lambda_stage(g, neg_lam)
        with ExitStack() as inner:
            sbi = lambda n, s: inner.enter_context(nc.sbuf_tensor(n, s, F32))
            q, k, v = sbi("a_q", [P, 4, S]), sbi("a_k", [P, 4, S]), sbi("a_v", [P, NT, S])
            toe = sbi("a_tables", [P, 2, S])
            two = lambda dst, t, scale: [features(128 * j, P, 256, g.x, [(dst[:, 2 * t + j, :], 0, P, scale, 0)]) for j in range(2)]
            plan = [two(q, t, A_QK ** -0.5) for t in range(2)] + [two(k, t, 1.0) for t in range(2)]
            plan += [[tokens(0, 256, 256, g.x, lambda i, t=t: v[:, i, 256 * t:256 * (t + 1)])] for t in range(2)]
            project(g, "a_proj", g.seg_a, plan)

            def unit(h, m):
                n = m * A_HEADS + h
                lo = 64 * (n % 2)
                return {"q": q[lo:lo + 64, n // 2, :], "k": lambda kb, w: k[lo:lo + 64, n // 2, kb * P:kb * P + w],
                        "v": lambda kb: v[:, kb, h * A_V:(h + 1) * A_V], "blocks": causal, "klen": P,
                        "bias": lambda i: biases(toe[:, h % 2, :], i)}
            attention(g, "a_attn", [[unit(h, 0), unit(h, 1)] for h in range(A_HEADS)], False,
                      lambda h, s: [(toe[:, s, :], toeplitz(g, STD, h))],
                      lambda h: (o[:, h, :], 0, P), gate_of=lambda h, u: neg_lam[:] if u else None)
        with ExitStack() as inner:
            sbi = lambda n, s: inner.enter_context(nc.sbuf_tensor(n, s, F32))
            q, k, v = sbi("b_q", [P, 3, 2, S]), sbi("b_k", [P, 3, 2, S]), sbi("b_v", [P, 3, NT, 256])
            toe = sbi("b_tables", [P, 2, 3, S])
            plan = []
            for i in range(N_PAIRS):
                for dst, scale in ((q, B_DIM ** -0.5), (k, 1.0)):
                    plan.append([features(128 * j, P, 256, g.x, [(dst[:, i, j, :], 0, P, scale, 0)]) for j in range(2)])
                plan.append([tokens(0, 256, 256, g.x, lambda t, i=i: v[:, i, t, :])])
            project(g, "b_proj", g.seg_b, plan)

            def unit(h, i):
                lo = 64 * (h % 2)
                return {"q": q[lo:lo + 64, i, h // 2, :], "k": lambda kb, w: k[lo:lo + 64, i, h // 2, kb * P:kb * P + w],
                        "v": lambda kb: v[:, i, kb, h * B_DIM:(h + 1) * B_DIM], "blocks": causal if i else banded, "klen": P,
                        "bias": lambda t: biases(toe[:, h % 2, i, :], t, 0 if i else max(0, t - 1))}
            attention(g, "b_attn", [[unit(h, i) for i in range(N_PAIRS)] for h in range(B_HEADS)], True,
                      lambda h, s: [(toe[:, s, i, :], toeplitz(g, (WIN, DIL4, DIL16)[i], A_HEADS + i * B_HEADS + h)) for i in range(N_PAIRS)],
                      lambda h: (o[64 * (h % 2):64 * (h % 2) + 64, 4 + h // 2, :], 64 * (h % 2), 64))
        load_small(g, "subln", [(sub_g[:, 0:1], a["f_subln"])])
        rms(g, "subln_norm", [{"src": [o[:, h, :]], "dst": [o[:, h, :]], "n": A_V, "eps": RMS_EPS, "gain": [sub_g[:, 0:1]],
                               "mult": 1.0 - LAM_INIT} for h in range(A_HEADS)])


def load_small(g, name, pairs, next_seg=None):
    nc = g.nc
    small_in = nc.alloc_semaphore(f"{name}_in")
    with nc.Block() as block:
        @block.sync
        def _(sp):
            for dst, src in pairs:
                sp.dma_start(dst, src).then_inc(small_in, 16)
            sp.wait_ge(small_in, 16 * len(pairs))


def odd_mixer(g, o):
    nc, a, ps, st = g.nc, g.a, g.ps, g.st
    with ExitStack() as ctx:
        sb = lambda n, s, c=ctx: c.enter_context(nc.sbuf_tensor(n, s, F32))
        cq, ckv = sb("cq", [P, 3, S]), sb("ckv", [P, 2, S])
        raw_k = sb("k_rope_raw", [96, S])
        qg, kvg = sb("q_norm_gain", [P, 3]), sb("kv_norm_gain", [P, 2])
        with ExitStack() as inner:
            sbi = lambda n, s: sb(n, s, inner)
            qc = sbi("c_q", [P, 4, S])
            kk = sbi("cmp_in", [P, 2, C_GROUPS, S])
            kd = sbi("c_k", [P, 2, C_GROUPS, S])
            vd = sbi("c_v", [P, 2, NT, P])
            gate = sbi("gates", [P, NT, 24])
            w2 = sbi("cmp_w2", [P, 2, 2, C_DIM])
            pe_t = sbi("cmp_pos", [P, 2, 16])
            pe_b = sbi("cmp_pos_bias", [P, 2, 2])
            hid = sbi("cmp_hidden", [P, 2, 2, C_GROUPS * CMP_BLOCKS])
            kc = sbi("cmp_k", [P, C_GROUPS, CMP_BLOCKS])
            vc = sbi("cmp_v", [CMP_BLOCKS, C_GROUPS, C_DIM])
            cb = sbi("cmp_bias", [P, CB_SPAN, C_HEADS])
            fwd = sbi("onehot_fwd", [33, FWD_LEN])
            tbl = sbi("bias_table_c", [33, C_HEADS])
            toe = sbi("c_tables", [P, 2, S])

            def both_halves(dst, gr):
                return [(dst[64 * half:64 * half + 64, gr, :], 64 * gr, 64 * gr + 64, 1.0, 0) for half in range(2)]

            def shifted(s):
                return [(kk[64 * half:64 * half + 64, s, gr, 0:S - half], 64 * gr, 64 * gr + 64, 1.0, half)
                        for gr in range(2) for half in range(2)]
            plan = [[features(128 * j, P, 256, g.x, [(qc[:, 2 * t + j, :], 0, P, C_DIM ** -0.5, 0)]) for j in range(2)] for t in range(2)]
            plan.append([features(128 * s, P, 256, g.x, shifted(s)) for s in range(2)])
            for b in range(2):
                plan.append([features(0, P, 256, g.x, both_halves(kd[:, b], 0) + both_halves(kd[:, b], 1)),
                             tokens(128, P, 256, g.x, lambda i, b=b: vd[:, b, i, :])])
            plan.append([tokens(0, 24, 24, g.x, lambda i: gate[:, i, :])])
            plan.append([features(0, 32, 32, g.x, [(raw_k[64:96, :], 0, 32, 1.0, 0)])])
            plan.append([features(128 * j, P, 256, g.x, [(cq[:, j, :], 0, P, 1.0, 0)]) for j in range(2)])
            plan.append([features(0, P, 256, g.x, [(cq[:, 2, :], 0, P, 1.0, 0)]), features(128, P, 256, g.x, [(ckv[:, 0, :], 0, P, 1.0, 0)])])
            plan.append([features(0, P, 128, g.x, [(ckv[:, 1, :], 0, P, 1.0, 0)])])
            project(g, "od_proj", g.seg_od, plan)
            load_small(g, "od_small", [
                (w2[:], a["od_cmp_w2"][0].rearrange("s (j p) n -> p s j n", p=P)),
                (pe_t[:], a["f_cmp_pe"]),
                (fwd[:], a["c_onehot_fwd"]), (tbl[0:32, :], a["rel_bias"][:, 0:C_HEADS]), (tbl[32:33, :], a["c_neg"][:, 0:C_HEADS]),
                (qg[:], a["f_q_norm"]),
                (kvg[:], a["f_kv_norm"])])
            compress(g, kk, w2, pe_t, pe_b, hid, kc, vc, cb, fwd, tbl, gate)

            def units(h):
                lo, gr = 64 * (h % 2), h // 4
                q = qc[lo:lo + 64, h // 2, :]
                full = [{"q": q, "k": lambda kb, w, b=b: kd[lo:lo + 64, b, gr, kb * P:kb * P + w],
                         "v": lambda kb, b=b: vd[:, b, kb, 64 * gr:64 * gr + 64], "blocks": causal, "klen": P,
                         "bias": lambda i: biases(toe[:, h % 2, :], i)} for b in range(2)]
                cmp_ = {"q": q, "k": lambda kb, w: kc[lo:lo + 64, gr, :], "v": lambda kb: vc[:, gr, :], "blocks": lambda i: [0],
                        "klen": CMP_BLOCKS, "guard": True, "bias": lambda i: cb[:, 24 - 8 * i:24 - 8 * i + CMP_BLOCKS, h]}
                return [cmp_] + full
            attention(g, "c_attn", [units(h) for h in range(C_HEADS)], False,
                      lambda h, s: [(toe[:, s, :], toeplitz(g, STD, h))],
                      lambda h: (o[64 * (h % 2):64 * (h % 2) + 64, h // 2, :], 64 * (h % 2), 64),
                      gate_of=lambda h, u: gate[:, :, 8 * u + h])
        rms(g, "lora_norm", [
            {"src": [cq[:, c, :] for c in range(3)], "dst": [cq[:, c, :] for c in range(3)], "n": D_Q_LORA, "eps": RMS_EPS,
             "gain": [qg[:, c:c + 1] for c in range(3)]},
            {"src": [ckv[:, c, :] for c in range(2)], "dst": [ckv[:, c, :] for c in range(2)], "n": D_KV_LORA, "eps": RMS_EPS,
             "gain": [kvg[:, c:c + 1] for c in range(2)]}])
        qm, km, vm = sb("m_q", [96, D_HEADS, S]), sb("m_k", [96, D_HEADS, S]), sb("m_v", [P, NT, S])
        mask = sb("m_mask", [P, 2, S])
        rot = sb("rope_swap", [96, 32])
        trig = sb("rope_trig", [96, 4, S])
        scale = (D_NOPE + D_ROPE) ** -0.5
        plan = [[features(96 * j, 96, 384, cq, [(qm[0:64, 4 * t + j, :], 0, 64, scale, 0), (qm[64:96, 4 * t + j, :], 64, 96, 1.0, 0)])
                 for j in range(4)] for t in range(2)]
        plan.append([features(128 * j, P, 512, ckv, [(km[0:64, 2 * j + e, :], 64 * e, 64 * e + 64, 1.0, 0) for e in range(2)])
                     for j in range(4)])
        plan.append([tokens(0, 512, 512, ckv, lambda i: vm[:, i, :])])
        project(g, "m_proj", g.seg_mla, plan)
        load_small(g, "rope", [(rot[64:96, :], a["c_rope_swap"]), (trig[64:96], a["c_rope_trig"].rearrange("k p t -> p k t"))])
        rope(g, qm, km, raw_k, rot, trig)

        def unit(h):
            return {"q": qm[:, h, :], "k": lambda kb, w: km[:, h, kb * P:kb * P + w], "v": lambda kb: vm[:, kb, 64 * h:64 * h + 64],
                    "blocks": causal, "klen": P, "bias": lambda i: biases(mask[:, h % 2, :], i)}
        attention(g, "m_attn", [[unit(h)] for h in range(D_HEADS)], False,
                  lambda h, s: [(mask[:, s, :], toeplitz(g, STD, 16))],
                  lambda h: (o[64 * (h % 2):64 * (h % 2) + 64, 4 + h // 2, :], 64 * (h % 2), 64))


def rope(g, qm, km, raw_k, rot, trig):
    nc, ps = g.nc, g.ps
    with ExitStack() as ctx:
        sem = lambda n: nc.alloc_semaphore(n)
        tmp = ctx.enter_context(nc.sbuf_tensor("rope_tmp", [96, 4, S], F32))
        swapped, part, turned, summed = sem("rope_swapped"), sem("rope_sin_part"), sem("rope_cos_part"), sem("rope_summed")
        src = [qm[64:96, h, :] for h in range(D_HEADS)] + [raw_k[64:96, :]]
        block = ctx.enter_context(nc.Block())

        @block.tensor
        def _(pe):
            for n, x in enumerate(src):
                if n >= 8:
                    pe.wait_ge(part, n - 7)
                nc.tensor.matmul(ps[64:96, n % 8, :], rot[64:96, :], x, start=True, stop=True).then_inc(swapped, 1)

        @block.vector
        def _(dve):
            for n, x in enumerate(src):
                k = 2 if n < D_HEADS else 0
                s = 2 * (n % 2)
                dve.wait_ge(swapped, n + 1)
                nc.vector.tensor_tensor(tmp[64:96, s, :], ps[64:96, n % 8, :], trig[64:96, k + 1, :], ALU.mult).then_inc(part, 1)
                nc.vector.tensor_tensor(tmp[64:96, s + 1, :], x, trig[64:96, k, :], ALU.mult).then_inc(turned, 1)
                dve.wait_ge(part, n + 1)
                dve.wait_ge(turned, n + 1)
                dst = x if n < D_HEADS else km[64:96, 0, :]
                nc.vector.tensor_tensor(dst, tmp[64:96, s, :], tmp[64:96, s + 1, :], ALU.add).then_inc(summed, 1)

        @block.gpsimd
        def _(pool):
            pool.wait_ge(summed, D_HEADS + 1)
            for h in range(1, D_HEADS):
                nc.gpsimd.tensor_copy(km[64:96, h, :], km[64:96, 0, :])


def compress(g, kk, w2, pe_t, pe_b, hid, kc, vc, cb, fwd, tbl, gate):
    nc, ps, st, seg = g.nc, g.ps, g.st, g.seg_cmp
    NB = C_GROUPS * CMP_BLOCKS
    with ExitStack() as ctx:
        sem = lambda n: nc.alloc_semaphore(n)
        cb_done, pe_done, pe_kept, hid_done, kv_done = (sem(f"cmp_{n}") for n in
            ("bias_done", "pos_done", "pos_kept", "hidden_ready", "kv_done"))
        block = ctx.enter_context(nc.Block())

        @block.sync
        def _(sp):
            st.feed(sp, seg)

        @block.tensor
        def _(pe):
            for u in range(CB_SPAN):
                lo = FWD_OFF + CMP_STRIDE * (24 - u) - (CMP_LEN - 1)
                last = nc.tensor.matmul(ps[:, 7, u * C_HEADS:(u + 1) * C_HEADS], fwd[:, lo:lo + P], tbl[:], start=True, stop=True,
                                        skip_group_check=True)
            last.then_inc(cb_done, 1)
            for t in range(4):
                s, half = t // 2, t % 2
                slot = st.wait(pe, seg, t).rearrange("p (c n) -> p c n", c=8)
                for cc in range(8):
                    c = 8 * half + cc
                    for j in range(2):
                        nc.tensor.matmul(ps[:, 2 * s + j, 0:NB], slot[:, cc, j * P:(j + 1) * P],
                                         kk[:, s, :, 2 * c:2 * c + CMP_STRIDE * (CMP_BLOCKS - 1) + 1:CMP_STRIDE],
                                         start=(c == 0), stop=(c == 15))
                        last = nc.tensor.matmul(ps[:, 4 + j, s:s + 1], slot[:, cc, j * P:(j + 1) * P], pe_t[:, s, c:c + 1],
                                                start=(c == 0), stop=(c == 15), skip_group_check=True)
                last.then_inc(st.used, 1)
            pe.wait_ge(hid_done, 4)
            for j in range(2):
                nc.tensor.matmul(ps[0:64, 6, 0:NB], w2[:, 0, j, :], hid[:, 0, j, :], start=(j == 0), stop=(j == 1))
            pe.wait_ge(cb_done, 2)
            for gr in range(C_GROUPS):
                for j in range(2):
                    last = nc.tensor.matmul(ps[0:CMP_BLOCKS, 7, 64 * gr:64 * gr + 64], hid[:, 1, j, gr * CMP_BLOCKS:(gr + 1) * CMP_BLOCKS],
                                            w2[:, 1, j, :], start=(j == 0), stop=(j == 1), skip_group_check=True)
            last.then_inc(kv_done, 1)

        @block.vector
        def _(dve):
            dve.wait_ge(cb_done, 1)
            nc.vector.tensor_copy(cb[:].rearrange("p u h -> p (u h)"), ps[:, 7, 0:CB_SPAN * C_HEADS]).then_inc(cb_done, 1)
            dve.wait_ge(st.used, seg["start"] + 4)
            for j in range(2):
                nc.vector.tensor_copy(pe_b[:, :, j], ps[:, 4 + j, 0:2]).then_inc(pe_kept, 1)
            dve.wait_ge(kv_done, 1)
            for half in range(2):
                nc.vector.tensor_copy(kc[64 * half:64 * half + 64].rearrange("p g c -> p (g c)"), ps[0:64, 6, 0:NB])
            nc.vector.tensor_copy(vc[:].rearrange("p g c -> p (g c)"), ps[0:CMP_BLOCKS, 7, 0:P])

        @block.scalar
        def _(act):
            nc.scalar.activation(gate[:].rearrange("p i k -> p (i k)"), gate[:].rearrange("p i k -> p (i k)"), ACT.Sigmoid)
            act.wait_ge(pe_kept, 2)
            for s in range(2):
                for j in range(2):
                    nc.scalar.activation(hid[:, s, j, :], ps[:, 2 * s + j, 0:NB], ACT.Gelu_apprx_tanh,
                                         bias=pe_b[:, s, j:j + 1], scale=1.0).then_inc(hid_done, 1)


def lru_decay(g, par, decay):
    nc = g.nc
    with ExitStack() as ctx:
        sb = lambda n: ctx.enter_context(nc.sbuf_tensor(f"decay_{n}", [BW, GATES], F32))
        par_in, step_done, exp_done = (nc.alloc_semaphore(f"decay_{n}") for n in ("params_in", "step", "exp_done"))
        neg, low, u, den, inv, z, z2, series = (sb(n) for n in ("neg", "low", "u", "den", "inv", "z", "z2", "series"))
        block = ctx.enter_context(nc.Block())
        lam = par[:, 7, :]

        @block.sync
        def _(sp):
            sp.dma_start(par[:], g.a["f_lru"]).then_inc(par_in, 16)

        @block.scalar
        def _(act):
            act.wait_ge(step_done, 2)
            nc.scalar.activation(u[:], low[:], ACT.Exp).then_inc(exp_done, 1)

        @block.vector
        def _(dve):
            steps = [0]

            def step(ins):
                steps[0] += 1
                ins.then_inc(step_done, 1)
                dve.wait_ge(step_done, steps[0])

            dve.wait_ge(par_in, 16)
            step(nc.vector.tensor_scalar(neg[:], lam, -1.0, None, ALU.mult))
            step(nc.vector.tensor_tensor(low[:], lam, neg[:], ALU.min))
            dve.wait_ge(exp_done, 1)
            step(nc.vector.tensor_scalar(den[:], u[:], 2.0, None, ALU.add))
            step(nc.vector.reciprocal(inv[:], den[:]))
            step(nc.vector.tensor_tensor(z[:], u[:], inv[:], ALU.mult))
            step(nc.vector.tensor_tensor(z2[:], z[:], z[:], ALU.mult))
            step(nc.vector.tensor_scalar(series[:], z2[:], 1.0 / 19, None, ALU.mult))
            for k in (17, 15, 13, 11, 9, 7, 5, 3):
                step(nc.vector.scalar_tensor_tensor(out=series[:], in0=series[:], scalar=1.0 / k, in1=z2[:], op0=ALU.add, op1=ALU.mult))
            step(nc.vector.scalar_tensor_tensor(out=series[:], in0=series[:], scalar=1.0, in1=z[:], op0=ALU.add, op1=ALU.mult))
            step(nc.vector.tensor_scalar(neg[:], neg[:], 0.0, -C_RG, ALU.max, ALU.mult))
            step(nc.vector.scalar_tensor_tensor(out=decay[:], in0=series[:], scalar=-2.0 * C_RG, in1=neg[:], op0=ALU.mult, op1=ALU.add))


def rglru(g, y, par, decay):
    nc, ps, st, seg, a = g.nc, g.ps, g.st, g.seg_lru, g.a
    with ExitStack() as ctx:
        sb = lambda n, s: ctx.enter_context(nc.sbuf_tensor(n, s, F32))
        sem = lambda n: nc.alloc_semaphore(n)
        K = 4
        pad = sb("lru_pad", [BW, 2, S + 3])
        xb = sb("lru_xb", [BW, 2, S])
        w = sb("lru_work", [BW, 2, 9, S])
        R, I, SG, LA, A, TH, E2, IX, GT = range(9)
        zeroed = sem("lru_zeroed")
        in_done, pad_kept, xb_ready, ri_done, sig_done, la_done, exp_done, em_done, sq_done, y_done, vstep, ystep = (sem(f"lru_{n}") for n in
            ("in_done", "x_kept", "conv_ready", "gates_done", "sigmoids_done", "log_decay_ready", "exps_done", "expm1_ready", "root_done", "y_done", "conv_step", "recurrence_step"))
        block = ctx.enter_context(nc.Block())
        last_t = GATES - 1

        @block.sync
        def _(sp):
            st.feed(sp, seg)

        @block.gpsimd
        def _(pool):
            pool.memset(pad[:, :, 0:3], 0.0).then_inc(zeroed, 1)

        @block.tensor
        def _(pe):
            def inputs(t, turn):
                slot = st.wait(pe, seg, t, turn)
                wv = slot[:, 0:CH * 2 * BW].rearrange("p (c s n) -> p c s n", c=CH, s=2)
                if turn is not None or t >= 2:
                    pe.wait_ge(sig_done, at(turn, 1, t) - 1)
                for s in range(2):
                    for c in range(CH):
                        last = nc.tensor.matmul(ps[0:BW, 2 * (t % 2) + s, :], wv[:, c, s, :], g.h[:, c, :],
                                                start=(c == 0), stop=(c == CH - 1))
                last.then_inc(in_done, 1)

            def gates(t, turn):
                slot = st.ring[:, (seg["start"] + t) % RING, :]
                pe.wait_ge(xb_ready, at(turn, 1, t) + 1)
                for s in range(2):
                    last = nc.tensor.matmul(ps[0:BW, 4 + 2 * (t % 2) + s, :], slot[0:BW, CH * 2 * BW + s * BW:CH * 2 * BW + (s + 1) * BW],
                                            xb[:, t % 2, :], start=True, stop=True)
                last.then_inc(st.used, 1)

            def tile(t, turn):
                inputs(t, turn)
                if turn is not None or t:
                    gates(t - 1, turn)
            loop_tiles(pe, GATES, RING, tile)
            gates(last_t, None)

        @block.scalar
        def _(act):
            act.wait_ge(zeroed, 1)

            def move(t, turn):
                act.wait_ge(in_done, at(turn, 1, t) + 1)
                if turn is not None or t >= 2:
                    act.wait_ge(xb_ready, at(turn, 1, t) - 1)
                nc.scalar.copy(pad[:, t % 2, 3:S + 3], ps[0:BW, 2 * (t % 2), :]).then_inc(pad_kept, 1)

            def gate(t, turn):
                r = t % 2
                n = at(turn, 1, t)
                act.wait_ge(st.used, n + (seg["start"] + 1))
                if turn is not None or t >= 2:
                    act.wait_ge(y_done, n - 1)
                col = lambda k: par[:, k, bass.ds(n, 1)]
                nc.scalar.activation(w[:, r, R, :], ps[0:BW, 4 + 2 * r, :], ACT.Sigmoid, bias=col(5), scale=1.0)
                nc.scalar.activation(w[:, r, I, :], ps[0:BW, 5 + 2 * r, :], ACT.Sigmoid, bias=col(6), scale=1.0)
                nc.scalar.copy(w[:, r, GT, :], ps[0:BW, 2 * r + 1, :])
                nc.scalar.activation(w[:, r, SG, :], ps[0:BW, 2 * r + 1, :], ACT.Sigmoid).then_inc(sig_done, 1)
                act.wait_ge(la_done, n + 1)
                nc.scalar.activation(w[:, r, A, :], w[:, r, LA, :], ACT.Exp)
                nc.scalar.activation(w[:, r, TH, :], w[:, r, LA, :], ACT.Tanh).then_inc(exp_done, 1)
                act.wait_ge(em_done, n + 1)
                nc.scalar.activation(w[:, r, E2, :], w[:, r, E2, :], ACT.Sqrt, bias=0.0, scale=-1.0).then_inc(sq_done, 1)

            def tile(t, turn):
                move(t, turn)
                if turn is not None or t:
                    gate(t - 1, turn)
            loop_tiles(act, GATES, RING, tile)
            gate(last_t, None)

        @block.vector
        def _(dve):
            dve.wait_ge(zeroed, 1)

            def conv(t, turn):
                r = t % 2
                n = at(turn, 1, t)
                m = at(turn, 3, t)
                col = lambda k: par[:, k, bass.ds(n, 1)]
                dve.wait_ge(pad_kept, n + 1)
                if turn is not None or t >= 2:
                    dve.wait_ge(em_done, n - 1)
                    dve.wait_ge(st.used, n + (seg["start"] - 1))
                nc.vector.tensor_scalar(xb[:, r, :], pad[:, r, 3:S + 3], col(3), col(4), ALU.mult, ALU.add).then_inc(vstep, 1)
                for k in (2, 1):
                    dve.wait_ge(vstep, m + (3 - k))
                    nc.vector.scalar_tensor_tensor(out=xb[:, r, :], in0=pad[:, r, k:S + k], scalar=col(k), in1=xb[:, r, :],
                                                   op0=ALU.mult, op1=ALU.add).then_inc(vstep, 1)
                dve.wait_ge(vstep, m + 3)
                nc.vector.scalar_tensor_tensor(out=xb[:, r, :], in0=pad[:, r, 0:S], scalar=col(0), in1=xb[:, r, :],
                                               op0=ALU.mult, op1=ALU.add).then_inc(xb_ready, 1)

            def recur(t, turn):
                r = t % 2
                n = at(turn, 1, t)
                m = at(turn, 4, t)
                dve.wait_ge(sig_done, n + 1)
                nc.vector.tensor_scalar(w[:, r, LA, :], w[:, r, R, :], decay[:, bass.ds(n, 1)], None, ALU.mult).then_inc(la_done, 1)
                nc.vector.tensor_tensor(w[:, r, IX, :], w[:, r, I, :], xb[:, r, :], ALU.mult).then_inc(ystep, 1)
                dve.wait_ge(exp_done, n + 1)
                nc.vector.tensor_tensor(w[:, r, E2, :], w[:, r, A, :], w[:, r, A, :], ALU.mult).then_inc(ystep, 1)
                dve.wait_ge(ystep, m + 2)
                nc.vector.scalar_tensor_tensor(out=w[:, r, E2, :], in0=w[:, r, E2, :], scalar=1.0, in1=w[:, r, TH, :],
                                               op0=ALU.add, op1=ALU.mult).then_inc(em_done, 1)
                dve.wait_ge(sq_done, n + 1)
                nc.vector.tensor_tensor(w[:, r, IX, :], w[:, r, IX, :], w[:, r, E2, :], ALU.mult).then_inc(ystep, 1)
                nc.vector.tensor_tensor(w[:, r, SG, :], w[:, r, SG, :], w[:, r, GT, :], ALU.mult)
                dve.wait_ge(ystep, m + 3)
                nc.vector.tensor_tensor_scan(w[:, r, TH, :], w[:, r, A, :], w[:, r, IX, :], 0.0, ALU.mult, ALU.add).then_inc(ystep, 1)
                dve.wait_ge(ystep, m + 4)
                dst = y[:, t, :] if turn is None else y[:, bass.ds(n, 1), :].rearrange("p c n -> p (c n)")
                nc.vector.tensor_tensor(dst, w[:, r, TH, :], w[:, r, SG, :], ALU.mult).then_inc(y_done, 1)

            def tile(t, turn):
                conv(t, turn)
                if turn is not None or t:
                    recur(t - 1, turn)
            loop_tiles(dve, GATES, RING, tile)
            recur(last_t, None)


def retention(g, y):
    nc, a = g.nc, g.a
    with ExitStack() as ctx:
        sb = lambda n, s: ctx.enter_context(nc.sbuf_tensor(n, s, F32))
        q, k, v = sb("r_q", [P, 2, S]), sb("r_k", [P, 2, S]), sb("r_v", [P, NT, R_V])
        gate = sb("r_gate", [P, 4, S])
        cs = sb("r_trig", [P, 2, S])
        dec = sb("r_decay", [P, R_HEADS, S])
        load_small(g, "ret_consts", [(cs[:], a["c_rotary"].rearrange("k p t -> p k t")), (dec[:], a["c_decay"].rearrange("h p t -> p h t"))])
        for h in range(R_HEADS):
            plan = [[features(128 * j, P, 256, g.h, [(q[:, j, :], 0, P, 1.0, 0)]) for j in range(2)],
                    [features(128 * j, P, 256, g.h, [(k[:, j, :], 0, P, R_QK ** -0.5, 0)]) for j in range(2)]]
            plan += [[tokens(0, 256, 256, g.h, lambda i, t=t: v[:, i, 256 * t:256 * (t + 1)])] for t in range(2)]
            plan += [[features(128 * j, P, 256, g.h, [(gate[:, 2 * t + j, :], 0, P, 1.0, 0)]) for j in range(2)] for t in range(2)]
            project(g, f"ret{h}_proj", g.seg_ret[h], plan)
            retain(g, h, q, k, v, gate, cs, dec, y)


def retain(g, h, q, k, v, gate, cs, dec, y):
    nc, ps = g.nc, g.ps
    n_ = f"ret{h}_"
    with ExitStack() as ctx:
        sb = lambda n, s: ctx.enter_context(nc.sbuf_tensor(n_ + n, s, F32))
        sem = lambda n: nc.alloc_semaphore(n_ + n)
        qr, kr = sb("q_turned", [P, 2, S]), sb("k_turned", [P, 2, S])
        tmp = sb("tmp", [P, 2, 2, S])
        s_t = sb("scores_t", [P, NT, S])
        o = sb("out", [P, 4, S])
        sq = sb("squares", [P, 4, S])
        rs = sb("rstd", [P, 4, S])
        part, turned, s_done, s_kept, o_done, o_kept, mean_done, centred, squared, sq_done, vs, rstd, silu, normed = (sem(n) for n in
            ("products", "turned", "scores_done", "scores_kept", "values_done", "out_kept", "mean_done", "centred", "squared",
             "squares_summed", "vector_step", "root_ready", "silu_done", "normed"))
        block = ctx.enter_context(nc.Block())
        cos, sin = cs[:, 0, :], cs[:, 1, :]

        @block.vector
        def _(dve):
            n = 0
            for src, dst in ((q, qr), (k, kr)):
                for half in range(2):
                    x1, x2 = (src[:, 0, :], src[:, 1, :]) if half == 0 else (src[:, 1, :], src[:, 0, :])
                    nc.vector.tensor_tensor(tmp[:, n % 2, 0, :], x1, cos, ALU.mult).then_inc(part, 1)
                    nc.vector.tensor_tensor(tmp[:, n % 2, 1, :], x2, sin, ALU.mult).then_inc(part, 1)
                    dve.wait_ge(part, 2 * (n + 1))
                    nc.vector.tensor_tensor(dst[:, half, :], tmp[:, n % 2, 0, :], tmp[:, n % 2, 1, :],
                                            ALU.add if half else ALU.subtract).then_inc(turned, 1)
                    n += 1
            for kb in range(NT):
                w = S - kb * P
                dve.wait_ge(s_done, kb + 1)
                nc.vector.tensor_tensor(s_t[:, kb, 0:w], ps[:, kb, 0:w], dec[:, h, 0:w], ALU.mult).then_inc(s_kept, 1)
            for c in range(4):
                dve.wait_ge(o_done, c + 1)
                nc.vector.tensor_copy(o[:, c, :], ps[:, 4 + c, :]).then_inc(o_kept, 1)
            dve.wait_ge(mean_done, 1)
            nc.vector.tensor_scalar(rs[:, 0, :], ps[:, 0, :], 1.0 / R_V, None, ALU.mult).then_inc(vs, 1)
            dve.wait_ge(vs, 1)
            for c in range(4):
                nc.vector.tensor_tensor(o[:, c, :], o[:, c, :], rs[:, 0, :], ALU.subtract).then_inc(centred, 1)
            dve.wait_ge(sq_done, 1)
            nc.vector.tensor_scalar(rs[:, 1, :], ps[:, 1, :], 1.0 / R_V, GN_EPS, ALU.mult, ALU.add).then_inc(vs, 1)
            dve.wait_ge(vs, 2)
            nc.vector.reciprocal(rs[:, 2, :], rs[:, 1, :]).then_inc(rstd, 1)
            dve.wait_ge(rstd, 2)
            for c in range(4):
                nc.vector.tensor_tensor(o[:, c, :], o[:, c, :], rs[:, 3, :], ALU.mult).then_inc(normed, 1)
            for c in range(4):
                dve.wait_ge(normed, c + 1)
                dve.wait_ge(silu, c + 1)
                nc.vector.tensor_tensor(y[:, 4 * h + c, :], o[:, c, :], gate[:, c, :], ALU.mult)

        @block.tensor
        def _(pe):
            pe.wait_ge(turned, 4)
            for kb in range(NT):
                for c in range(2):
                    last = nc.tensor.matmul(ps[:, kb, 0:S - kb * P], kr[:, c, kb * P:(kb + 1) * P], qr[:, c, kb * P:S],
                                            start=(c == 0), stop=(c == 1))
                last.then_inc(s_done, 1)
            for c in range(4):
                for kb in range(NT):
                    pe.wait_ge(s_kept, kb + 1)
                    last = nc.tensor.matmul(ps[:, 4 + c, kb * P:S], v[:, kb, c * P:(c + 1) * P], s_t[:, kb, 0:S - kb * P],
                                            start=(kb == 0), stop=(kb == NT - 1), skip_group_check=True)
                last.then_inc(o_done, 1)
            for c in range(4):
                pe.wait_ge(o_kept, c + 1)
                last = nc.tensor.matmul(ps[:, 0, :], g.mean_w[:], o[:, c, :], start=(c == 0), stop=(c == 3))
            last.then_inc(mean_done, 1)
            for c in range(4):
                pe.wait_ge(squared, c + 1)
                last = nc.tensor.matmul(ps[:, 1, :], g.mean_w[:], sq[:, c, :], start=(c == 0), stop=(c == 3))
            last.then_inc(sq_done, 1)

        @block.scalar
        def _(act):
            for c in range(4):
                nc.scalar.activation(gate[:, c, :], gate[:, c, :], ACT.Silu).then_inc(silu, 1)
            for c in range(4):
                act.wait_ge(centred, c + 1)
                nc.scalar.activation(sq[:, c, :], o[:, c, :], ACT.Square).then_inc(squared, 1)
            act.wait_ge(rstd, 1)
            nc.scalar.activation(rs[:, 3, :], rs[:, 2, :], ACT.Sqrt).then_inc(rstd, 1)


def finish(g, out, src):
    nc, ps = g.nc, g.ps
    with ExitStack() as ctx:
        sem = lambda n: nc.alloc_semaphore(n)
        xt = ctx.enter_context(nc.sbuf_tensor("out_tokens", [P, NT, D], F32))
        turned, kept, out_done = sem("out_turned"), sem("out_kept"), sem("out_stored")
        block = ctx.enter_context(nc.Block())

        @block.tensor
        def _(pe):
            for t in range(NT):
                for half in range(2):
                    for c in range(4):
                        last = nc.tensor.transpose(ps[:, 2 * t + half, c * P:(c + 1) * P],
                                                   src[:, 4 * half + c, t * P:(t + 1) * P], g.ident[:])
                    last.then_inc(turned, 1)

        @block.vector
        def _(dve):
            for t in range(NT):
                for half in range(2):
                    dve.wait_ge(turned, 2 * t + half + 1)
                    nc.vector.tensor_copy(xt[:, t, half * S:(half + 1) * S], ps[:, 2 * t + half, :]).then_inc(kept, 1)

        @block.sync
        def _(sp):
            o = out.rearrange("b (t p) d -> p (b t) d", p=P)
            for t in range(NT):
                sp.wait_ge(kept, 2 * (t + 1))
                sp.dma_start(o[:, t, :], xt[:, t, :]).then_inc(out_done, 16)
            sp.wait_ge(out_done, 16 * NT)


def program(nc, a, out, stop=None):
    with ExitStack() as ctx:
        g = Program(nc, ctx, a)
        g.plan()
        chunks = lambda t: [t[:, c, :] for c in range(CH)]
        todo = []

        def even():
            even_mixer(g, g.h)

        def ffn(l):
            with nc.sbuf_tensor(f"ffn{l}_act", [P, FF_CH, S], F32) as act_t:
                with nc.sbuf_tensor(f"ffn{l}_taps", [P, 4, FF_CH], F32) as cw:
                    ffn_up(g, l, act_t, cw)
                down(g, f"ffn{l}_down", g.seg_down[l], act_t, P, "ln", 2 * l + 1, FF_CH)

        def pre(l):
            rms(g, f"pre{l}", [{"src": chunks(g.x), "dst": chunks(g.h), "n": D, "eps": RMS_EPS_2,
                                "gain": [g.norm_pre[:, l, c:c + 1] for c in range(CH)]}])

        def lru():
            pre(0)
            with nc.sbuf_tensor("lru_y", [BW, GATES, S], F32) as y:
                with nc.sbuf_tensor("lru_params", [BW, 8, GATES], F32) as par, nc.sbuf_tensor("lru_decay", [BW, GATES], F32) as decay:
                    lru_decay(g, par, decay)
                    rglru(g, y, par, decay)
                down(g, "lru_down", g.seg_lru_out, y, BW, "rms", 0, GATES)

        def ret():
            pre(1)
            with nc.sbuf_tensor("ret_y", [P, 16, S], F32) as y:
                retention(g, y)
                down(g, "ret_down", g.seg_ret_out, y, P, "rms", 1, 16)

        stages = [("start", lambda: start(g)), ("even", even),
                  ("ln0", lambda: down(g, "ev_down", g.seg_ev_out, g.h, P, "ln", 0, 6)),
                  ("ffn0", lambda: ffn(0)), ("odd", lambda: odd_mixer(g, g.h)),
                  ("ln2", lambda: down(g, "od_down", g.seg_od_out, g.h, P, "ln", 2, 8)),
                  ("ffn1", lambda: ffn(1)), ("lru", lru), ("ret", ret)]
        held = nc.snapshot_sems()
        for name, stage in stages:
            stage()
            nc.clear_and_free_semaphores(nc.allocated_since(held))
            nc.all_engine_barrier()
            if name == stop:
                break
        finish(g, out, g.h if stop in ("even", "odd") else g.x)


def shape_tables():
    import numpy as np
    f32 = np.float32

    def bucket(dist):
        n = np.maximum(dist, 0)
        nf = np.maximum(n, 1).astype(f32)
        large = 16 + (np.log(nf / f32(16)) / f32(math.log(2048 / 16)) * f32(16)).astype(np.int32)
        return np.where(n < 16, n, np.minimum(large, 31))

    def onehot(dist, valid):
        t = np.zeros((33, dist.size), f32)
        t[bucket(dist), np.arange(dist.size)] = 1.0
        t[:, ~valid] = 0.0
        t[32] = ~valid
        return t

    dist = np.arange(TOE) - (P - 1)
    kinds = [dist >= 0, (dist >= 0) & (dist <= 128), (dist >= 0) & (dist % 4 == 0), (dist >= 0) & (dist % 16 == 0)]
    fwd = np.arange(FWD_LEN) - FWD_OFF
    out = {"c_ident": np.eye(P, dtype=f32),
           "c_onehot": np.stack([onehot(dist, v) for v in kinds]),
           "c_onehot_fwd": onehot(fwd, fwd >= 0),
           "c_neg": np.full((1, 16), NEG, f32)}
    half = D_ROPE // 2
    swap = np.zeros((D_ROPE, D_ROPE), f32)
    for i in range(half):
        swap[half + i, i] = -1.0
        swap[i, half + i] = 1.0
    pos = np.arange(S, dtype=f32)
    ang = pos[None, :] * (f32(10000.0) ** (-np.arange(half, dtype=f32) / f32(half)))[:, None]
    c, s = np.tile(np.cos(ang), (2, 1)), np.tile(np.sin(ang), (2, 1))
    sc = f32((D_NOPE + D_ROPE) ** -0.5)
    out["c_rope_swap"] = swap
    out["c_rope_trig"] = np.stack([c, s, c * sc, s * sc]).astype(f32)
    ang = pos[None, :] * (f32(10000.0) ** (-np.arange(0, R_QK, 2, dtype=f32) / f32(R_QK)))[:, None]
    out["c_rotary"] = np.stack([np.cos(ang), np.sin(ang)]).astype(f32)
    log_g = np.log(1.0 - np.exp2(-5.0 - np.arange(R_HEADS, dtype=np.float64)))
    diff = np.arange(S)[None, :] - np.arange(P)[:, None]
    out["c_decay"] = np.where(diff[None] >= 0, np.exp(np.maximum(diff, 0)[None] * log_g[:, None, None]), 0.0).astype(f32)
    return out


def arranged(inputs):
    import numpy as np
    v = {n: np.asarray(x) for n, x in inputs.items()}
    small = ("ln_g", "ln_b", "norm_pre_2", "norm_post_2", "ffn_conv_w", "ffn_conv_b", "ev_subln", "od_cmp_pe", "od_q_norm",
             "od_kv_norm", "lru_conv_w_2", "lru_conv_b_2", "lru_b_a_2", "lru_b_x_2", "lru_lambda_2")
    out = {n: x for n, x in v.items() if n not in small}

    def columns(x, p=P):
        x = x.reshape(x.shape[:-1] + (x.shape[-1] // p, p))
        return np.moveaxis(x, -1, 0)

    out["f_ln_g"] = columns(v["ln_g"].reshape(2 * DEPTH, D))
    out["f_ln_b"] = columns(v["ln_b"].reshape(2 * DEPTH, D))
    out["f_norm_pre"], out["f_norm_post"] = columns(v["norm_pre_2"]), columns(v["norm_post_2"])
    taps = np.concatenate([v["ffn_conv_w"], v["ffn_conv_b"][:, None]], axis=1)
    out["f_ffn_conv"] = np.stack([columns(t) for t in taps])
    out["f_subln"] = v["ev_subln"].reshape(P, 1)
    out["f_cmp_pe"] = columns(v["od_cmp_pe"][0].reshape(2, CMP_LEN * C_DIM))
    out["f_q_norm"], out["f_kv_norm"] = columns(v["od_q_norm"][0]), columns(v["od_kv_norm"][0])
    out["f_lru"] = columns(np.concatenate([v["lru_conv_w_2"][0]] + [v[n] for n in
                           ("lru_conv_b_2", "lru_b_a_2", "lru_b_x_2", "lru_lambda_2")]), BW)
    return out


def kernel(**inputs):
    import numpy as _np
    import concourse.bacc as _bacc
    from concourse import mybir as _mybir
    from concourse.bass_utils import run_bass_kernel_spmd as _run

    nc = _bacc.Bacc("TRN2", target_bir_lowering=False, num_devices=1)
    arrays, args = {}, {}
    for name, value in {**arranged(inputs), **shape_tables()}.items():
        a = _np.ascontiguousarray(value)
        arrays[f"in_{name}_dram"] = a
        args[name] = nc.dram_tensor(f"in_{name}_dram", a.shape, _mybir.dt.from_np(a.dtype), kind="ExternalInput").ap()
    out = nc.dram_tensor("out_0_dram", (1, S, D), F32, kind="ExternalOutput").ap()
    program(nc, args, out)
    r = _run(nc, [arrays], core_ids=[0])
    return r.results[0]["out_0_dram"]
```

```python
import math
from contextlib import ExitStack

import concourse.bass as bass
from concourse import mybir

F32 = mybir.dt.float32
F32R = mybir.dt.float32r
ALU = mybir.AluOpType
ACT = mybir.ActivationFunctionType
AX_X = mybir.AxisListType.X

P = 128
D = 1024
S = 512
NT = S // P
CH = D // P
RING = 4
SLOT = 2048
NEG = -1.0e30
LN_EPS = 1e-5
RMS_EPS = 1e-5
RMS_EPS_2 = 1e-6
GN_EPS = 1e-5
DEPTH = 2
ALPHA = (2 * DEPTH) ** 0.25
LAM_INIT = 0.8 - 0.6 * math.exp(-0.3 * 0)

A_HEADS, A_QK, A_V = 4, 64, 128
B_HEADS, B_DIM, N_PAIRS = 4, 64, 3
C_HEADS, C_DIM, C_GROUPS = 8, 64, 2
CMP_BLOCKS, CMP_LEN, CMP_STRIDE, CMP_HIDDEN = 31, 32, 16, 256
D_HEADS, D_NOPE, D_ROPE, D_V = 8, 64, 32, 64
D_Q_LORA, D_KV_LORA = 384, 256
D_FF = 2816
FF_CH = D_FF // P
D_RNN = 1536
GATES, BW = 16, 96
C_RG = 8.0
R_HEADS, R_QK, R_V = 4, 256, 512

TOE = 640
STD, WIN, DIL4, DIL16 = range(4)
KINDS = 4
TCOLS = 17
CB_SPAN = 55
FWD_OFF = 511
FWD_LEN = FWD_OFF + 24 * CMP_STRIDE - 31 + P


class Stream:

    def __init__(self, nc, ctx):
        self.nc = nc
        self.ring = ctx.enter_context(nc.sbuf_tensor("weight_ring", [P, RING, SLOT], F32))
        self.high = ctx.enter_context(nc.sbuf_tensor("weight_high", [P, 2, SLOT], F32R))
        self.low = ctx.enter_context(nc.sbuf_tensor("weight_low", [P, 2, SLOT], F32R))
        self.loaded = [ctx.enter_context(nc.semaphore(f"weights_loaded_{s}")) for s in range(RING)]
        self.high_ready = ctx.enter_context(nc.semaphore("weights_high_ready"))
        self.ready = ctx.enter_context(nc.semaphore("weights_ready"))
        self.used = ctx.enter_context(nc.semaphore("weights_used"))
        self.tiles = 0
        self.count = [0] * RING
        self.segments = []

    def segment(self, count, pieces, load, size=SLOT, kp=P):
        seg = {"start": self.tiles, "count": count, "pieces": pieces, "load": load, "base": list(self.count),
               "size": size, "kp": kp}
        for t in range(count):
            self.count[(self.tiles + t) % RING] += 16 * pieces
        self.tiles += count
        self.segments.append(seg)
        return seg

    def issue(self, sp, seg, t, turn=None):
        n = seg["start"] + t
        slot = n % RING
        t_now = t if turn is None else turn * RING + t
        if n >= RING:
            sp.wait_ge(self.ready, seg["start"] - RING + 1 + t_now)
        for dst, src in seg["load"](t_now, self.ring[:, slot, :]):
            sp.dma_start(dst, src).then_inc(self.loaded[slot], 16)

    def rest(self, sp, seg):
        turns = (seg["count"] - RING) // RING
        if turns > 1:
            with sp.Fori(0, turns) as turn:
                for t in range(RING, 2 * RING):
                    self.issue(sp, seg, t, turn)
        else:
            turns = 0
        for t in range(RING * (turns + 1), seg["count"]):
            self.issue(sp, seg, t)

    def first(self, sp, seg):
        for t in range(min(RING, seg["count"])):
            self.issue(sp, seg, t)

    def feed(self, sp, seg):
        self.rest(sp, seg)
        k = self.segments.index(seg)
        if k + 1 < len(self.segments):
            self.first(sp, self.segments[k + 1])

    def _part(self, store, seg, t):
        size = seg["size"] if isinstance(seg["size"], int) else seg["size"][t]
        return store[0:seg["kp"], (seg["start"] + t) % (RING if store is self.ring else 2), 0:size]

    def take_high(self, act, seg, t, turn=None):
        slot = (seg["start"] + t) % RING
        level = seg["base"][slot] + 16 * seg["pieces"] * (t // RING + 1)
        act.wait_ge(self.loaded[slot], level if turn is None else turn * (16 * seg["pieces"]) + level)
        if seg["start"] + t >= 2:
            act.wait_ge(self.used, at(turn, 1, t) + (seg["start"] - 1))
        self.nc.scalar.copy(self._part(self.high, seg, t), self._part(self.ring, seg, t)).then_inc(self.high_ready, 1)

    def take_low(self, dve, seg, t, turn=None):
        dve.wait_ge(self.high_ready, at(turn, 1, t) + (seg["start"] + 1))
        self.nc.vector.tensor_tensor(self._part(self.low, seg, t), self._part(self.ring, seg, t),
                                     self._part(self.high, seg, t).bitcast(F32), ALU.subtract).then_inc(self.ready, 1)

    def next(self, take, eng, seg, t, turn=None):
        if turn is not None or t + 1 < seg["count"]:
            take(eng, seg, t + 1, turn)
        else:
            k = self.segments.index(seg)
            if k + 1 < len(self.segments):
                take(eng, self.segments[k + 1], 0)

    def wait(self, pe, seg, t, turn=None):
        pe.wait_ge(self.ready, at(turn, 1, t) + (seg["start"] + 1))
        slot = (seg["start"] + t) % 2
        return self.high[:, slot, :], self.low[:, slot, :]


def passes(w, x):
    return [(w[0], x[0]), (w[0], x[1]), (w[1], x[0])]


def loop_tiles(eng, count, first, body):
    for t in range(first):
        body(t, None)
    turns = (count - first - 1) // RING
    if turns > 1:
        with eng.Fori(0, turns) as turn:
            for t in range(first, first + RING):
                body(t, turn)
    else:
        turns = 0
    for t in range(first + turns * RING, count):
        body(t, None)


def at(turn, step, t):
    return step * t if turn is None else turn * (step * RING) + step * t


class Program:
    def __init__(self, nc, ctx, a):
        self.nc, self.a = nc, a
        sb = lambda name, shape: ctx.enter_context(nc.sbuf_tensor(name, shape, F32))
        self.x = sb("residual", [P, CH, S])
        self.h = sb("mixer_in", [P, CH, S])
        self.parts = self.parts_scope = None
        self.ident = sb("ident", [P, P])
        self.mean_w = sb("mean_weights", [P, P])
        self.ln_g = sb("ln_gain", [P, 2 * DEPTH, CH])
        self.ln_b = sb("ln_shift", [P, 2 * DEPTH, CH])
        self.norm_pre = sb("norm_pre", [P, DEPTH, CH])
        self.norm_post = sb("norm_post", [P, DEPTH, CH])
        self.ps = ctx.enter_context(nc.psum_tensor("banks", [P, 8, S], F32))
        self.st = Stream(nc, ctx)
        self.rev = nc.dram_tensor("distance_rows", [KINDS, TCOLS, TOE], F32, kind="Internal")

    def open_parts(self, name):
        self.parts_scope = ExitStack()
        self.parts = tuple(self.parts_scope.enter_context(self.nc.sbuf_tensor(f"{name}_{part}", [P, CH, S], F32R, side="right"))
                           for part in ("high", "low"))

    def close_parts(self):
        self.parts_scope.close()

    def plan(self):
        st, a = self.st, self.a

        def cols(w, col_of, width):
            w_v = w.rearrange("(c p) n -> p c n", p=P)
            chunks = w_v.shape[1]
            def load(t, slot):
                view = slot[:, 0:chunks * width].rearrange("p (c n) -> p c n", c=chunks)
                return [(view, w_v[:, :, bass.ds(col_of(t), width)])]
            return load

        def rows(w, kp):
            w_v = w.rearrange("(t c p) n -> p t c n", p=kp, c=2)
            def load(t, slot):
                view = slot[0:kp, :].rearrange("p (c n) -> p c n", c=2)
                return [(view, w_v[:, bass.ds(t, 1), :, :].rearrange("p t c n -> p (t c) n"))]
            return load

        def ffn_up(l):
            w_v = a["ffn_w_up"][l].rearrange("(c p) (s n) -> p c s n", p=P, s=2)
            def load(t, slot):
                view = slot.rearrange("p (c s n) -> p c s n", c=CH, s=2)
                return [(view[:, :, s, :], w_v[:, :, s, bass.ds(t * P, P)]) for s in range(2)]
            return load

        ev = a["ev_w_in"][0]
        self.seg_a = st.segment(6, 1, cols(ev, lambda t: t * 256, 256))
        self.seg_b = st.segment(9, 1, cols(ev, lambda t: (t + 6) * 256, 256))
        self.seg_ev_out = st.segment(3, 1, rows(a["ev_w_out"][0], P))
        self.seg_up, self.seg_down = [None, None], [None, None]
        self.seg_up[0] = st.segment(FF_CH, 2, ffn_up(0))
        self.seg_down[0] = st.segment(FF_CH // 2, 1, rows(a["ffn_w_down"][0], P))
        od = a["od_w_in"][0].rearrange("(c p) n -> p c n", p=P)
        C0 = 2 * 512 + 3 * 2 * 2 * 64 - 512
        gate0, cq0 = C0, C0 + 24
        ckv0 = cq0 + D_Q_LORA
        kr0 = ckv0 + D_KV_LORA
        self.od_tiles = [(0, 256), (256, 256), (512, 256), (768, 256), (1024, 256), (gate0, 24), (kr0 - 96, P),
                         (cq0, 256), (cq0 + 256, 256), (cq0 + 512, 128)]
        def load_od(t, slot):
            c, w = self.od_tiles[t]
            return [(slot[:, 0:CH * w].rearrange("p (c n) -> p c n", c=CH), od[:, :, c:c + w])]
        self.seg_od = st.segment(len(self.od_tiles), 1, load_od, [CH * w for _, w in self.od_tiles])
        w1 = a["od_cmp_w1"][0].rearrange("s (u c p) n -> s u p c n", p=P, u=2)
        def load_w1(t, slot):
            return [(slot.rearrange("p (c n) -> p c n", c=8), w1[t // 2, t % 2])]
        self.seg_cmp = st.segment(4, 1, load_w1)
        uq = a["od_w_uq"][0].rearrange("(c p) n -> p c n", p=P)
        def load_mla(t, slot):
            if t < 2:
                return [(slot[:, 0:3 * 384].rearrange("p (c n) -> p c n", c=3), uq[:, :, 384 * t:384 * (t + 1)])]
            w = a["od_w_uk" if t == 2 else "od_w_uv"][0]
            return [(slot[:, 0:1024].rearrange("p (c n) -> p c n", c=2), w.rearrange("(c p) n -> p c n", p=P))]
        self.seg_mla = st.segment(4, 1, load_mla, [3 * 384, 3 * 384, 1024, 1024])
        self.seg_od_out = st.segment(4, 1, rows(a["od_w_out"][0], P))
        self.seg_up[1] = st.segment(FF_CH, 2, ffn_up(1))
        self.seg_down[1] = st.segment(FF_CH // 2, 1, rows(a["ffn_w_down"][1], P))
        lru = a["lru_w_in_2"][0].rearrange("(c p) (s n) -> p c s n", p=P, s=2)
        def load_lru(t, slot):
            view = slot[:, 0:CH * 2 * BW].rearrange("p (c s n) -> p c s n", c=CH, s=2)
            return [(view[:, :, s, :], lru[:, :, s, bass.ds(t * BW, BW)]) for s in range(2)]
        self.seg_lru = st.segment(GATES, 2, load_lru, CH * 2 * BW)
        self.seg_lru_out = st.segment(GATES // 2, 1, rows(a["lru_w_out_2"][0], BW), SLOT, BW)
        ret = a["ret_w_in_2"][0]
        def ret_col(t):
            h, k = divmod(t, 6)
            return [256 * h, 1024 + 256 * h, 2048 + 512 * h, 2048 + 512 * h + 256,
                    4096 + 512 * h, 4096 + 512 * h + 256][k]
        self.seg_ret = [st.segment(6, 1, cols(ret, lambda t, h=h: ret_col(6 * h + t), 256)) for h in range(R_HEADS)]
        self.seg_ret_out = st.segment(R_HEADS * 2, 1, rows(a["ret_w_out_2"][0], P))


def start(g):
    nc, a, ps = g.nc, g.a, g.ps
    with ExitStack() as ctx:
        sb = lambda n, s: ctx.enter_context(nc.sbuf_tensor(n, s, F32))
        sem = lambda n: nc.alloc_semaphore(n)
        xt = sb("x_tokens", [P, NT, D])
        onehot = sb("onehot", [33, KINDS, TOE])
        tbl = sb("bias_table", [33, TCOLS])
        rows = sb("distance_rows_sb", [TCOLS, KINDS, TOE])
        x_in, small_in, const_in, high = sem("x_in"), sem("small_in"), sem("const_in"), sem("x_high")
        turned, kept, rows_done, rows_kept, rows_out, cleared = (
            sem("x_turned"), sem("x_kept"), sem("rows_done"), sem("rows_kept"), sem("rows_out"), sem("table_cleared"))
        block = ctx.enter_context(nc.Block())

        @block.sync
        def _(sp):
            sp.dma_start(xt[:], a["x"].rearrange("b (t p) d -> p (b t) d", p=P)).then_inc(x_in, 16)
            sp.dma_start(g.ident[:], a["c_ident"]).then_inc(x_in, 16)
            sp.dma_start(onehot[:], a["c_onehot"].rearrange("k b m -> b k m")).then_inc(const_in, 16)
            sp.wait_ge(cleared, 2)
            sp.dma_start(tbl[0:32, 0:16], a["rel_bias"]).then_inc(const_in, 16)
            g.st.first(sp, g.seg_a)
            for dst, src in ((g.ln_g, "f_ln_g"), (g.ln_b, "f_ln_b"), (g.norm_pre, "f_norm_pre"), (g.norm_post, "f_norm_post")):
                sp.dma_start(dst[:], a[src]).then_inc(small_in, 16)
            sp.wait_ge(rows_kept, 2 * KINDS)
            sp.dma_start(g.rev.rearrange("k h m -> h k m"), rows[:]).then_inc(rows_out, 16)
            sp.wait_ge(rows_out, 16)
            sp.wait_ge(small_in, 16 * 4)

        @block.gpsimd
        def _(pool):
            pool.memset(g.mean_w[:], 1.0)
            pool.memset(tbl[:], 0.0).then_inc(cleared, 1)
            pool.wait_ge(cleared, 1)
            pool.memset(tbl[32:33, :], NEG).then_inc(cleared, 1)

        @block.tensor
        def _(pe):
            pe.wait_ge(x_in, 32)
            for c in range(CH):
                for t in range(NT):
                    last = nc.tensor.transpose(ps[:, c % 4, t * P:(t + 1) * P], xt[:, t, c * P:(c + 1) * P], g.ident[:])
                    if t == 0 and c >= 4:
                        pass
                last.then_inc(turned, 1)
                if c >= 3 and c < CH - 1:
                    pe.wait_ge(kept, c - 2)
            pe.wait_ge(const_in, 32)
            pe.wait_ge(cleared, 2)
            for k in range(KINDS):
                for half in range(2):
                    lo = half * (TOE // 2)
                    nc.tensor.matmul(ps[0:TCOLS, 4 + (2 * k + half) % 4, 0:TOE // 2], tbl[:], onehot[:, k, lo:lo + TOE // 2],
                                     start=True, stop=True).then_inc(rows_done, 1)
                    if 2 * k + half >= 3 and 2 * k + half < 2 * KINDS - 1:
                        pe.wait_ge(rows_kept, 2 * k + half - 2)

        @block.vector
        def _(dve):
            for c in range(CH):
                dve.wait_ge(turned, c + 1)
                nc.vector.tensor_copy(g.x[:, c, :], ps[:, c % 4, :]).then_inc(kept, 1)
            for c in range(CH):
                dve.wait_ge(high, c + 1)
                nc.vector.tensor_tensor(g.parts[1][:, c, :], g.x[:, c, :], g.parts[0][:, c, :].bitcast(F32), ALU.subtract)
            g.st.take_low(dve, g.seg_a, 0)

        @block.scalar
        def _(act):
            for c in range(CH):
                act.wait_ge(kept, c + 1)
                nc.scalar.copy(g.parts[0][:, c, :], g.x[:, c, :]).then_inc(high, 1)
            for u in range(2 * KINDS):
                act.wait_ge(rows_done, u + 1)
                lo = (u % 2) * (TOE // 2)
                nc.scalar.copy(rows[:, u // 2, lo:lo + TOE // 2], ps[0:TCOLS, 4 + u % 4, 0:TOE // 2]).then_inc(rows_kept, 1)
            g.st.take_high(act, g.seg_a, 0)


def project(g, name, seg, plan):
    nc, ps, st = g.nc, g.ps, g.st
    units = []
    for t, tile in enumerate(plan):
        for item in tile:
            if item["kind"] == "F":
                units.append((t, item, None))
            else:
                units += [(t, item, q) for q in range(NT)]
    with ExitStack() as ctx:
        sem = lambda n: nc.alloc_semaphore(n)
        done = sem(f"{name}_tile_done")
        kept = [sem(f"{name}_kept_by_scalar"), sem(f"{name}_kept_by_vector")]
        block = ctx.enter_context(nc.Block())

        @block.sync
        def _(sp):
            st.feed(sp, seg)

        last_of = [u + 1 == len(units) or units[u + 1][0] != units[u][0] for u in range(len(units))]

        def wait_product(eng, u):
            if last_of[u]:
                eng.wait_ge(st.used, seg["start"] + units[u][0] + 1)
            else:
                eng.wait_ge(done, last_of[:u + 1].count(False))

        @block.tensor
        def _(pe):
            now = -1
            for u, (t, item, q) in enumerate(units):
                if t != now:
                    slot = st.wait(pe, seg, t)
                    now = t
                if u >= 8:
                    pe.wait_ge(kept[u % 2], (u - 8) // 2 + 1)
                width, col, n = item["tile"], item["col"], item["n"]
                chunks = item["x"][0].shape[1]
                both = [part[:, 0:chunks * width].rearrange("p (c n) -> p c n", c=chunks) for part in slot]
                for c in range(chunks):
                    for k, (w, x) in enumerate(passes(both, item["x"])):
                        first, final = c == 0 and k == 0, c == chunks - 1 and k == 2
                        if q is None:
                            last = nc.tensor.matmul(ps[0:n, u % 8, :], w[:, c, col:col + n], x[:, c, :], start=first, stop=final)
                        else:
                            last = nc.tensor.matmul(ps[:, u % 8, 0:n], x[:, c, q * P:(q + 1) * P], w[:, c, col:col + n],
                                                    start=first, stop=final)
                last.then_inc(st.used if last_of[u] else done, 1)

        def keep(eng, parity):
            now = -1
            for u, (t, item, q) in enumerate(units):
                if t != now:
                    now = t
                    st.next((st.take_high, st.take_low)[parity], eng, seg, t)
                if u % 2 != parity:
                    continue
                wait_product(eng, u)
                if q is None:
                    outs = [(dst, ps[lo:hi, u % 8, c0:c0 + dst.shape[-1]], scale) for dst, lo, hi, scale, c0 in item["out"]]
                else:
                    outs = [(item["out"](q), ps[:, u % 8, 0:item["n"]], 1.0)]
                for dst, bank, scale in outs:
                    if parity == 0:
                        last = nc.scalar.mul(dst, bank, scale)
                    else:
                        last = nc.vector.tensor_scalar(dst, bank, scale, None, ALU.mult)
                last.then_inc(kept[parity], 1)

        @block.scalar
        def _(act):
            keep(act, 0)

        @block.vector
        def _(dve):
            keep(dve, 1)


def features(col, n, tile, x, out):
    return {"kind": "F", "col": col, "n": n, "tile": tile, "x": x, "out": out}


def tokens(col, n, tile, x, out):
    return {"kind": "T", "col": col, "n": n, "tile": tile, "x": x, "out": out}


def attention(g, name, heads, shared, tables, out_of, gate_of=None, next_seg=None):
    nc, ps, st = g.nc, g.ps, g.st
    NH = len(heads)
    U = max(len(u) for u in heads)
    width = lambda u, i: len(u["blocks"](i)) * u["klen"]
    cap = max(sum(width(u, i) for u in us for i in range(NT)) for us in heads)

    def packs(u):
        where, bank, col = {}, 0, 0
        for kb in sorted({kb for i in range(NT) for kb in u["blocks"](i)}):
            ts = [i for i in range(NT) if kb in u["blocks"](i)]
            if col + len(ts) * P > S:
                bank, col = bank + 1, 0
            where[kb] = (bank, col, ts[0], len(ts))
            col += len(ts) * P
        return where, bank + 1

    flat = [(h, k, u) for h in range(NH) for k, u in enumerate(heads[h])]
    first_of = [0]
    for us in heads:
        first_of.append(first_of[-1] + len(us))
    banks_before = [0]
    for h, k, u in flat:
        banks_before.append(banks_before[-1] + packs(u)[1])

    with ExitStack() as ctx:
        sb = lambda n, s: ctx.enter_context(nc.sbuf_tensor(n, s, F32))
        sem = lambda n: nc.alloc_semaphore(n)
        sc = sb(f"{name}_scores", [P, 2, cap])
        pt = sb(f"{name}_weights_t", [P, 2, 3 * S])
        stat = sb(f"{name}_stats", [P, 2, 6, U, NT])
        s_ready, s_kept, negmax, exped, normed = (sem(f"{name}_{n}") for n in
            ("scores_ready", "scores_kept", "negmax_ready", "exp_done", "weights_ready"))
        t_ready, t_kept, pv_done, o_kept, dve_step = (sem(f"{name}_{n}") for n in
            ("turned", "turned_kept", "values_done", "out_kept", "vector_step"))
        table_in = [sem(f"{name}_table_in_{s}") for s in range(2)]
        block = ctx.enter_context(nc.Block())

        def place(h, k, i):
            o = 0
            for kk, u in enumerate(heads[h]):
                for ii in range(NT):
                    w = width(u, ii)
                    if (kk, ii) == (k, i):
                        return o, w
                    o += w

        @block.sync
        def _(sp):
            if next_seg is not None:
                st.first(sp, next_seg)
            for h in range(NH):
                if h >= 2:
                    sp.wait_ge(s_kept, NT * first_of[h - 1])
                for dst, src in tables(h, h % 2):
                    sp.dma_start(dst, src).then_inc(table_in[h % 2], 16)

        @block.tensor
        def _(pe):
            def scores(h):
                for k, u in enumerate(heads[h]):
                    n = first_of[h] + k
                    for i in range(NT):
                        if n:
                            pe.wait_ge(s_kept, NT * (n - 1) + i + 1)
                        kb = u["blocks"](i)
                        nc.tensor.matmul(ps[:, i, 0:width(u, i)], u["q"][:, i * P:(i + 1) * P],
                                         u["k"](kb[0], width(u, i)), start=True, stop=True).then_inc(s_ready, 1)

            def values(h):
                dv0, dv = out_of(h)[1:3]
                o = ps[dv0:dv0 + dv, 7, :]
                total = sum(len(packs(u)[0]) for u in heads[h])
                done = 0
                for k, u in enumerate(heads[h]):
                    n = first_of[h] + k
                    where, nb = packs(u)
                    for b in range(nb):
                        if n:
                            pe.wait_ge(t_kept, banks_before[n])
                        for kb in sorted(where):
                            bank, col, i0, cnt = where[kb]
                            if bank != b:
                                continue
                            for i in range(i0, i0 + cnt):
                                pe.wait_ge(normed, NT * n + i + 1)
                                off, w = place(h, k, i)
                                j = u["blocks"](i).index(kb) * u["klen"]
                                last = nc.tensor.transpose(ps[0:u["klen"], 4 + bank, col + (i - i0) * P:col + (i - i0 + 1) * P],
                                                           sc[:, h % 2, off + j:off + j + u["klen"]], g.ident[:])
                        last.then_inc(t_ready, 1)
                    for kb in sorted(where):
                        bank, col, i0, cnt = where[kb]
                        pe.wait_ge(t_kept, banks_before[n] + bank + 1)
                        if done == 0 and h:
                            pe.wait_ge(o_kept, h)
                        last = nc.tensor.matmul(o[:, i0 * P:(i0 + cnt) * P], u["v"](kb),
                                                pt[0:u["klen"], n % 2, bank * S + col:bank * S + col + cnt * P],
                                                start=(done == 0), stop=(done == total - 1), skip_group_check=True)
                        done += 1
                    last.then_inc(pv_done, 1)

            scores(0)
            for h in range(NH):
                if h + 1 < NH:
                    scores(h + 1)
                values(h)

        @block.vector
        def _(dve):
            steps = [0]

            def step(ins):
                steps[0] += 1
                ins.then_inc(dve_step, 1)
                dve.wait_ge(dve_step, steps[0])

            def masked(h):
                slot = h % 2
                dve.wait_ge(table_in[slot], 16 * sum(len(tables(hh, hh % 2)) for hh in range(slot, h + 1, 2)))
                if h >= 2:
                    dve.wait_ge(t_ready, banks_before[first_of[h - 1]])
                for k, u in enumerate(heads[h]):
                    n = first_of[h] + k
                    for i in range(NT):
                        off, w = place(h, k, i)
                        dve.wait_ge(s_ready, NT * n + i + 1)
                        nc.vector.tensor_tensor_reduce(sc[:, slot, off:off + w], ps[:, i, 0:w], u["bias"](i), 1.0, 3 * NEG,
                                                       ALU.add, ALU.max, stat[:, slot, 0, k, i:i + 1]).then_inc(s_kept, 1)
                nu = len(heads[h])
                dve.wait_ge(s_kept, NT * first_of[h + 1])
                if shared:
                    step(nc.vector.tensor_reduce(stat[:, slot, 5, 0, :], stat[:, slot, 0, :, :].rearrange("p u i -> p i u"),
                                                 AX_X, ALU.max))
                    nc.vector.tensor_scalar(stat[:, slot, 1, 0, :], stat[:, slot, 5, 0, :], -1.0, None, ALU.mult).then_inc(negmax, 1)
                else:
                    for k, u in enumerate(heads[h]):
                        ins = nc.vector.tensor_scalar(stat[:, slot, 1, k, :], stat[:, slot, 0, k, :],
                                                      NEG * 1e-8 if u.get("guard") else 3 * NEG, -1.0, ALU.max, ALU.mult)
                    ins.then_inc(negmax, 1)

            def normal(h):
                slot = h % 2
                nu = len(heads[h])
                dve.wait_ge(exped, NT * first_of[h + 1])
                if shared:
                    step(nc.vector.tensor_reduce(stat[:, slot, 5, 0, :], stat[:, slot, 2, :, :].rearrange("p u i -> p i u"),
                                                 AX_X, ALU.add))
                    step(nc.vector.reciprocal(stat[:, slot, 4, 0, :], stat[:, slot, 5, 0, :]))
                else:
                    step(nc.vector.tensor_scalar(stat[:, slot, 5, 0:nu, :], stat[:, slot, 2, 0:nu, :], 1e-30, None, ALU.max))
                    step(nc.vector.reciprocal(stat[:, slot, 4, 0:nu, :], stat[:, slot, 5, 0:nu, :]))
                    if gate_of is not None:
                        for k in range(nu):
                            if gate_of(h, k) is not None:
                                ins = nc.vector.tensor_tensor(stat[:, slot, 4, k, :], stat[:, slot, 4, k, :], gate_of(h, k), ALU.mult)
                        step(ins)
                for k, u in enumerate(heads[h]):
                    for i in range(NT):
                        off, w = place(h, k, i)
                        kk = 0 if shared else k
                        nc.vector.tensor_scalar(sc[:, slot, off:off + w], sc[:, slot, off:off + w],
                                                stat[:, slot, 4, kk, i:i + 1], None, ALU.mult).then_inc(normed, 1)

            masked(0)
            for h in range(NH):
                if h + 1 < NH:
                    masked(h + 1)
                normal(h)

        @block.scalar
        def _(act):
            def exps(h):
                act.wait_ge(negmax, h + 1)
                if h >= 2:
                    act.wait_ge(normed, NT * first_of[h - 1])
                for k, u in enumerate(heads[h]):
                    for i in range(NT):
                        off, w = place(h, k, i)
                        kk = 0 if shared else k
                        nc.scalar.activation(sc[:, h % 2, off:off + w], sc[:, h % 2, off:off + w], ACT.Exp,
                                             bias=stat[:, h % 2, 1, kk, i:i + 1], scale=1.0,
                                             accum_out=stat[:, h % 2, 2, k, i:i + 1]).then_inc(exped, 1)

            exps(0)
            for h in range(NH):
                if h + 1 < NH:
                    exps(h + 1)
                for k, u in enumerate(heads[h]):
                    n = first_of[h] + k
                    where, nb = packs(u)
                    for b in range(nb):
                        act.wait_ge(t_ready, banks_before[n] + b + 1)
                        if n >= 2:
                            act.wait_ge(pv_done, n - 1)
                        cols = max(col + cnt * P for bank, col, _, cnt in where.values() if bank == b)
                        nc.scalar.copy(pt[0:u["klen"], n % 2, b * S:b * S + cols], ps[0:u["klen"], 4 + b, 0:cols]).then_inc(t_kept, 1)
                act.wait_ge(pv_done, first_of[h + 1])
                dst, dv0, dv = out_of(h)
                nc.scalar.copy(dst, ps[dv0:dv0 + dv, 7, :]).then_inc(o_kept, 1)


def down(g, name, seg, src, kp, kind, l, src_chunks):
    nc, ps, st = g.nc, g.ps, g.st
    ntile = src_chunks // 2
    if kind == "ln":
        g.open_parts(name)
    with ExitStack() as ctx:
        sb = lambda n, s: ctx.enter_context(nc.sbuf_tensor(n, s, F32))
        sem = lambda n: nc.alloc_semaphore(n)
        sq = g.h
        y = sb(f"{name}_y", [P, CH, S]) if kind == "rms" else g.x
        rs = sb(f"{name}_rstd", [P, 3, S])
        sh, sl = (ctx.enter_context(nc.sbuf_tensor(f"{name}_src_{n}", [P, 4, S], F32R)) for n in ("high", "low"))
        src_high, src_low, x_done, x_high = (sem(f"{name}_{n}") for n in ("source_high", "source_low", "x_done", "x_high"))
        y_kept, mean_done, centred, squared, sq_done, v_step, rstd, scaled = (sem(f"{name}_{n}") for n in
            ("y_kept", "mean_done", "centred", "squared", "squares_summed", "vector_step", "root_ready", "scaled"))
        block = ctx.enter_context(nc.Block())

        def pair(t, turn):
            return src[0:kp, 2 * t:2 * t + 2, :] if turn is None else src[0:kp, bass.ds(turn * (2 * RING) + 2 * t, 2), :]

        @block.sync
        def _(sp):
            st.feed(sp, seg)

        @block.tensor
        def _(pe):
            def tile(t, turn):
                parts = [part[0:kp, :].rearrange("p (c n) -> p c n", c=2) for part in st.wait(pe, seg, t, turn)]
                pe.wait_ge(src_low, at(turn, 1, t) + 1)
                for j in range(2):
                    xs = [part[0:kp, 2 * (t % 2) + j, :] for part in (sh, sl)]
                    for b in range(8):
                        for k, (w, x) in enumerate(passes(parts, xs)):
                            last = nc.tensor.matmul(ps[:, b, :], w[:, j, b * P:(b + 1) * P], x,
                                                    start=(turn is None and t == 0 and j == 0 and k == 0),
                                                    stop=(turn is None and t == ntile - 1 and j == 1 and k == 2),
                                                    skip_group_check=True)
                last.then_inc(st.used, 1)
            loop_tiles(pe, ntile, 1, tile)
            if kind == "ln":
                pe.wait_ge(y_kept, 1)
                for c in range(CH):
                    pe.wait_ge(y_kept, c + 1)
                    last = nc.tensor.matmul(ps[:, 0, :], g.mean_w[:], y[:, c, :], start=(c == 0), stop=(c == CH - 1))
                last.then_inc(mean_done, 1)
            else:
                pe.wait_ge(y_kept, 2)
            for c in range(CH):
                pe.wait_ge(squared, c + 1)
                last = nc.tensor.matmul(ps[:, 1, :], g.mean_w[:], sq[:, c, :], start=(c == 0), stop=(c == CH - 1))
            last.then_inc(sq_done, 1)

        @block.vector
        def _(dve):
            steps = [0]

            def step(ins):
                steps[0] += 1
                ins.then_inc(v_step, 1)
                dve.wait_ge(v_step, steps[0])

            def low(t, turn):
                lo = 2 * (t % 2)
                dve.wait_ge(src_high, at(turn, 1, t) + 1)
                nc.vector.tensor_tensor(sl[0:kp, lo:lo + 2, :], pair(t, turn), sh[0:kp, lo:lo + 2, :].bitcast(F32),
                                        ALU.subtract).then_inc(src_low, 1)

            def tile(t, turn):
                st.next(st.take_low, dve, seg, t, turn)
                if turn is not None or t + 1 < ntile:
                    low(t + 1, turn)
            low(0, None)
            loop_tiles(dve, ntile, 1, tile)
            dve.wait_ge(st.used, seg["start"] + ntile)
            if kind == "ln":
                for c in range(CH):
                    nc.vector.scalar_tensor_tensor(out=g.x[:, c, :], in0=g.x[:, c, :], scalar=ALPHA, in1=ps[:, c, :],
                                                   op0=ALU.mult, op1=ALU.add).then_inc(y_kept, 1)
                dve.wait_ge(mean_done, 1)
                step(nc.vector.tensor_scalar(rs[:, 0, :], ps[:, 0, :], 1.0 / D, None, ALU.mult))
                for c in range(CH):
                    nc.vector.tensor_tensor(g.x[:, c, :], g.x[:, c, :], rs[:, 0, :], ALU.subtract).then_inc(centred, 1)
            else:
                for c in range(CH):
                    nc.vector.tensor_copy(y[:, c, :], ps[:, c, :]).then_inc(y_kept, 1)
            dve.wait_ge(sq_done, 1)
            step(nc.vector.tensor_scalar(rs[:, 1, :], ps[:, 1, :], 1.0 / D, LN_EPS if kind == "ln" else RMS_EPS_2, ALU.mult, ALU.add))
            nc.vector.reciprocal(rs[:, 2, :], rs[:, 1, :]).then_inc(rstd, 1)
            dve.wait_ge(rstd, 2)
            for c in range(CH):
                if kind == "ln":
                    nc.vector.scalar_tensor_tensor(out=g.x[:, c, :], in0=g.x[:, c, :], scalar=g.ln_g[:, l, c:c + 1],
                                                   in1=rs[:, 0, :], op0=ALU.mult, op1=ALU.mult).then_inc(scaled, 1)
                else:
                    nc.vector.scalar_tensor_tensor(out=y[:, c, :], in0=y[:, c, :], scalar=g.norm_post[:, l, c:c + 1],
                                                   in1=rs[:, 0, :], op0=ALU.mult, op1=ALU.mult).then_inc(scaled, 1)
            if kind == "rms":
                for c in range(CH):
                    dve.wait_ge(scaled, c + 1)
                    nc.vector.tensor_tensor(g.x[:, c, :], g.x[:, c, :], y[:, c, :], ALU.add)
            else:
                for c in range(CH):
                    dve.wait_ge(x_high, c + 1)
                    nc.vector.tensor_tensor(g.parts[1][:, c, :], g.x[:, c, :], g.parts[0][:, c, :].bitcast(F32), ALU.subtract)

        @block.scalar
        def _(act):
            def high(t, turn):
                if turn is not None or t >= 2:
                    act.wait_ge(st.used, at(turn, 1, t) + (seg["start"] - 1))
                lo = 2 * (t % 2)
                nc.scalar.copy(sh[0:kp, lo:lo + 2, :], pair(t, turn)).then_inc(src_high, 1)

            def tile(t, turn):
                st.next(st.take_high, act, seg, t, turn)
                if turn is not None or t + 1 < ntile:
                    high(t + 1, turn)
            high(0, None)
            loop_tiles(act, ntile, 1, tile)
            for c in range(CH):
                act.wait_ge(centred if kind == "ln" else y_kept, c + 1)
                nc.scalar.activation(sq[:, c, :], y[:, c, :], ACT.Square).then_inc(squared, 1)
            act.wait_ge(rstd, 1)
            nc.scalar.activation(rs[:, 0, :], rs[:, 2, :], ACT.Sqrt).then_inc(rstd, 1)
            if kind == "ln":
                for c in range(CH):
                    act.wait_ge(scaled, c + 1)
                    nc.scalar.activation(g.x[:, c, :], g.x[:, c, :], ACT.Identity, bias=g.ln_b[:, l, c:c + 1], scale=1.0).then_inc(x_done, 1)
                for c in range(CH):
                    act.wait_ge(x_done, c + 1)
                    nc.scalar.copy(g.parts[0][:, c, :], g.x[:, c, :]).then_inc(x_high, 1)


def ffn_up(g, l, act_t, cw):
    nc, ps, st, seg = g.nc, g.ps, g.st, g.seg_up[l]
    with ExitStack() as ctx:
        sb = lambda n, s: ctx.enter_context(nc.sbuf_tensor(n, s, F32))
        sem = lambda n: nc.alloc_semaphore(n)
        conv = sb(f"ffn{l}_conv", [P, RING, S + 2])
        gel = sb(f"ffn{l}_gelu", [P, RING, S])
        n_ = f"ffn{l}_"
        par_in, done, zeroed, g_kept, t1, t2, t3, gelu_done, act_done = (sem(n_ + n) for n in
            ("params_in", "tile_done", "margins_zero", "gate_copied", "tap_1", "tap_2", "tap_3", "gelu_done", "act_done"))
        block = ctx.enter_context(nc.Block())

        @block.sync
        def _(sp):
            sp.dma_start(cw[:], g.a["f_ffn_conv"][l]).then_inc(par_in, 16)
            st.feed(sp, seg)

        @block.tensor
        def _(pe):
            def tile(t, turn):
                both = [part.rearrange("p (c s n) -> p c s n", c=CH, s=2) for part in st.wait(pe, seg, t, turn)]
                if turn is not None or t >= RING:
                    pe.wait_ge(act_done, at(turn, 1, t) - (RING - 1))
                for s in (1, 0):
                    for c in range(CH):
                        for k, (w, x) in enumerate(passes(both, g.parts)):
                            last = nc.tensor.matmul(ps[:, 2 * (t % RING) + s, :], w[:, c, s, :], x[:, c, :],
                                                    start=(c == 0 and k == 0), stop=(c == CH - 1 and k == 2))
                    last.then_inc(done if s else st.used, 1)
            loop_tiles(pe, FF_CH, RING, tile)

        @block.gpsimd
        def _(pool):
            pool.memset(conv[:, :, 0:2], 0.0).then_inc(zeroed, 1)

        @block.scalar
        def _(act):
            act.wait_ge(par_in, 16)

            def tile(t, turn):
                st.next(st.take_high, act, seg, t, turn)
                act.wait_ge(done, at(turn, 1, t) + 1)
                if turn is not None or t >= RING:
                    act.wait_ge(t3, at(turn, 1, t) - (RING - 1))
                nc.scalar.copy(conv[:, t % RING, 2:S + 2], ps[:, 2 * (t % RING) + 1, :]).then_inc(g_kept, 1)
                act.wait_ge(t3, at(turn, 1, t) + 1)
                nc.scalar.activation(gel[:, t % RING, :], gel[:, t % RING, :], ACT.Gelu_apprx_tanh).then_inc(gelu_done, 1)
            loop_tiles(act, FF_CH, RING, tile)

        @block.vector
        def _(dve):
            dve.wait_ge(par_in, 16)
            dve.wait_ge(zeroed, 1)

            def tile(t, turn):
                f = bass.ds(at(turn, 1, t), 1)
                r = t % RING
                st.next(st.take_low, dve, seg, t, turn)
                tap = lambda k: cw[:, k, f]
                dve.wait_ge(g_kept, at(turn, 1, t) + 1)
                nc.vector.tensor_scalar(gel[:, r, :], conv[:, r, 2:S + 2], tap(2), tap(3), ALU.mult, ALU.add).then_inc(t1, 1)
                dve.wait_ge(t1, at(turn, 1, t) + 1)
                nc.vector.scalar_tensor_tensor(out=gel[:, r, :], in0=conv[:, r, 1:S + 1], scalar=tap(1), in1=gel[:, r, :],
                                               op0=ALU.mult, op1=ALU.add).then_inc(t2, 1)
                dve.wait_ge(t2, at(turn, 1, t) + 1)
                nc.vector.scalar_tensor_tensor(out=gel[:, r, :], in0=conv[:, r, 0:S], scalar=tap(0), in1=gel[:, r, :],
                                               op0=ALU.mult, op1=ALU.add).then_inc(t3, 1)
                dve.wait_ge(gelu_done, at(turn, 1, t) + 1)
                dve.wait_ge(st.used, at(turn, 1, t) + (seg["start"] + 1))
                dst = act_t[:, t, :] if turn is None else act_t[:, f, :].rearrange("p c n -> p (c n)")
                nc.vector.tensor_tensor(dst, gel[:, r, :], ps[:, 2 * r, :], ALU.mult).then_inc(act_done, 1)
            loop_tiles(dve, FF_CH, RING, tile)


def rms(g, name, groups):
    nc, ps = g.nc, g.ps
    flat = [(k, c) for k, gr in enumerate(groups) for c in range(len(gr["src"]))]
    with ExitStack() as ctx:
        sb = lambda n, s: ctx.enter_context(nc.sbuf_tensor(n, s, F32))
        sem = lambda n: nc.alloc_semaphore(n)
        G = len(groups)
        sq = sb(f"{name}_squares", [P, len(flat), S])
        rs = sb(f"{name}_rstd", [P, 3, G, S])
        squared, summed, ms_done, inv_done, root, scaled, high = (sem(f"{name}_{n}") for n in
            ("squared", "squares_summed", "mean_square", "inverse", "root_ready", "scaled", "high_done"))
        split = [(gr["dst"][c], gr["parts"][0][c], gr["parts"][1][c]) for gr in groups if "parts" in gr for c in range(len(gr["src"]))]
        block = ctx.enter_context(nc.Block())

        @block.scalar
        def _(act):
            for n, (k, c) in enumerate(flat):
                nc.scalar.activation(sq[:, n, :], groups[k]["src"][c], ACT.Square).then_inc(squared, 1)
            for k in range(G):
                act.wait_ge(inv_done, k + 1)
                nc.scalar.activation(rs[:, 2, k, :], rs[:, 1, k, :], ACT.Sqrt).then_inc(root, 1)
            for n, (dst, hi, lo) in enumerate(split):
                act.wait_ge(scaled, n + 1)
                nc.scalar.copy(hi, dst).then_inc(high, 1)

        @block.tensor
        def _(pe):
            for n, (k, c) in enumerate(flat):
                pe.wait_ge(squared, n + 1)
                last_c = c == len(groups[k]["src"]) - 1
                mm = nc.tensor.matmul(ps[:, k, :], g.mean_w[:], sq[:, n, :], start=(c == 0), stop=last_c)
                if last_c:
                    mm.then_inc(summed, 1)

        @block.vector
        def _(dve):
            for k, gr in enumerate(groups):
                m2 = gr.get("mult", 1.0) ** 2
                dve.wait_ge(summed, k + 1)
                nc.vector.tensor_scalar(rs[:, 0, k, :], ps[:, k, :], 1.0 / (gr["n"] * m2), gr["eps"] / m2,
                                        ALU.mult, ALU.add).then_inc(ms_done, 1)
                dve.wait_ge(ms_done, k + 1)
                nc.vector.reciprocal(rs[:, 1, k, :], rs[:, 0, k, :]).then_inc(inv_done, 1)
            for k, gr in enumerate(groups):
                dve.wait_ge(root, k + 1)
                for c, src in enumerate(gr["src"]):
                    nc.vector.scalar_tensor_tensor(out=gr["dst"][c], in0=src, scalar=gr["gain"][c], in1=rs[:, 2, k, :],
                                                   op0=ALU.mult, op1=ALU.mult).then_inc(scaled, 1)
            for n, (dst, hi, lo) in enumerate(split):
                dve.wait_ge(high, n + 1)
                nc.vector.tensor_tensor(lo, dst, hi.bitcast(F32), ALU.subtract)


def toeplitz(g, kind, col):
    base = g.rev[kind, col, :]
    return bass.AP(tensor=base.tensor, offset=base.offset, ap=[[1, P], [1, S]])


def biases(table, i, first_block=0):
    top = P * (i - first_block + 1) - 1
    return table[:, top::-1]


def causal(i):
    return list(range(i + 1))


def banded(i):
    return list(range(max(0, i - 1), i + 1))


def lambda_stage(g, neg_lam):
    nc, a = g.nc, g.a
    with ExitStack() as ctx:
        sb = lambda n, s: ctx.enter_context(nc.sbuf_tensor(n, s, F32))
        sem = lambda n: nc.alloc_semaphore(n)
        lp = sb("lambda_params", [P, 4, A_QK])
        prod = sb("lambda_products", [P, 2, A_QK])
        dots, ex = sb("lambda_dots", [P, 2]), sb("lambda_exps", [P, 2])
        lp_in, v, e = sem("lambda_in"), sem("lambda_vector"), sem("lambda_exp")
        block = ctx.enter_context(nc.Block())

        @block.sync
        def _(sp):
            sp.dma_start(lp[:], a["ev_lambda"][0].partition_broadcast(P)).then_inc(lp_in, 16)

        @block.vector
        def _(dve):
            dve.wait_ge(lp_in, 16)
            pairs = lp[:].rearrange("p (k two) d -> p two k d", two=2)
            nc.vector.tensor_tensor(prod[:], pairs[:, 0], pairs[:, 1], ALU.mult).then_inc(v, 1)
            dve.wait_ge(v, 1)
            nc.vector.tensor_reduce(dots[:], prod[:], AX_X, ALU.add).then_inc(v, 1)
            dve.wait_ge(e, 1)
            nc.vector.tensor_tensor(dots[:, 0:1], ex[:, 1:2], ex[:, 0:1], ALU.subtract).then_inc(v, 1)
            dve.wait_ge(v, 3)
            for i in range(NT):
                nc.vector.tensor_scalar(neg_lam[:, i:i + 1], dots[:, 0:1], -LAM_INIT, None, ALU.add)

        @block.scalar
        def _(act):
            act.wait_ge(v, 2)
            nc.scalar.activation(ex[:], dots[:], ACT.Exp).then_inc(e, 1)


def even_mixer(g, o):
    nc, a = g.nc, g.a
    with ExitStack() as ctx:
        sb = lambda n, s: ctx.enter_context(nc.sbuf_tensor(n, s, F32))
        neg_lam, sub_g = sb("neg_lambda", [P, NT]), sb("subln_gain", [P, 1])
        lambda_stage(g, neg_lam)
        with ExitStack() as inner:
            sbi = lambda n, s: inner.enter_context(nc.sbuf_tensor(n, s, F32))
            q, k, v = sbi("a_q", [P, 4, S]), sbi("a_k", [P, 4, S]), sbi("a_v", [P, NT, S])
            toe = sbi("a_tables", [P, 2, S])
            two = lambda dst, t, scale: [features(128 * j, P, 256, g.parts, [(dst[:, 2 * t + j, :], 0, P, scale, 0)]) for j in range(2)]
            plan = [two(q, t, A_QK ** -0.5) for t in range(2)] + [two(k, t, 1.0) for t in range(2)]
            plan += [[tokens(0, 256, 256, g.parts, lambda i, t=t: v[:, i, 256 * t:256 * (t + 1)])] for t in range(2)]
            project(g, "a_proj", g.seg_a, plan)

            def unit(h, m):
                n = m * A_HEADS + h
                lo = 64 * (n % 2)
                return {"q": q[lo:lo + 64, n // 2, :], "k": lambda kb, w: k[lo:lo + 64, n // 2, kb * P:kb * P + w],
                        "v": lambda kb: v[:, kb, h * A_V:(h + 1) * A_V], "blocks": causal, "klen": P,
                        "bias": lambda i: biases(toe[:, h % 2, :], i)}
            attention(g, "a_attn", [[unit(h, 0), unit(h, 1)] for h in range(A_HEADS)], False,
                      lambda h, s: [(toe[:, s, :], toeplitz(g, STD, h))],
                      lambda h: (o[:, h, :], 0, P), gate_of=lambda h, u: neg_lam[:] if u else None)
        with ExitStack() as inner:
            sbi = lambda n, s: inner.enter_context(nc.sbuf_tensor(n, s, F32))
            q, k, v = sbi("b_q", [P, 3, 2, S]), sbi("b_k", [P, 3, 2, S]), sbi("b_v", [P, 3, NT, 256])
            toe = sbi("b_tables", [P, 2, 3, S])
            plan = []
            for i in range(N_PAIRS):
                for dst, scale in ((q, B_DIM ** -0.5), (k, 1.0)):
                    plan.append([features(128 * j, P, 256, g.parts, [(dst[:, i, j, :], 0, P, scale, 0)]) for j in range(2)])
                plan.append([tokens(0, 256, 256, g.parts, lambda t, i=i: v[:, i, t, :])])
            project(g, "b_proj", g.seg_b, plan)
            g.close_parts()

            def unit(h, i):
                lo = 64 * (h % 2)
                return {"q": q[lo:lo + 64, i, h // 2, :], "k": lambda kb, w: k[lo:lo + 64, i, h // 2, kb * P:kb * P + w],
                        "v": lambda kb: v[:, i, kb, h * B_DIM:(h + 1) * B_DIM], "blocks": causal if i else banded, "klen": P,
                        "bias": lambda t: biases(toe[:, h % 2, i, :], t, 0 if i else max(0, t - 1))}
            attention(g, "b_attn", [[unit(h, i) for i in range(N_PAIRS)] for h in range(B_HEADS)], True,
                      lambda h, s: [(toe[:, s, i, :], toeplitz(g, (WIN, DIL4, DIL16)[i], A_HEADS + i * B_HEADS + h)) for i in range(N_PAIRS)],
                      lambda h: (o[64 * (h % 2):64 * (h % 2) + 64, 4 + h // 2, :], 64 * (h % 2), 64))
        load_small(g, "subln", [(sub_g[:, 0:1], a["f_subln"])])
        rms(g, "subln_norm", [{"src": [o[:, h, :]], "dst": [o[:, h, :]], "n": A_V, "eps": RMS_EPS, "gain": [sub_g[:, 0:1]],
                               "mult": 1.0 - LAM_INIT} for h in range(A_HEADS)])


def load_small(g, name, pairs, next_seg=None):
    nc = g.nc
    small_in = nc.alloc_semaphore(f"{name}_in")
    with nc.Block() as block:
        @block.sync
        def _(sp):
            for dst, src in pairs:
                sp.dma_start(dst, src).then_inc(small_in, 16)
            sp.wait_ge(small_in, 16 * len(pairs))


def odd_mixer(g, o):
    nc, a, ps, st = g.nc, g.a, g.ps, g.st
    with ExitStack() as ctx:
        sb = lambda n, s, c=ctx: c.enter_context(nc.sbuf_tensor(n, s, F32))
        lora = ctx.enter_context(ExitStack())
        far = lambda n, s, dt=F32: lora.enter_context(nc.sbuf_tensor(n, s, dt))
        cq, ckv = far("cq", [P, 3, S]), far("ckv", [P, 2, S])
        raw_k = far("k_rope_raw", [96, S])
        qg, kvg = far("q_norm_gain", [P, 3]), far("kv_norm_gain", [P, 2])
        with ExitStack() as inner:
            sbi = lambda n, s: sb(n, s, inner)
            qc = sbi("c_q", [P, 4, S])
            kd = sbi("c_k", [P, 2, C_GROUPS, S])
            vd = sbi("c_v", [P, 2, NT, P])
            gate = sbi("gates", [P, NT, 24])
            w2 = sbi("cmp_w2", [P, 2, 2, C_DIM])
            pe_b = sbi("cmp_pos_bias", [P, 2, 2])
            hid = sbi("cmp_hidden", [P, 2, 2, C_GROUPS * CMP_BLOCKS])
            kc = sbi("cmp_k", [P, C_GROUPS, CMP_BLOCKS])
            vc = sbi("cmp_v", [CMP_BLOCKS, C_GROUPS, C_DIM])
            cb = sbi("cmp_bias", [P, CB_SPAN, C_HEADS])
            fwd = sbi("onehot_fwd", [33, FWD_LEN])
            tbl = sbi("bias_table_c", [33, C_HEADS])
            toe = sbi("c_tables", [P, 2, S])
            cmp_scope = inner.enter_context(ExitStack())
            kk = sb("cmp_in", [P, 2, C_GROUPS, S], cmp_scope)
            pe_t = sb("cmp_pos", [P, 2, 16], cmp_scope)

            def both_halves(dst, gr):
                return [(dst[64 * half:64 * half + 64, gr, :], 64 * gr, 64 * gr + 64, 1.0, 0) for half in range(2)]

            def shifted(s):
                return [(kk[64 * half:64 * half + 64, s, gr, 0:S - half], 64 * gr, 64 * gr + 64, 1.0, half)
                        for gr in range(2) for half in range(2)]
            plan = [[features(128 * j, P, 256, g.parts, [(qc[:, 2 * t + j, :], 0, P, C_DIM ** -0.5, 0)]) for j in range(2)] for t in range(2)]
            plan.append([features(128 * s, P, 256, g.parts, shifted(s)) for s in range(2)])
            for b in range(2):
                plan.append([features(0, P, 256, g.parts, both_halves(kd[:, b], 0) + both_halves(kd[:, b], 1)),
                             tokens(128, P, 256, g.parts, lambda i, b=b: vd[:, b, i, :])])
            plan.append([tokens(0, 24, 24, g.parts, lambda i: gate[:, i, :])])
            plan.append([features(0, P, P, g.parts, [(raw_k[64:96, :], 96, P, 1.0, 0)])])
            plan.append([features(128 * j, P, 256, g.parts, [(cq[:, j, :], 0, P, 1.0, 0)]) for j in range(2)])
            plan.append([features(0, P, 256, g.parts, [(cq[:, 2, :], 0, P, 1.0, 0)]), features(128, P, 256, g.parts, [(ckv[:, 0, :], 0, P, 1.0, 0)])])
            plan.append([features(0, P, 128, g.parts, [(ckv[:, 1, :], 0, P, 1.0, 0)])])
            project(g, "od_proj", g.seg_od, plan)
            g.close_parts()
            load_small(g, "od_small", [
                (w2[:], a["od_cmp_w2"][0].rearrange("s (j p) n -> p s j n", p=P)),
                (pe_t[:], a["f_cmp_pe"]),
                (fwd[:], a["c_onehot_fwd"]), (tbl[0:32, :], a["rel_bias"][:, 0:C_HEADS]), (tbl[32:33, :], a["c_neg"][:, 0:C_HEADS]),
                (qg[:], a["f_q_norm"]),
                (kvg[:], a["f_kv_norm"])])
            compress(g, kk, w2, pe_t, pe_b, hid, kc, vc, cb, fwd, tbl, gate)
            cmp_scope.close()

            def units(h):
                lo, gr = 64 * (h % 2), h // 4
                q = qc[lo:lo + 64, h // 2, :]
                full = [{"q": q, "k": lambda kb, w, b=b: kd[lo:lo + 64, b, gr, kb * P:kb * P + w],
                         "v": lambda kb, b=b: vd[:, b, kb, 64 * gr:64 * gr + 64], "blocks": causal, "klen": P,
                         "bias": lambda i: biases(toe[:, h % 2, :], i)} for b in range(2)]
                cmp_ = {"q": q, "k": lambda kb, w: kc[lo:lo + 64, gr, :], "v": lambda kb: vc[:, gr, :], "blocks": lambda i: [0],
                        "klen": CMP_BLOCKS, "guard": True, "bias": lambda i: cb[:, 24 - 8 * i:24 - 8 * i + CMP_BLOCKS, h]}
                return [cmp_] + full
            attention(g, "c_attn", [units(h) for h in range(C_HEADS)], False,
                      lambda h, s: [(toe[:, s, :], toeplitz(g, STD, h))],
                      lambda h: (o[64 * (h % 2):64 * (h % 2) + 64, h // 2, :], 64 * (h % 2), 64),
                      gate_of=lambda h, u: gate[:, :, 8 * u + h])
        cqp = [far(f"cq_{n}", [P, 3, S], F32R) for n in ("high", "low")]
        ckvp = [far(f"ckv_{n}", [P, 2, S], F32R) for n in ("high", "low")]
        rms(g, "lora_norm", [
            {"parts": [[p[:, c, :] for c in range(3)] for p in cqp], "src": [cq[:, c, :] for c in range(3)], "dst": [cq[:, c, :] for c in range(3)], "n": D_Q_LORA, "eps": RMS_EPS,
             "gain": [qg[:, c:c + 1] for c in range(3)]},
            {"parts": [[p[:, c, :] for c in range(2)] for p in ckvp], "src": [ckv[:, c, :] for c in range(2)], "dst": [ckv[:, c, :] for c in range(2)], "n": D_KV_LORA, "eps": RMS_EPS,
             "gain": [kvg[:, c:c + 1] for c in range(2)]}])
        qm, km, vm = (ctx.enter_context(nc.sbuf_tensor(n, shape, F32, side="right")) for n, shape in
                      (("m_q", [96, D_HEADS, S]), ("m_k", [96, D_HEADS, S]), ("m_v", [P, NT, S])))
        rot = far("rope_swap", [96, 32])
        trig = far("rope_trig", [96, 4, S])
        scale = (D_NOPE + D_ROPE) ** -0.5
        plan = [[features(96 * j, 96, 384, cqp, [(qm[0:64, 4 * t + j, :], 0, 64, scale, 0), (qm[64:96, 4 * t + j, :], 64, 96, 1.0, 0)])
                 for j in range(4)] for t in range(2)]
        plan.append([features(128 * j, P, 512, ckvp, [(km[0:64, 2 * j + e, :], 64 * e, 64 * e + 64, 1.0, 0) for e in range(2)])
                     for j in range(4)])
        plan.append([tokens(0, 512, 512, ckvp, lambda i: vm[:, i, :])])
        project(g, "m_proj", g.seg_mla, plan)
        load_small(g, "rope", [(rot[64:96, :], a["c_rope_swap"]), (trig[64:96], a["c_rope_trig"].rearrange("k p t -> p k t"))])
        rope(g, qm, km, raw_k, rot, trig)
        lora.close()
        mask = sb("m_mask", [P, 2, S])

        def unit(h):
            return {"q": qm[:, h, :], "k": lambda kb, w: km[:, h, kb * P:kb * P + w], "v": lambda kb: vm[:, kb, 64 * h:64 * h + 64],
                    "blocks": causal, "klen": P, "bias": lambda i: biases(mask[:, h % 2, :], i)}
        attention(g, "m_attn", [[unit(h)] for h in range(D_HEADS)], False,
                  lambda h, s: [(mask[:, s, :], toeplitz(g, STD, 16))],
                  lambda h: (o[64 * (h % 2):64 * (h % 2) + 64, 4 + h // 2, :], 64 * (h % 2), 64))


def rope(g, qm, km, raw_k, rot, trig):
    nc, ps = g.nc, g.ps
    with ExitStack() as ctx:
        sem = lambda n: nc.alloc_semaphore(n)
        tmp = ctx.enter_context(nc.sbuf_tensor("rope_tmp", [96, 4, S], F32))
        swapped, part, turned, summed = sem("rope_swapped"), sem("rope_sin_part"), sem("rope_cos_part"), sem("rope_summed")
        src = [qm[64:96, h, :] for h in range(D_HEADS)] + [raw_k[64:96, :]]
        block = ctx.enter_context(nc.Block())

        @block.tensor
        def _(pe):
            for n, x in enumerate(src):
                if n >= 8:
                    pe.wait_ge(part, n - 7)
                nc.tensor.matmul(ps[64:96, n % 8, :], rot[64:96, :], x, start=True, stop=True).then_inc(swapped, 1)

        @block.vector
        def _(dve):
            for n, x in enumerate(src):
                k = 2 if n < D_HEADS else 0
                s = 2 * (n % 2)
                dve.wait_ge(swapped, n + 1)
                nc.vector.tensor_tensor(tmp[64:96, s, :], ps[64:96, n % 8, :], trig[64:96, k + 1, :], ALU.mult).then_inc(part, 1)
                nc.vector.tensor_tensor(tmp[64:96, s + 1, :], x, trig[64:96, k, :], ALU.mult).then_inc(turned, 1)
                dve.wait_ge(part, n + 1)
                dve.wait_ge(turned, n + 1)
                dst = x if n < D_HEADS else km[64:96, 0, :]
                nc.vector.tensor_tensor(dst, tmp[64:96, s, :], tmp[64:96, s + 1, :], ALU.add).then_inc(summed, 1)

        @block.gpsimd
        def _(pool):
            pool.wait_ge(summed, D_HEADS + 1)
            for h in range(1, D_HEADS):
                nc.gpsimd.tensor_copy(km[64:96, h, :], km[64:96, 0, :])


def compress(g, kk, w2, pe_t, pe_b, hid, kc, vc, cb, fwd, tbl, gate):
    nc, ps, st, seg = g.nc, g.ps, g.st, g.seg_cmp
    NB = C_GROUPS * CMP_BLOCKS
    with ExitStack() as ctx:
        sem = lambda n: nc.alloc_semaphore(n)
        cb_done, pe_kept, hid_done, kv_done, high, low = (sem(f"cmp_{n}") for n in
            ("bias_done", "pos_kept", "hidden_ready", "kv_done", "in_high", "in_low"))
        kk_parts = [ctx.enter_context(nc.sbuf_tensor(f"cmp_in_{n}", [P, 2, C_GROUPS, S], F32R)) for n in ("high", "low")]
        pos_parts = [ctx.enter_context(nc.sbuf_tensor(f"cmp_pos_{n}", [P, 2, 16, 2], F32R)) for n in ("high", "low")]
        splits = [(kk[64 * e:64 * e + 64, :, :, 0:S - e], *(p[64 * e:64 * e + 64, :, :, 0:S - e] for p in kk_parts)) for e in range(2)]
        splits += [(pe_t[:], *(p[:, :, :, e] for p in pos_parts)) for e in range(2)]
        block = ctx.enter_context(nc.Block())

        @block.sync
        def _(sp):
            st.feed(sp, seg)

        @block.tensor
        def _(pe):
            for u in range(CB_SPAN):
                lo = FWD_OFF + CMP_STRIDE * (24 - u) - (CMP_LEN - 1)
                last = nc.tensor.matmul(ps[:, 7, u * C_HEADS:(u + 1) * C_HEADS], fwd[:, lo:lo + P], tbl[:], start=True, stop=True,
                                        skip_group_check=True)
            last.then_inc(cb_done, 1)
            pe.wait_ge(low, 4)
            for t in range(4):
                s, half = t // 2, t % 2
                both = [part.rearrange("p (c n) -> p c n", c=8) for part in st.wait(pe, seg, t)]
                for cc in range(8):
                    c = 8 * half + cc
                    for j in range(2):
                        for n, (w, x) in enumerate(passes(both, kk_parts)):
                            nc.tensor.matmul(ps[:, 2 * s + j, 0:NB], w[:, cc, j * P:(j + 1) * P],
                                             x[:, s, :, 2 * c:2 * c + CMP_STRIDE * (CMP_BLOCKS - 1) + 1:CMP_STRIDE]
                                             .rearrange("p g b -> p b g"),
                                             start=(c == 0 and n == 0), stop=(c == 15 and n == 2))
                        for n, (w, x) in enumerate(passes(both, pos_parts)):
                            last = nc.tensor.matmul(ps[:, 4 + j, 2 * s:2 * s + 2], w[:, cc, j * P:(j + 1) * P], x[:, s, c, :],
                                                    start=(c == 0 and n == 0), stop=(c == 15 and n == 2), skip_group_check=True)
                last.then_inc(st.used, 1)
            pe.wait_ge(hid_done, 4)
            for j in range(2):
                nc.tensor.matmul(ps[0:64, 6, 0:NB], w2[:, 0, j, :], hid[:, 0, j, :], start=(j == 0), stop=(j == 1))
            pe.wait_ge(cb_done, 2)
            for gr in range(C_GROUPS):
                for j in range(2):
                    last = nc.tensor.matmul(ps[0:CMP_BLOCKS, 7, 64 * gr:64 * gr + 64], hid[:, 1, j, gr:NB:C_GROUPS],
                                            w2[:, 1, j, :], start=(j == 0), stop=(j == 1), skip_group_check=True)
            last.then_inc(kv_done, 1)

        @block.vector
        def _(dve):
            dve.wait_ge(cb_done, 1)
            nc.vector.tensor_copy(cb[:].rearrange("p u h -> p (u h)"), ps[:, 7, 0:CB_SPAN * C_HEADS]).then_inc(cb_done, 1)
            for n, (whole, hi, lo) in enumerate(splits):
                dve.wait_ge(high, n + 1)
                nc.vector.tensor_tensor(lo, whole, hi.bitcast(F32), ALU.subtract).then_inc(low, 1)
            for t in range(4):
                st.next(st.take_low, dve, seg, t)
            dve.wait_ge(st.used, seg["start"] + 4)
            for j in range(2):
                nc.vector.tensor_copy(pe_b[:, :, j], ps[:, 4 + j, 0:4:2]).then_inc(pe_kept, 1)
            dve.wait_ge(kv_done, 1)
            for half in range(2):
                nc.vector.tensor_copy(kc[64 * half:64 * half + 64].rearrange("p g c -> p c g"),
                                      ps[0:64, 6, 0:NB].rearrange("p (c g) -> p c g", g=C_GROUPS))
            nc.vector.tensor_copy(vc[:].rearrange("p g c -> p (g c)"), ps[0:CMP_BLOCKS, 7, 0:P])

        @block.scalar
        def _(act):
            nc.scalar.activation(gate[:].rearrange("p i k -> p (i k)"), gate[:].rearrange("p i k -> p (i k)"), ACT.Sigmoid)
            for whole, hi, _ in splits:
                nc.scalar.copy(hi, whole).then_inc(high, 1)
            for t in range(4):
                st.next(st.take_high, act, seg, t)
            act.wait_ge(pe_kept, 2)
            for s in range(2):
                for j in range(2):
                    nc.scalar.activation(hid[:, s, j, :], ps[:, 2 * s + j, 0:NB], ACT.Gelu_apprx_tanh,
                                         bias=pe_b[:, s, j:j + 1], scale=1.0).then_inc(hid_done, 1)


def lru_decay(g, par, decay):
    nc = g.nc
    with ExitStack() as ctx:
        sb = lambda n: ctx.enter_context(nc.sbuf_tensor(f"decay_{n}", [BW, GATES], F32))
        par_in, step_done, exp_done = (nc.alloc_semaphore(f"decay_{n}") for n in ("params_in", "step", "exp_done"))
        neg, low, u, den, inv, z, z2, series = (sb(n) for n in ("neg", "low", "u", "den", "inv", "z", "z2", "series"))
        block = ctx.enter_context(nc.Block())
        lam = par[:, 7, :]

        @block.sync
        def _(sp):
            sp.dma_start(par[:], g.a["f_lru"]).then_inc(par_in, 16)

        @block.scalar
        def _(act):
            act.wait_ge(step_done, 2)
            nc.scalar.activation(u[:], low[:], ACT.Exp).then_inc(exp_done, 1)

        @block.vector
        def _(dve):
            steps = [0]

            def step(ins):
                steps[0] += 1
                ins.then_inc(step_done, 1)
                dve.wait_ge(step_done, steps[0])

            dve.wait_ge(par_in, 16)
            step(nc.vector.tensor_scalar(neg[:], lam, -1.0, None, ALU.mult))
            step(nc.vector.tensor_tensor(low[:], lam, neg[:], ALU.min))
            dve.wait_ge(exp_done, 1)
            step(nc.vector.tensor_scalar(den[:], u[:], 2.0, None, ALU.add))
            step(nc.vector.reciprocal(inv[:], den[:]))
            step(nc.vector.tensor_tensor(z[:], u[:], inv[:], ALU.mult))
            step(nc.vector.tensor_tensor(z2[:], z[:], z[:], ALU.mult))
            step(nc.vector.tensor_scalar(series[:], z2[:], 1.0 / 19, None, ALU.mult))
            for k in (17, 15, 13, 11, 9, 7, 5, 3):
                step(nc.vector.scalar_tensor_tensor(out=series[:], in0=series[:], scalar=1.0 / k, in1=z2[:], op0=ALU.add, op1=ALU.mult))
            step(nc.vector.scalar_tensor_tensor(out=series[:], in0=series[:], scalar=1.0, in1=z[:], op0=ALU.add, op1=ALU.mult))
            step(nc.vector.tensor_scalar(neg[:], neg[:], 0.0, -C_RG, ALU.max, ALU.mult))
            step(nc.vector.scalar_tensor_tensor(out=decay[:], in0=series[:], scalar=-2.0 * C_RG, in1=neg[:], op0=ALU.mult, op1=ALU.add))


def rglru(g, y, par, decay):
    nc, ps, st, seg, a = g.nc, g.ps, g.st, g.seg_lru, g.a
    with ExitStack() as ctx:
        sb = lambda n, s: ctx.enter_context(nc.sbuf_tensor(n, s, F32))
        sem = lambda n: nc.alloc_semaphore(n)
        K = 4
        pad = sb("lru_pad", [BW, 2, S + 3])
        xb = sb("lru_xb", [BW, 2, S])
        w = sb("lru_work", [BW, 2, 7, S])
        R, I, SG, A, TH, E2, GT = range(7)
        LA, IX = R, I
        zeroed = sem("lru_zeroed")
        gw = sb("lru_gate_weights", [BW, 2, 2, BW])
        gate_in = [sem(f"lru_gate_weights_in_{s}") for s in range(2)]
        pad_kept, xb_ready, ri_done, sig_done, la_done, exp_done, em_done, sq_done, y_done, vstep, ystep = (sem(f"lru_{n}") for n in
            ("x_kept", "conv_ready", "gates_done", "sigmoids_done", "log_decay_ready", "exps_done", "expm1_ready", "root_done", "y_done", "conv_step", "recurrence_step"))
        block = ctx.enter_context(nc.Block())
        last_t = GATES - 1

        @block.sync
        def _(sp):
            st.feed(sp, seg)

        @block.gpsimd
        def _(pool):
            pool.memset(pad[:, :, 0:3], 0.0).then_inc(zeroed, 1)

            def tile(t, turn):
                if turn is not None or t >= 2:
                    pool.wait_ge(ri_done, at(turn, 1, t) - 1)
                for s, name in enumerate(("lru_w_a_2", "lru_w_x_2")):
                    block_w = a[name][0, bass.ds(at(turn, 1, t), 1)].rearrange("t p n -> p (t n)")
                    pool.dma_start(gw[:, t % 2, s, :], block_w).then_inc(gate_in[t % 2], 16)
            loop_tiles(pool, GATES, RING, tile)

        @block.tensor
        def _(pe):
            def inputs(t, turn):
                both = [part[:, 0:CH * 2 * BW].rearrange("p (c s n) -> p c s n", c=CH, s=2) for part in st.wait(pe, seg, t, turn)]
                if turn is not None or t >= 2:
                    pe.wait_ge(sig_done, at(turn, 1, t) - 1)
                for s in range(2):
                    for c in range(CH):
                        for k, (wp, x) in enumerate(passes(both, g.parts)):
                            last = nc.tensor.matmul(ps[0:BW, 2 * (t % 2) + s, :], wp[:, c, s, :], x[:, c, :],
                                                    start=(c == 0 and k == 0), stop=(c == CH - 1 and k == 2))
                last.then_inc(st.used, 1)

            def gates(t, turn):
                pe.wait_ge(gate_in[t % 2], 32 * (t // 2 + 1) if turn is None else turn * (16 * RING) + 32 * (t // 2 + 1))
                pe.wait_ge(xb_ready, at(turn, 1, t) + 1)
                for s in range(2):
                    last = nc.tensor.matmul(ps[0:BW, 4 + 2 * (t % 2) + s, :], gw[:, t % 2, s, :],
                                            xb[:, t % 2, :], start=True, stop=True)
                last.then_inc(ri_done, 1)

            def tile(t, turn):
                inputs(t, turn)
                if turn is not None or t:
                    gates(t - 1, turn)
            loop_tiles(pe, GATES, RING, tile)
            gates(last_t, None)

        @block.scalar
        def _(act):
            act.wait_ge(zeroed, 1)

            def move(t, turn):
                act.wait_ge(st.used, at(turn, 1, t) + (seg["start"] + 1))
                if turn is not None or t >= 2:
                    act.wait_ge(xb_ready, at(turn, 1, t) - 1)
                nc.scalar.copy(pad[:, t % 2, 3:S + 3], ps[0:BW, 2 * (t % 2), :]).then_inc(pad_kept, 1)

            def gate(t, turn):
                r = t % 2
                n = at(turn, 1, t)
                act.wait_ge(ri_done, n + 1)
                if turn is not None or t >= 2:
                    act.wait_ge(y_done, n - 1)
                col = lambda k: par[:, k, bass.ds(n, 1)]
                nc.scalar.activation(w[:, r, R, :], ps[0:BW, 4 + 2 * r, :], ACT.Sigmoid, bias=col(5), scale=1.0)
                nc.scalar.activation(w[:, r, I, :], ps[0:BW, 5 + 2 * r, :], ACT.Sigmoid, bias=col(6), scale=1.0)
                nc.scalar.copy(w[:, r, GT, :], ps[0:BW, 2 * r + 1, :])
                nc.scalar.activation(w[:, r, SG, :], ps[0:BW, 2 * r + 1, :], ACT.Sigmoid).then_inc(sig_done, 1)
                act.wait_ge(la_done, n + 1)
                nc.scalar.activation(w[:, r, A, :], w[:, r, LA, :], ACT.Exp)
                nc.scalar.activation(w[:, r, TH, :], w[:, r, LA, :], ACT.Tanh).then_inc(exp_done, 1)
                act.wait_ge(em_done, n + 1)
                nc.scalar.activation(w[:, r, E2, :], w[:, r, E2, :], ACT.Sqrt, bias=0.0, scale=-1.0).then_inc(sq_done, 1)

            def tile(t, turn):
                st.next(st.take_high, act, seg, t, turn)
                move(t, turn)
                if turn is not None or t:
                    gate(t - 1, turn)
            loop_tiles(act, GATES, RING, tile)
            gate(last_t, None)

        @block.vector
        def _(dve):
            dve.wait_ge(zeroed, 1)

            def conv(t, turn):
                r = t % 2
                n = at(turn, 1, t)
                m = at(turn, 3, t)
                col = lambda k: par[:, k, bass.ds(n, 1)]
                dve.wait_ge(pad_kept, n + 1)
                if turn is not None or t >= 2:
                    dve.wait_ge(em_done, n - 1)
                    dve.wait_ge(ri_done, n - 1)
                nc.vector.tensor_scalar(xb[:, r, :], pad[:, r, 3:S + 3], col(3), col(4), ALU.mult, ALU.add).then_inc(vstep, 1)
                for k in (2, 1):
                    dve.wait_ge(vstep, m + (3 - k))
                    nc.vector.scalar_tensor_tensor(out=xb[:, r, :], in0=pad[:, r, k:S + k], scalar=col(k), in1=xb[:, r, :],
                                                   op0=ALU.mult, op1=ALU.add).then_inc(vstep, 1)
                dve.wait_ge(vstep, m + 3)
                nc.vector.scalar_tensor_tensor(out=xb[:, r, :], in0=pad[:, r, 0:S], scalar=col(0), in1=xb[:, r, :],
                                               op0=ALU.mult, op1=ALU.add).then_inc(xb_ready, 1)

            def recur(t, turn):
                r = t % 2
                n = at(turn, 1, t)
                m = at(turn, 4, t)
                dve.wait_ge(sig_done, n + 1)
                nc.vector.tensor_scalar(w[:, r, LA, :], w[:, r, R, :], decay[:, bass.ds(n, 1)], None, ALU.mult).then_inc(la_done, 1)
                nc.vector.tensor_tensor(w[:, r, IX, :], w[:, r, I, :], xb[:, r, :], ALU.mult).then_inc(ystep, 1)
                dve.wait_ge(exp_done, n + 1)
                nc.vector.tensor_tensor(w[:, r, E2, :], w[:, r, A, :], w[:, r, A, :], ALU.mult).then_inc(ystep, 1)
                dve.wait_ge(ystep, m + 2)
                nc.vector.scalar_tensor_tensor(out=w[:, r, E2, :], in0=w[:, r, E2, :], scalar=1.0, in1=w[:, r, TH, :],
                                               op0=ALU.add, op1=ALU.mult).then_inc(em_done, 1)
                dve.wait_ge(sq_done, n + 1)
                nc.vector.tensor_tensor(w[:, r, IX, :], w[:, r, IX, :], w[:, r, E2, :], ALU.mult).then_inc(ystep, 1)
                nc.vector.tensor_tensor(w[:, r, SG, :], w[:, r, SG, :], w[:, r, GT, :], ALU.mult)
                dve.wait_ge(ystep, m + 3)
                nc.vector.tensor_tensor_scan(w[:, r, TH, :], w[:, r, A, :], w[:, r, IX, :], 0.0, ALU.mult, ALU.add).then_inc(ystep, 1)
                dve.wait_ge(ystep, m + 4)
                dst = y[:, t, :] if turn is None else y[:, bass.ds(n, 1), :].rearrange("p c n -> p (c n)")
                nc.vector.tensor_tensor(dst, w[:, r, TH, :], w[:, r, SG, :], ALU.mult).then_inc(y_done, 1)

            def tile(t, turn):
                st.next(st.take_low, dve, seg, t, turn)
                conv(t, turn)
                if turn is not None or t:
                    recur(t - 1, turn)
            loop_tiles(dve, GATES, RING, tile)
            recur(last_t, None)


def retention(g, y):
    nc, a = g.nc, g.a
    with ExitStack() as ctx:
        sb = lambda n, s: ctx.enter_context(nc.sbuf_tensor(n, s, F32))
        qk, v = sb("r_qk", [P, 4, S]), sb("r_v", [P, NT, R_V])
        q, k = qk[:, 0:2, :], qk[:, 2:4, :]
        gate = sb("r_gate", [P, 4, S])
        cs = sb("r_trig", [P, 2, S])
        dec = sb("r_decay", [P, S])
        tmp = sb("r_tmp", [P, 4, S])
        load_small(g, "ret_consts", [(cs[:], a["c_rotary"].rearrange("k p t -> p k t"))])
        for h in range(R_HEADS):
            plan = [[features(128 * j, P, 256, g.parts, [(q[:, j, :], 0, P, 1.0, 0)]) for j in range(2)],
                    [features(128 * j, P, 256, g.parts, [(k[:, j, :], 0, P, R_QK ** -0.5, 0)]) for j in range(2)]]
            plan += [[tokens(0, 256, 256, g.parts, lambda i, t=t: v[:, i, 256 * t:256 * (t + 1)])] for t in range(2)]
            plan += [[features(128 * j, P, 256, g.parts, [(gate[:, 2 * t + j, :], 0, P, 1.0, 0)]) for j in range(2)] for t in range(2)]
            project(g, f"ret{h}_proj", g.seg_ret[h], plan)
            retain(g, h, qk, v, gate, cs, dec, tmp, y)


def retain(g, h, qk, v, gate, cs, dec, tmp, y):
    nc, ps = g.nc, g.ps
    n_ = f"ret{h}_"
    with ExitStack() as ctx:
        sem = lambda n: nc.alloc_semaphore(n_ + n)
        s_t, o = g.h[:, 0:NT, :], g.h[:, NT:2 * NT, :]
        sq = qk
        rs = tmp
        decay_in = sem("decay_in")
        part, turned, s_done, s_kept, o_done, o_kept, mean_done, centred, squared, sq_done, vs, rstd, silu, normed = (sem(n) for n in
            ("products", "turned", "scores_done", "scores_kept", "values_done", "out_kept", "mean_done", "centred", "squared",
             "squares_summed", "vector_step", "root_ready", "silu_done", "normed"))
        block = ctx.enter_context(nc.Block())
        cos, sin = cs[:, 0, :], cs[:, 1, :]

        @block.sync
        def _(sp):
            sp.dma_start(dec[:], g.a["c_decay"][h]).then_inc(decay_in, 16)

        @block.vector
        def _(dve):
            for n in range(2):
                x1, x2 = qk[:, 2 * n, :], qk[:, 2 * n + 1, :]
                if n:
                    dve.wait_ge(turned, 2)
                for m, (x, f) in enumerate(((x1, cos), (x2, sin), (x2, cos), (x1, sin))):
                    nc.vector.tensor_tensor(tmp[:, m, :], x, f, ALU.mult).then_inc(part, 1)
                dve.wait_ge(part, 4 * (n + 1))
                nc.vector.tensor_tensor(x1, tmp[:, 0, :], tmp[:, 1, :], ALU.subtract).then_inc(turned, 1)
                nc.vector.tensor_tensor(x2, tmp[:, 2, :], tmp[:, 3, :], ALU.add).then_inc(turned, 1)
            dve.wait_ge(decay_in, 16)
            for kb in range(NT):
                w = S - kb * P
                dve.wait_ge(s_done, kb + 1)
                nc.vector.tensor_tensor(s_t[:, kb, 0:w], ps[:, kb, 0:w], dec[:, 0:w], ALU.mult).then_inc(s_kept, 1)
            for c in range(4):
                dve.wait_ge(o_done, c + 1)
                nc.vector.tensor_copy(o[:, c, :], ps[:, 4 + c, :]).then_inc(o_kept, 1)
            dve.wait_ge(mean_done, 1)
            nc.vector.tensor_scalar(rs[:, 0, :], ps[:, 0, :], 1.0 / R_V, None, ALU.mult).then_inc(vs, 1)
            dve.wait_ge(vs, 1)
            for c in range(4):
                nc.vector.tensor_tensor(o[:, c, :], o[:, c, :], rs[:, 0, :], ALU.subtract).then_inc(centred, 1)
            dve.wait_ge(sq_done, 1)
            nc.vector.tensor_scalar(rs[:, 1, :], ps[:, 1, :], 1.0 / R_V, GN_EPS, ALU.mult, ALU.add).then_inc(vs, 1)
            dve.wait_ge(vs, 2)
            nc.vector.reciprocal(rs[:, 2, :], rs[:, 1, :]).then_inc(rstd, 1)
            dve.wait_ge(rstd, 2)
            for c in range(4):
                nc.vector.tensor_tensor(o[:, c, :], o[:, c, :], rs[:, 3, :], ALU.mult).then_inc(normed, 1)
            for c in range(4):
                dve.wait_ge(normed, c + 1)
                dve.wait_ge(silu, c + 1)
                nc.vector.tensor_tensor(y[:, 4 * h + c, :], o[:, c, :], gate[:, c, :], ALU.mult)

        @block.tensor
        def _(pe):
            pe.wait_ge(turned, 4)
            for kb in range(NT):
                for c in range(2):
                    last = nc.tensor.matmul(ps[:, kb, 0:S - kb * P], qk[:, 2 + c, kb * P:(kb + 1) * P], qk[:, c, kb * P:S],
                                            start=(c == 0), stop=(c == 1))
                last.then_inc(s_done, 1)
            for c in range(4):
                for kb in range(NT):
                    pe.wait_ge(s_kept, kb + 1)
                    last = nc.tensor.matmul(ps[:, 4 + c, kb * P:S], v[:, kb, c * P:(c + 1) * P], s_t[:, kb, 0:S - kb * P],
                                            start=(kb == 0), stop=(kb == NT - 1), skip_group_check=True)
                last.then_inc(o_done, 1)
            for c in range(4):
                pe.wait_ge(o_kept, c + 1)
                last = nc.tensor.matmul(ps[:, 0, :], g.mean_w[:], o[:, c, :], start=(c == 0), stop=(c == 3))
            last.then_inc(mean_done, 1)
            for c in range(4):
                pe.wait_ge(squared, c + 1)
                last = nc.tensor.matmul(ps[:, 1, :], g.mean_w[:], sq[:, c, :], start=(c == 0), stop=(c == 3))
            last.then_inc(sq_done, 1)

        @block.scalar
        def _(act):
            for c in range(4):
                nc.scalar.activation(gate[:, c, :], gate[:, c, :], ACT.Silu).then_inc(silu, 1)
            for c in range(4):
                act.wait_ge(centred, c + 1)
                nc.scalar.activation(sq[:, c, :], o[:, c, :], ACT.Square).then_inc(squared, 1)
            act.wait_ge(rstd, 1)
            nc.scalar.activation(rs[:, 3, :], rs[:, 2, :], ACT.Sqrt).then_inc(rstd, 1)


def finish(g, out, src):
    nc, ps = g.nc, g.ps
    with ExitStack() as ctx:
        sem = lambda n: nc.alloc_semaphore(n)
        xt = ctx.enter_context(nc.sbuf_tensor("out_tokens", [P, NT, D], F32))
        turned, kept, out_done = sem("out_turned"), sem("out_kept"), sem("out_stored")
        block = ctx.enter_context(nc.Block())

        @block.tensor
        def _(pe):
            for t in range(NT):
                for half in range(2):
                    for c in range(4):
                        last = nc.tensor.transpose(ps[:, 2 * t + half, c * P:(c + 1) * P],
                                                   src[:, 4 * half + c, t * P:(t + 1) * P], g.ident[:])
                    last.then_inc(turned, 1)

        @block.vector
        def _(dve):
            for t in range(NT):
                for half in range(2):
                    dve.wait_ge(turned, 2 * t + half + 1)
                    nc.vector.tensor_copy(xt[:, t, half * S:(half + 1) * S], ps[:, 2 * t + half, :]).then_inc(kept, 1)

        @block.sync
        def _(sp):
            o = out.rearrange("b (t p) d -> p (b t) d", p=P)
            for t in range(NT):
                sp.wait_ge(kept, 2 * (t + 1))
                sp.dma_start(o[:, t, :], xt[:, t, :]).then_inc(out_done, 16)
            sp.wait_ge(out_done, 16 * NT)


def program(nc, a, out, stop=None):
    with ExitStack() as ctx:
        g = Program(nc, ctx, a)
        g.plan()
        chunks = lambda t: [t[:, c, :] for c in range(CH)]
        todo = []

        def begin():
            g.open_parts("x_tokens_in")
            start(g)

        def even():
            even_mixer(g, g.h)

        def ffn(l):
            with nc.sbuf_tensor(f"ffn{l}_act", [P, FF_CH, S], F32) as act_t:
                with nc.sbuf_tensor(f"ffn{l}_taps", [P, 4, FF_CH], F32) as cw:
                    ffn_up(g, l, act_t, cw)
                g.close_parts()
                down(g, f"ffn{l}_down", g.seg_down[l], act_t, P, "ln", 2 * l + 1, FF_CH)

        def pre(l):
            if l == 0:
                g.close_parts()
            g.open_parts(f"pre{l}_out")
            rms(g, f"pre{l}", [{"src": chunks(g.x), "dst": chunks(g.h), "n": D, "eps": RMS_EPS_2,
                                "gain": [g.norm_pre[:, l, c:c + 1] for c in range(CH)], "parts": [chunks(p) for p in g.parts]}])

        def lru():
            pre(0)
            with nc.sbuf_tensor("lru_y", [BW, GATES, S], F32) as y:
                with nc.sbuf_tensor("lru_params", [BW, 8, GATES], F32) as par, nc.sbuf_tensor("lru_decay", [BW, GATES], F32) as decay:
                    lru_decay(g, par, decay)
                    rglru(g, y, par, decay)
                g.close_parts()
                down(g, "lru_down", g.seg_lru_out, y, BW, "rms", 0, GATES)

        def ret():
            pre(1)
            with nc.sbuf_tensor("ret_y", [P, 16, S], F32) as y:
                retention(g, y)
                g.close_parts()
                down(g, "ret_down", g.seg_ret_out, y, P, "rms", 1, 16)

        stages = [("start", begin), ("even", even),
                  ("ln0", lambda: down(g, "ev_down", g.seg_ev_out, g.h, P, "ln", 0, 6)),
                  ("ffn0", lambda: ffn(0)), ("odd", lambda: odd_mixer(g, g.h)),
                  ("ln2", lambda: down(g, "od_down", g.seg_od_out, g.h, P, "ln", 2, 8)),
                  ("ffn1", lambda: ffn(1)), ("lru", lru), ("ret", ret)]
        held = nc.snapshot_sems()
        for name, stage in stages:
            stage()
            nc.clear_and_free_semaphores(nc.allocated_since(held))
            nc.all_engine_barrier()
            if name == stop:
                break
        finish(g, out, g.h if stop in ("even", "odd") else g.x)


def shape_tables():
    import numpy as np
    f32 = np.float32

    def bucket(dist):
        n = np.maximum(dist, 0)
        nf = np.maximum(n, 1).astype(f32)
        large = 16 + (np.log(nf / f32(16)) / f32(math.log(2048 / 16)) * f32(16)).astype(np.int32)
        return np.where(n < 16, n, np.minimum(large, 31))

    def onehot(dist, valid):
        t = np.zeros((33, dist.size), f32)
        t[bucket(dist), np.arange(dist.size)] = 1.0
        t[:, ~valid] = 0.0
        t[32] = ~valid
        return t

    dist = np.arange(TOE) - (P - 1)
    kinds = [dist >= 0, (dist >= 0) & (dist <= 128), (dist >= 0) & (dist % 4 == 0), (dist >= 0) & (dist % 16 == 0)]
    fwd = np.arange(FWD_LEN) - FWD_OFF
    out = {"c_ident": np.eye(P, dtype=f32),
           "c_onehot": np.stack([onehot(dist, v) for v in kinds]),
           "c_onehot_fwd": onehot(fwd, fwd >= 0),
           "c_neg": np.full((1, 16), NEG, f32)}
    half = D_ROPE // 2
    swap = np.zeros((D_ROPE, D_ROPE), f32)
    for i in range(half):
        swap[half + i, i] = -1.0
        swap[i, half + i] = 1.0
    pos = np.arange(S, dtype=f32)
    ang = pos[None, :] * (f32(10000.0) ** (-np.arange(half, dtype=f32) / f32(half)))[:, None]
    c, s = np.tile(np.cos(ang), (2, 1)), np.tile(np.sin(ang), (2, 1))
    sc = f32((D_NOPE + D_ROPE) ** -0.5)
    out["c_rope_swap"] = swap
    out["c_rope_trig"] = np.stack([c, s, c * sc, s * sc]).astype(f32)
    ang = pos[None, :] * (f32(10000.0) ** (-np.arange(0, R_QK, 2, dtype=f32) / f32(R_QK)))[:, None]
    out["c_rotary"] = np.stack([np.cos(ang), np.sin(ang)]).astype(f32)
    log_g = np.log(1.0 - np.exp2(-5.0 - np.arange(R_HEADS, dtype=np.float64)))
    diff = np.arange(S)[None, :] - np.arange(P)[:, None]
    out["c_decay"] = np.where(diff[None] >= 0, np.exp(np.maximum(diff, 0)[None] * log_g[:, None, None]), 0.0).astype(f32)
    return out


def arranged(inputs):
    import numpy as np
    v = {n: np.asarray(x) for n, x in inputs.items()}
    small = ("ln_g", "ln_b", "norm_pre_2", "norm_post_2", "ffn_conv_w", "ffn_conv_b", "ev_subln", "od_cmp_pe", "od_q_norm",
             "od_kv_norm", "lru_conv_w_2", "lru_conv_b_2", "lru_b_a_2", "lru_b_x_2", "lru_lambda_2")
    out = {n: x for n, x in v.items() if n not in small}

    def columns(x, p=P):
        x = x.reshape(x.shape[:-1] + (x.shape[-1] // p, p))
        return np.moveaxis(x, -1, 0)

    out["f_ln_g"] = columns(v["ln_g"].reshape(2 * DEPTH, D))
    out["f_ln_b"] = columns(v["ln_b"].reshape(2 * DEPTH, D))
    out["f_norm_pre"], out["f_norm_post"] = columns(v["norm_pre_2"]), columns(v["norm_post_2"])
    taps = np.concatenate([v["ffn_conv_w"], v["ffn_conv_b"][:, None]], axis=1)
    out["f_ffn_conv"] = np.stack([columns(t) for t in taps])
    out["f_subln"] = v["ev_subln"].reshape(P, 1)
    out["f_cmp_pe"] = columns(v["od_cmp_pe"][0].reshape(2, CMP_LEN * C_DIM))
    out["f_q_norm"], out["f_kv_norm"] = columns(v["od_q_norm"][0]), columns(v["od_kv_norm"][0])
    out["f_lru"] = columns(np.concatenate([v["lru_conv_w_2"][0]] + [v[n] for n in
                           ("lru_conv_b_2", "lru_b_a_2", "lru_b_x_2", "lru_lambda_2")]), BW)
    return out


def kernel(**inputs):
    import numpy as _np
    import concourse.bacc as _bacc
    from concourse import mybir as _mybir
    from concourse.bass_utils import run_bass_kernel_spmd as _run

    nc = _bacc.Bacc("TRN2", target_bir_lowering=False, num_devices=1)
    arrays, args = {}, {}
    for name, value in {**arranged(inputs), **shape_tables()}.items():
        a = _np.ascontiguousarray(value)
        arrays[f"in_{name}_dram"] = a
        args[name] = nc.dram_tensor(f"in_{name}_dram", a.shape, _mybir.dt.from_np(a.dtype), kind="ExternalInput").ap()
    out = nc.dram_tensor("out_0_dram", (1, S, D), F32, kind="ExternalOutput").ap()
    program(nc, args, out)
    r = _run(nc, [arrays], core_ids=[0])
    return r.results[0]["out_0_dram"]
```

```python
import math
from contextlib import ExitStack

import concourse.bass as bass
from concourse import mybir

F32 = mybir.dt.float32
F32R = mybir.dt.float32r
ALU = mybir.AluOpType
ACT = mybir.ActivationFunctionType
AX_X = mybir.AxisListType.X

P = 128
D = 1024
S = 512
NT = S // P
CH = D // P
RING = 4
SLOT = 2048
NEG = -1.0e30
LN_EPS = 1e-5
RMS_EPS = 1e-5
RMS_EPS_2 = 1e-6
GN_EPS = 1e-5
DEPTH = 2
ALPHA = (2 * DEPTH) ** 0.25
LAM_INIT = 0.8 - 0.6 * math.exp(-0.3 * 0)

A_HEADS, A_QK, A_V = 4, 64, 128
B_HEADS, B_DIM, N_PAIRS = 4, 64, 3
C_HEADS, C_DIM, C_GROUPS = 8, 64, 2
CMP_BLOCKS, CMP_LEN, CMP_STRIDE, CMP_HIDDEN = 31, 32, 16, 256
D_HEADS, D_NOPE, D_ROPE, D_V = 8, 64, 32, 64
D_Q_LORA, D_KV_LORA = 384, 256
D_FF = 2816
FF_CH = D_FF // P
GATES, BW = 16, 96
C_RG = 8.0
R_HEADS, R_QK, R_V = 4, 256, 512

TOE = 640
STD, WIN, DIL4, DIL16 = range(4)
KINDS = 4
TCOLS = 17


class Stream:

    def __init__(self, nc, ctx):
        self.nc = nc
        self.ring = ctx.enter_context(nc.sbuf_tensor("weight_ring", [P, RING, SLOT], F32))
        self.high = ctx.enter_context(nc.sbuf_tensor("weight_high", [P, 2, SLOT], F32R))
        self.low = ctx.enter_context(nc.sbuf_tensor("weight_low", [P, 2, SLOT], F32R))
        self.loaded = [ctx.enter_context(nc.semaphore(f"weights_loaded_{s}")) for s in range(RING)]
        self.high_ready = ctx.enter_context(nc.semaphore("weights_high_ready"))
        self.ready = ctx.enter_context(nc.semaphore("weights_ready"))
        self.used = ctx.enter_context(nc.semaphore("weights_used"))
        self.tiles = 0
        self.count = [0] * RING
        self.segments = []

    def segment(self, count, pieces, load, size=SLOT, kp=P):
        seg = {"start": self.tiles, "count": count, "pieces": pieces, "load": load, "base": list(self.count),
               "size": size, "kp": kp}
        for t in range(count):
            self.count[(self.tiles + t) % RING] += 16 * pieces
        self.tiles += count
        self.segments.append(seg)
        return seg

    def issue(self, sp, seg, t, turn=None):
        n = seg["start"] + t
        slot = n % RING
        t_now = t if turn is None else turn * RING + t
        if n >= RING:
            sp.wait_ge(self.ready, seg["start"] - RING + 1 + t_now)
        for dst, src in seg["load"](t_now, self.ring[:, slot, :]):
            sp.dma_start(dst, src).then_inc(self.loaded[slot], 16)

    def rest(self, sp, seg):
        turns = (seg["count"] - RING) // RING
        if turns > 1:
            with sp.Fori(0, turns) as turn:
                for t in range(RING, 2 * RING):
                    self.issue(sp, seg, t, turn)
        else:
            turns = 0
        for t in range(RING * (turns + 1), seg["count"]):
            self.issue(sp, seg, t)

    def first(self, sp, seg):
        for t in range(min(RING, seg["count"])):
            self.issue(sp, seg, t)

    def feed(self, sp, seg):
        self.rest(sp, seg)
        k = self.segments.index(seg)
        if k + 1 < len(self.segments):
            self.first(sp, self.segments[k + 1])

    def _part(self, store, seg, t):
        size = seg["size"] if isinstance(seg["size"], int) else seg["size"][t]
        return store[0:seg["kp"], (seg["start"] + t) % (RING if store is self.ring else 2), 0:size]

    def take_high(self, act, seg, t, turn=None):
        slot = (seg["start"] + t) % RING
        level = seg["base"][slot] + 16 * seg["pieces"] * (t // RING + 1)
        act.wait_ge(self.loaded[slot], level if turn is None else turn * (16 * seg["pieces"]) + level)
        if seg["start"] + t >= 2:
            act.wait_ge(self.used, at(turn, 1, t) + (seg["start"] - 1))
        self.nc.scalar.copy(self._part(self.high, seg, t), self._part(self.ring, seg, t)).then_inc(self.high_ready, 1)

    def take_low(self, dve, seg, t, turn=None):
        dve.wait_ge(self.high_ready, at(turn, 1, t) + (seg["start"] + 1))
        self.nc.vector.tensor_tensor(self._part(self.low, seg, t), self._part(self.ring, seg, t),
                                     self._part(self.high, seg, t).bitcast(F32), ALU.subtract).then_inc(self.ready, 1)

    def next(self, take, eng, seg, t, turn=None):
        if turn is not None or t + 1 < seg["count"]:
            take(eng, seg, t + 1, turn)
        else:
            k = self.segments.index(seg)
            if k + 1 < len(self.segments):
                take(eng, self.segments[k + 1], 0)

    def wait(self, pe, seg, t, turn=None):
        pe.wait_ge(self.ready, at(turn, 1, t) + (seg["start"] + 1))
        slot = (seg["start"] + t) % 2
        return self.high[:, slot, :], self.low[:, slot, :]


def passes(w, x):
    return [(w[0], x[0]), (w[0], x[1]), (w[1], x[0])]


def loop_tiles(eng, count, first, body):
    for t in range(first):
        body(t, None)
    turns = (count - first - 1) // RING
    if turns > 1:
        with eng.Fori(0, turns) as turn:
            for t in range(first, first + RING):
                body(t, turn)
    else:
        turns = 0
    for t in range(first + turns * RING, count):
        body(t, None)


def at(turn, step, t):
    return step * t if turn is None else turn * (step * RING) + step * t


class Program:
    def __init__(self, nc, ctx, a):
        self.nc, self.a = nc, a
        sb = lambda name, shape: ctx.enter_context(nc.sbuf_tensor(name, shape, F32))
        self.x = sb("residual", [P, CH, S])
        self.h = sb("mixer_in", [P, CH, S])
        self.rstd = sb("norm_root", [P, S])
        self.parts = self.parts_scope = None
        self.ident = sb("ident", [P, P])
        self.mean_w = sb("mean_weights", [P, P])
        self.ln_g = sb("ln_gain", [P, 2 * DEPTH, CH])
        self.ln_b = sb("ln_shift", [P, 2 * DEPTH, CH])
        self.norm_pre = sb("norm_pre", [P, DEPTH, CH])
        self.norm_post = sb("norm_post", [P, DEPTH, CH])
        self.lru_par = ctx.enter_context(nc.sbuf_tensor("lru_params", [BW, 8, GATES], F32))
        self.lru_decay = ctx.enter_context(nc.sbuf_tensor("lru_decay", [BW, GATES], F32))
        self.ps = ctx.enter_context(nc.psum_tensor("banks", [P, 8, S], F32))
        self.st = Stream(nc, ctx)
        self.rev = nc.dram_tensor("distance_rows", [KINDS, TCOLS, TOE], F32, kind="Internal")

    def open_parts(self, name):
        self.parts_scope = ExitStack()
        self.parts = tuple(self.parts_scope.enter_context(self.nc.sbuf_tensor(f"{name}_{part}", [P, CH, S], F32R, side="right"))
                           for part in ("high", "low"))

    def close_parts(self):
        self.parts_scope.close()

    def plan(self):
        st, a = self.st, self.a

        def cols(w, col_of, width):
            w_v = w.rearrange("(c p) n -> p c n", p=P)
            chunks = w_v.shape[1]
            def load(t, slot):
                view = slot[:, 0:chunks * width].rearrange("p (c n) -> p c n", c=chunks)
                return [(view, w_v[:, :, bass.ds(col_of(t), width)])]
            return load

        def rows(w, kp):
            w_v = w.rearrange("(t c p) n -> p t c n", p=kp, c=2)
            def load(t, slot):
                view = slot[0:kp, :].rearrange("p (c n) -> p c n", c=2)
                return [(view, w_v[:, bass.ds(t, 1), :, :].rearrange("p t c n -> p (t c) n"))]
            return load

        def ffn_up(l):
            w_v = a["ffn_w_up"][l].rearrange("(c p) (s n) -> p c s n", p=P, s=2)
            def load(t, slot):
                view = slot.rearrange("p (c s n) -> p c s n", c=CH, s=2)
                return [(view[:, :, s, :], w_v[:, :, s, bass.ds(t * P, P)]) for s in range(2)]
            return load

        ev = a["ev_w_in"][0]
        self.seg_a = st.segment(6, 1, cols(ev, lambda t: t * 256, 256))
        self.seg_b = st.segment(9, 1, cols(ev, lambda t: (t + 6) * 256, 256))
        self.seg_ev_out = st.segment(3, 1, rows(a["ev_w_out"][0], P))
        self.seg_up, self.seg_down = [None, None], [None, None]
        self.seg_up[0] = st.segment(FF_CH, 2, ffn_up(0))
        self.seg_down[0] = st.segment(FF_CH // 2, 1, rows(a["ffn_w_down"][0], P))
        od = a["od_w_in"][0].rearrange("(c p) n -> p c n", p=P)
        C0 = 2 * 512 + 3 * 2 * 2 * 64 - 512
        gate0, cq0 = C0, C0 + 24
        ckv0 = cq0 + D_Q_LORA
        kr0 = ckv0 + D_KV_LORA
        self.od_tiles = [(0, 256), (256, 256), (512, 256), (768, 256), (1024, 256), (gate0, 24), (kr0 - 96, P),
                         (cq0, 256), (cq0 + 256, 256), (cq0 + 512, 128)]
        def load_od(t, slot):
            c, w = self.od_tiles[t]
            return [(slot[:, 0:CH * w].rearrange("p (c n) -> p c n", c=CH), od[:, :, c:c + w])]
        self.seg_od = st.segment(len(self.od_tiles), 1, load_od, [CH * w for _, w in self.od_tiles])
        w1 = a["od_cmp_w1"][0].rearrange("s (t c p) n -> s t p c n", p=P, t=4)
        def load_w1(t, slot):
            view = slot.rearrange("p (c s n) -> p c s n", c=4, s=2)
            return [(view[:, :, s, :], w1[s, t]) for s in range(2)]
        self.seg_cmp = st.segment(4, 2, load_w1)
        uq = a["od_w_uq"][0].rearrange("(c p) n -> p c n", p=P)
        def load_mla(t, slot):
            if t < 2:
                return [(slot[:, 0:3 * 384].rearrange("p (c n) -> p c n", c=3), uq[:, :, 384 * t:384 * (t + 1)])]
            w = a["od_w_uk" if t == 2 else "od_w_uv"][0]
            return [(slot[:, 0:1024].rearrange("p (c n) -> p c n", c=2), w.rearrange("(c p) n -> p c n", p=P))]
        self.seg_mla = st.segment(4, 1, load_mla, [3 * 384, 3 * 384, 1024, 1024])
        self.seg_od_out = st.segment(4, 1, rows(a["od_w_out"][0], P))
        self.seg_up[1] = st.segment(FF_CH, 2, ffn_up(1))
        self.seg_down[1] = st.segment(FF_CH // 2, 1, rows(a["ffn_w_down"][1], P))
        lru = a["lru_w_in_2"][0].rearrange("(c p) (s n) -> p c s n", p=P, s=2)
        def load_lru(t, slot):
            view = slot[:, 0:CH * 2 * BW].rearrange("p (c s n) -> p c s n", c=CH, s=2)
            return [(view[:, :, s, :], lru[:, :, s, bass.ds(t * BW, BW)]) for s in range(2)]
        self.seg_lru = st.segment(GATES, 2, load_lru, CH * 2 * BW)
        self.seg_lru_out = st.segment(GATES // 2, 1, rows(a["lru_w_out_2"][0], BW), SLOT, BW)
        ret = a["ret_w_in_2"][0]
        def ret_col(t):
            h, k = divmod(t, 6)
            return [256 * h, 1024 + 256 * h, 2048 + 512 * h, 2048 + 512 * h + 256,
                    4096 + 512 * h, 4096 + 512 * h + 256][k]
        self.seg_ret = [st.segment(6, 1, cols(ret, lambda t, h=h: ret_col(6 * h + t), 256)) for h in range(R_HEADS)]
        self.seg_ret_out = st.segment(R_HEADS * 2, 1, rows(a["ret_w_out_2"][0], P))


def start(g):
    nc, a, ps = g.nc, g.a, g.ps
    with ExitStack() as ctx:
        sb = lambda n, s: ctx.enter_context(nc.sbuf_tensor(n, s, F32))
        sem = lambda n: nc.alloc_semaphore(n)
        xt = sb("x_tokens", [P, NT, D])
        onehot = sb("onehot", [33, KINDS, TOE])
        tbl = sb("bias_table", [33, TCOLS])
        rows = sb("distance_rows_sb", [TCOLS, KINDS, TOE])
        x_in, small_in, const_in, high = sem("x_in"), sem("small_in"), sem("const_in"), sem("x_high")
        turned, kept, rows_done, rows_kept, rows_out, cleared = (
            sem("x_turned"), sem("x_kept"), sem("rows_done"), sem("rows_kept"), sem("rows_out"), sem("table_cleared"))
        block = ctx.enter_context(nc.Block())

        @block.sync
        def _(sp):
            sp.dma_start(xt[:], a["x"].rearrange("b (t p) d -> p (b t) d", p=P)).then_inc(x_in, 16)
            sp.dma_start(g.ident[:], a["c_ident"]).then_inc(x_in, 16)
            sp.dma_start(onehot[:], a["c_onehot"].rearrange("k b m -> b k m")).then_inc(const_in, 16)
            sp.wait_ge(cleared, 2)
            sp.dma_start(tbl[0:32, 0:16], a["rel_bias"]).then_inc(const_in, 16)
            g.st.first(sp, g.seg_a)
            for dst, src in ((g.ln_g, "f_ln_g"), (g.ln_b, "f_ln_b"), (g.norm_pre, "f_norm_pre"), (g.norm_post, "f_norm_post")):
                sp.dma_start(dst[:], a[src]).then_inc(small_in, 16)
            sp.wait_ge(rows_kept, 2 * KINDS)
            sp.dma_start(g.rev.rearrange("k h m -> h k m"), rows[:]).then_inc(rows_out, 16)
            sp.wait_ge(rows_out, 16)
            sp.wait_ge(small_in, 16 * 4)

        @block.gpsimd
        def _(pool):
            pool.memset(g.mean_w[:], 1.0)
            pool.memset(tbl[:], 0.0).then_inc(cleared, 1)
            pool.wait_ge(cleared, 1)
            pool.memset(tbl[32:33, :], NEG).then_inc(cleared, 1)

        @block.tensor
        def _(pe):
            pe.wait_ge(x_in, 32)
            for c in range(CH):
                for t in range(NT):
                    last = nc.tensor.transpose(ps[:, c % 4, t * P:(t + 1) * P], xt[:, t, c * P:(c + 1) * P], g.ident[:])
                last.then_inc(turned, 1)
                if c >= 3 and c < CH - 1:
                    pe.wait_ge(kept, c - 2)
            pe.wait_ge(const_in, 32)
            pe.wait_ge(cleared, 2)
            for k in range(KINDS):
                for half in range(2):
                    lo = half * (TOE // 2)
                    nc.tensor.matmul(ps[0:TCOLS, 4 + (2 * k + half) % 4, 0:TOE // 2], tbl[:], onehot[:, k, lo:lo + TOE // 2],
                                     start=True, stop=True).then_inc(rows_done, 1)
                    if 2 * k + half >= 3 and 2 * k + half < 2 * KINDS - 1:
                        pe.wait_ge(rows_kept, 2 * k + half - 2)

        @block.vector
        def _(dve):
            for c in range(CH):
                dve.wait_ge(turned, c + 1)
                nc.vector.tensor_copy(g.x[:, c, :], ps[:, c % 4, :]).then_inc(kept, 1)
            for c in range(CH):
                dve.wait_ge(high, c + 1)
                nc.vector.tensor_tensor(g.parts[1][:, c, :], g.x[:, c, :], g.parts[0][:, c, :].bitcast(F32), ALU.subtract)
            g.st.take_low(dve, g.seg_a, 0)

        @block.scalar
        def _(act):
            for c in range(CH):
                act.wait_ge(kept, c + 1)
                nc.scalar.copy(g.parts[0][:, c, :], g.x[:, c, :]).then_inc(high, 1)
            for u in range(2 * KINDS):
                act.wait_ge(rows_done, u + 1)
                lo = (u % 2) * (TOE // 2)
                nc.scalar.copy(rows[:, u // 2, lo:lo + TOE // 2], ps[0:TCOLS, 4 + u % 4, 0:TOE // 2]).then_inc(rows_kept, 1)
            g.st.take_high(act, g.seg_a, 0)


def project(g, name, seg, plan, vector_extra=(), scalar_extra=(), normed=None, small=()):
    nc, ps, st = g.nc, g.ps, g.st
    units = []
    for t, tile in enumerate(plan):
        for item in tile:
            if item["kind"] == "F":
                units.append((t, item, None))
            else:
                units += [(t, item, q) for q in range(NT)]
    with ExitStack() as ctx:
        sem = lambda n: nc.alloc_semaphore(n)
        done = sem(f"{name}_tile_done")
        small_in = sem(f"{name}_small_in")
        kept = [sem(f"{name}_kept_by_scalar"), sem(f"{name}_kept_by_vector")]
        block = ctx.enter_context(nc.Block())

        @block.sync
        def _(sp):
            for dst, src, landed in small:
                sp.dma_start(dst, src).then_inc(landed or small_in, 16)
            st.feed(sp, seg)
            sems = [landed or small_in for _, _, landed in small]
            for landed in dict.fromkeys(sems):
                sp.wait_ge(landed, 16 * sems.count(landed))

        last_of = [u + 1 == len(units) or units[u + 1][0] != units[u][0] for u in range(len(units))]

        def wait_product(eng, u):
            if last_of[u]:
                eng.wait_ge(st.used, seg["start"] + units[u][0] + 1)
            else:
                eng.wait_ge(done, last_of[:u + 1].count(False))

        @block.tensor
        def _(pe):
            def product(u, slot, c):
                t, item, q = units[u]
                width, col, n = item["tile"], item["col"], item["n"]
                chunks = item["x"][0].shape[1]
                both = [part[:, 0:chunks * width].rearrange("p (c n) -> p c n", c=chunks) for part in slot]
                for k, (w, x) in enumerate(passes(both, item["x"])):
                    first, final = c == 0 and k == 0, c == chunks - 1 and k == 2
                    if q is None:
                        last = nc.tensor.matmul(ps[0:n, u % 8, :], w[:, c, col:col + n], x[:, c, :], start=first, stop=final)
                    else:
                        last = nc.tensor.matmul(ps[:, u % 8, 0:n], x[:, c, q * P:(q + 1) * P], w[:, c, col:col + n],
                                                start=first, stop=final)
                if c == chunks - 1:
                    last.then_inc(st.used if last_of[u] else done, 1)

            u = 0
            if normed:
                slot = st.wait(pe, seg, 0)
                u = last_of.index(True) + 1
                for c in range(units[0][1]["x"][0].shape[1]):
                    pe.wait_ge(normed[2], c + 1)
                    for v in range(u):
                        product(v, slot, c)
                pe.wait_ge(normed[2], normed[3])
            now = 0 if normed else -1
            for u in range(u, len(units)):
                t, item, q = units[u]
                if t != now:
                    slot = st.wait(pe, seg, t)
                    now = t
                if u >= 8:
                    pe.wait_ge(kept[u % 2], (u - 8) // 2 + 1)
                for c in range(item["x"][0].shape[1]):
                    product(u, slot, c)

        def keep(eng, parity):
            now = -1
            for u, (t, item, q) in enumerate(units):
                if t != now:
                    now = t
                    st.next((st.take_high, st.take_low)[parity], eng, seg, t)
                    for at_tile, extra in (scalar_extra, vector_extra)[parity]:
                        if at_tile == t:
                            extra(eng, kept)
                if u % 2 != parity:
                    continue
                wait_product(eng, u)
                if q is None:
                    outs = [(dst, ps[lo:hi, u % 8, c0:c0 + dst.shape[-1]], scale) for dst, lo, hi, scale, c0 in item["out"]]
                else:
                    outs = [(item["out"](q), ps[:, u % 8, 0:item["n"]], 1.0)]
                for dst, bank, scale in outs:
                    if parity == 0:
                        last = nc.scalar.mul(dst, bank, scale)
                    else:
                        last = nc.vector.tensor_scalar(dst, bank, scale, None, ALU.mult)
                last.then_inc(kept[parity], 1)

        @block.scalar
        def _(act):
            if normed:
                normed[1](act)
            keep(act, 0)

        @block.vector
        def _(dve):
            if normed:
                normed[0](dve)
            keep(dve, 1)


def features(col, n, tile, x, out):
    return {"kind": "F", "col": col, "n": n, "tile": tile, "x": x, "out": out}


def tokens(col, n, tile, x, out):
    return {"kind": "T", "col": col, "n": n, "tile": tile, "x": x, "out": out}


def first_tables(tables):
    return [(dst, src, None) for h in range(2) for dst, src in tables(h, h)]


def attention(g, name, heads, shared, tables, out_of, gate_of=None):
    nc, ps = g.nc, g.ps
    NH = len(heads)
    AHEAD = 4 if shared or max(len(us) for us in heads) == 1 else 3
    SLOTS = AHEAD + 1
    width = lambda u, i: len(u["blocks"](i)) * u["klen"]
    cap = max(sum(width(u, i) for i in range(NT)) for us in heads for u in us)

    def packs(u):
        where, bank, col = {}, 0, 0
        for kb in sorted({kb for i in range(NT) for kb in u["blocks"](i)}):
            ts = [i for i in range(NT) if kb in u["blocks"](i)]
            if col + len(ts) * P > S:
                bank, col = bank + 1, 0
            where[kb] = (bank, col, ts[0], len(ts))
            col += len(ts) * P
        return where, bank + 1

    flat = [(h, k, u) for h in range(NH) for k, u in enumerate(heads[h])]
    N = len(flat)
    first_of = [0]
    for us in heads:
        first_of.append(first_of[-1] + len(us))
    banks_before = [0]
    for h, k, u in flat:
        banks_before.append(banks_before[-1] + packs(u)[1])
    place = lambda u, i: (sum(width(u, ii) for ii in range(i)), width(u, i))

    with ExitStack() as ctx:
        sb = lambda n, s: ctx.enter_context(nc.sbuf_tensor(n, s, F32))
        sem = lambda n: nc.alloc_semaphore(n)
        sc = sb(f"{name}_scores", [P, SLOTS, cap])
        pt = sb(f"{name}_weights_t", [P, 2, 3 * S])
        top, neg, den, inv, coef = (sb(f"{name}_{n}", [P, N, NT]) for n in ("max", "neg_max", "sum", "inverse", "coefficient"))
        head_top, apart, factor, total = (sb(f"{name}_{n}", s) for n, s in
            (("head_max", [P, NT]), ("apart", [P, N, NT]), ("factor", [P, N, NT]), ("total", [P, 2, NT])))
        s_ready, s_kept, negmax, exped, normed = (sem(f"{name}_{n}") for n in
            ("scores_ready", "scores_kept", "negmax_ready", "exp_done", "weights_ready"))
        t_ready, t_kept, pv_done, o_kept, dve_step, apart_done, factor_done = (sem(f"{name}_{n}") for n in
            ("turned", "turned_kept", "values_done", "out_kept", "vector_step", "apart_ready", "factor_ready"))
        table_in = [sem(f"{name}_table_in_{s}") for s in range(2)]
        block = ctx.enter_context(nc.Block())

        @block.sync
        def _(sp):
            for h in range(2, NH):
                sp.wait_ge(s_kept, NT * first_of[h - 1])
                for dst, src in tables(h, h % 2):
                    sp.dma_start(dst, src).then_inc(table_in[h % 2], 16)

        @block.tensor
        def _(pe):
            def scores(n):
                h, k, u = flat[n]
                for i in range(NT):
                    if n:
                        pe.wait_ge(s_kept, NT * (n - 1) + i + 1)
                    kb = u["blocks"](i)
                    nc.tensor.matmul(ps[:, i, 0:width(u, i)], u["q"][:, i * P:(i + 1) * P],
                                     u["k"](kb[0], width(u, i)), start=True, stop=True).then_inc(s_ready, 1)

            def turn(n):
                h, k, u = flat[n]
                where, nb = packs(u)
                if n:
                    pe.wait_ge(t_kept, banks_before[n])
                for b in range(nb):
                    for kb in sorted(where):
                        bank, col, i0, cnt = where[kb]
                        if bank != b:
                            continue
                        for i in range(i0, i0 + cnt):
                            pe.wait_ge(normed, NT * n + i + 1)
                            off, w = place(u, i)
                            j = u["blocks"](i).index(kb) * u["klen"]
                            last = nc.tensor.transpose(ps[0:u["klen"], 4 + bank, col + (i - i0) * P:col + (i - i0 + 1) * P],
                                                       sc[:, n % SLOTS, off + j:off + j + u["klen"]], g.ident[:])
                    last.then_inc(t_ready, 1)

            def values(n):
                h, k, u = flat[n]
                _, dv0, dv = out_of(h)
                o = ps[dv0:dv0 + dv, 7, :]
                where, nb = packs(u)
                for kb in sorted(where):
                    bank, col, i0, cnt = where[kb]
                    pe.wait_ge(t_kept, banks_before[n] + bank + 1)
                    if k == 0 and kb == 0 and h:
                        pe.wait_ge(o_kept, h)
                    last = nc.tensor.matmul(o[:, i0 * P:(i0 + cnt) * P], u["v"](kb),
                                            pt[0:u["klen"], n % 2, bank * S + col:bank * S + col + cnt * P],
                                            start=(k == 0 and kb == 0), stop=(k == len(heads[h]) - 1 and kb == max(where)),
                                            skip_group_check=True)
                last.then_inc(pv_done, 1)

            for n in range(min(AHEAD, N)):
                scores(n)
            for n in range(N):
                turn(n)
                if n + AHEAD < N:
                    scores(n + AHEAD)
                values(n)

        @block.vector
        def _(dve):
            steps = [0]

            def step(ins):
                steps[0] += 1
                ins.then_inc(dve_step, 1)
                dve.wait_ge(dve_step, steps[0])

            def masked(n):
                h, k, u = flat[n]
                if k == 0 and h >= 2:
                    dve.wait_ge(table_in[h % 2], 16 * sum(len(tables(hh, hh % 2)) for hh in range(2 + h % 2, h + 1, 2)))
                if n >= SLOTS:
                    dve.wait_ge(t_ready, banks_before[n - SLOTS + 1])
                for i in range(NT):
                    off, w = place(u, i)
                    dve.wait_ge(s_ready, NT * n + i + 1)
                    nc.vector.tensor_tensor_reduce(sc[:, n % SLOTS, off:off + w], ps[:, i, 0:w], u["bias"](i), 1.0, 3 * NEG,
                                                   ALU.add, ALU.max, top[:, n, i:i + 1]).then_inc(s_kept, 1)
                dve.wait_ge(s_kept, NT * (n + 1))
                nc.vector.tensor_scalar(neg[:, n, :], top[:, n, :], NEG * 1e-8 if u.get("guard") else 3 * NEG, -1.0,
                                        ALU.max, ALU.mult).then_inc(negmax, 1)
                if shared and n + 1 == first_of[h + 1]:
                    a, b = first_of[h], first_of[h + 1]
                    step(nc.vector.tensor_reduce(head_top[:], top[:, a:b, :].rearrange("p u i -> p i u"), AX_X, ALU.max))
                    for m in range(a, b):
                        nc.vector.tensor_tensor(apart[:, m, :], top[:, m, :], head_top[:], ALU.subtract).then_inc(apart_done, 1)

            def coefficients(n):
                h, k, u = flat[n]
                if shared:
                    if k:
                        return
                    a, b = n, first_of[h + 1]
                    dve.wait_ge(exped, NT * b)
                    dve.wait_ge(factor_done, h + 1)
                    step(nc.vector.tensor_tensor(inv[:, a:b, :], factor[:, a:b, :], den[:, a:b, :], ALU.mult))
                    step(nc.vector.tensor_reduce(total[:, 0, :], inv[:, a:b, :].rearrange("p u i -> p i u"), AX_X, ALU.add))
                    step(nc.vector.reciprocal(total[:, 1, :], total[:, 0, :]))
                    for m in range(a, b):
                        ins = nc.vector.tensor_tensor(coef[:, m, :], factor[:, m, :], total[:, 1, :], ALU.mult)
                    step(ins)
                    return
                dve.wait_ge(exped, NT * (n + 1))
                if u.get("guard"):
                    step(nc.vector.tensor_scalar(den[:, n, :], den[:, n, :], 1e-30, None, ALU.max))
                gate = gate_of(h, k) if gate_of is not None else None
                step(nc.vector.reciprocal((coef if gate is None else inv)[:, n, :], den[:, n, :]))
                if gate is not None:
                    step(nc.vector.tensor_tensor(coef[:, n, :], inv[:, n, :], gate, ALU.mult))

            def normal(n):
                h, k, u = flat[n]
                coefficients(n)
                for i in range(NT):
                    off, w = place(u, i)
                    nc.vector.tensor_scalar(sc[:, n % SLOTS, off:off + w], sc[:, n % SLOTS, off:off + w],
                                            coef[:, n, i:i + 1], None, ALU.mult).then_inc(normed, 1)

            for n in range(min(AHEAD, N)):
                masked(n)
            normal(0)
            for n in range(N):
                if n + 1 < N:
                    normal(n + 1)
                if n + AHEAD < N:
                    masked(n + AHEAD)

        @block.scalar
        def _(act):
            def exps(n):
                h, k, u = flat[n]
                act.wait_ge(negmax, n + 1)
                for i in range(NT):
                    off, w = place(u, i)
                    nc.scalar.activation(sc[:, n % SLOTS, off:off + w], sc[:, n % SLOTS, off:off + w], ACT.Exp,
                                         bias=neg[:, n, i:i + 1], scale=1.0, accum_out=den[:, n, i:i + 1]).then_inc(exped, 1)
                if shared and n + 1 == first_of[h + 1]:
                    a, b = first_of[h], first_of[h + 1]
                    act.wait_ge(apart_done, b)
                    nc.scalar.activation(factor[:, a:b, :], apart[:, a:b, :], ACT.Exp).then_inc(factor_done, 1)

            for n in range(min(AHEAD - 1, N)):
                exps(n)
            for n in range(N):
                h, k, u = flat[n]
                where, nb = packs(u)
                for b in range(nb):
                    act.wait_ge(t_ready, banks_before[n] + b + 1)
                    if n >= 2:
                        act.wait_ge(pv_done, n - 1)
                    cols = max(col + cnt * P for bank, col, _, cnt in where.values() if bank == b)
                    nc.scalar.copy(pt[0:u["klen"], n % 2, b * S:b * S + cols], ps[0:u["klen"], 4 + b, 0:cols]).then_inc(t_kept, 1)
                if n + AHEAD - 1 < N:
                    exps(n + AHEAD - 1)
                if n + 1 == first_of[h + 1]:
                    act.wait_ge(pv_done, n + 1)
                    dst, dv0, dv = out_of(h)
                    nc.scalar.copy(dst, ps[dv0:dv0 + dv, 7, :]).then_inc(o_kept, 1)


def down(g, name, seg, src, kp, kind, l, src_chunks, then, extra=None, out=None):
    nc, ps, st = g.nc, g.ps, g.st
    ntile = src_chunks // 2
    ln = kind == "ln"
    with ExitStack() as ctx:
        sb = lambda n, s: ctx.enter_context(nc.sbuf_tensor(n, s, F32))
        sem = lambda n: nc.alloc_semaphore(f"{name}_{n}")
        sq = g.h
        rs = sb(f"{name}_rows", [P, 3, S])
        total, shift, inv = rs[:, 0, :], rs[:, 1, :], rs[:, 2, :]
        rstd = g.rstd
        sh, sl = (ctx.enter_context(nc.sbuf_tensor(f"{name}_src_{n}", [P, 4, S], F32R)) for n in ("high", "low"))
        src_high, src_low, bank_done, kept, added, sums_done, centred, squared, paired, v_step, inverse, root, scaled, x_done = (
            sem(n) for n in ("source_high", "source_low", "bank_done", "kept", "added", "sums_done", "centred", "squared",
                             "squares_paired", "vector_step", "inverse_ready", "root_ready", "scaled", "x_done"))
        pre_squared, pre_summed, turned, out_kept, out_done = (sem(n) for n in
            ("pre_squared", "pre_squares_summed", "turned", "out_kept", "out_stored"))
        block = ctx.enter_context(nc.Block())

        tokens_out = src[:, 0:CH, :].rearrange("p (t h) n -> p t (h n)", h=2) if then == "out" else None

        def pair(t, turn):
            return src[0:kp, 2 * t:2 * t + 2, :] if turn is None else src[0:kp, bass.ds(turn * (2 * RING) + 2 * t, 2), :]

        def wait_bank(eng, b):
            if b < 7:
                eng.wait_ge(bank_done, b + 1)
            else:
                eng.wait_ge(st.used, seg["start"] + ntile)

        @block.sync
        def _(sp):
            for dst, param, landed in (extra[2] if extra else []):
                sp.dma_start(dst, param).then_inc(landed, 16)
            st.feed(sp, seg)
            if then == "out":
                o = out.rearrange("b (t p) d -> p (b t) d", p=P)
                for half in range(2):
                    cols = slice(half * S, (half + 1) * S)
                    sp.wait_ge(out_kept, 4 * (half + 1))
                    sp.dma_start(o[:, :, cols], tokens_out[:, :, cols]).then_inc(out_done, 16)
                sp.wait_ge(out_done, 32)

        @block.tensor
        def _(pe):
            def tile(t, turn):
                final = turn is None and t == ntile - 1
                parts = [part[0:kp, :].rearrange("p (c n) -> p c n", c=2) for part in st.wait(pe, seg, t, turn)]
                pe.wait_ge(src_low, at(turn, 1, t) + 1)

                def product(j, b):
                    xs = [part[0:kp, 2 * (t % 2) + j, :] for part in (sh, sl)]
                    for k, (w, x) in enumerate(passes(parts, xs)):
                        last = nc.tensor.matmul(ps[:, b, :], w[:, j, b * P:(b + 1) * P], x,
                                                start=(turn is None and t == 0 and j == 0 and k == 0),
                                                stop=(final and j == 1 and k == 2), skip_group_check=True)
                    return last
                if final:
                    for b in range(8):
                        for j in range(2):
                            last = product(j, b)
                        last.then_inc(st.used if b == 7 else bank_done, 1)
                else:
                    for j in range(2):
                        for b in range(8):
                            last = product(j, b)
                    last.then_inc(st.used, 1)
            loop_tiles(pe, ntile, 1, tile)
            pe.wait_ge(added, CH - 1)
            pe.wait_ge(kept, CH if ln else 1)
            nc.tensor.matmul(ps[:, 0, :], g.mean_w[:], total, start=True, stop=True).then_inc(sums_done, 1)
            if ln:
                for c in range(4):
                    pe.wait_ge(squared, c + 1)
                    nc.tensor.matmul(ps[:, 1, :], g.mean_w[:], sq[:, c, :], start=(c == 0), stop=False)
                for n, c in enumerate((4, 6)):
                    pe.wait_ge(paired, n + 1)
                    last = nc.tensor.matmul(ps[:, 1, :], g.mean_w[:], sq[:, c, :], start=False, stop=(c == 6))
                last.then_inc(sums_done, 1)
            if then == "pre":
                for c in range(CH):
                    pe.wait_ge(pre_squared, c + 1)
                    last = nc.tensor.matmul(ps[:, 0, :], g.mean_w[:], sq[:, c, :], start=(c == 0), stop=(c == CH - 1))
                last.then_inc(pre_summed, 1)
            if then == "out":
                for c in range(CH):
                    pe.wait_ge(x_done, c + 1)
                    for t in range(NT):
                        last = nc.tensor.transpose(ps[:, c, t * P:(t + 1) * P], g.x[:, c, t * P:(t + 1) * P], g.ident[:])
                    last.then_inc(turned, 1)

        @block.vector
        def _(dve):
            steps = [0]

            def step(ins):
                steps[0] += 1
                ins.then_inc(v_step, 1)
                dve.wait_ge(v_step, steps[0])

            def low(t, turn):
                lo = 2 * (t % 2)
                dve.wait_ge(src_high, at(turn, 1, t) + 1)
                nc.vector.tensor_tensor(sl[0:kp, lo:lo + 2, :], pair(t, turn), sh[0:kp, lo:lo + 2, :].bitcast(F32),
                                        ALU.subtract).then_inc(src_low, 1)

            def tile(t, turn):
                st.next(st.take_low, dve, seg, t, turn)
                if turn is not None or t + 1 < ntile:
                    low(t + 1, turn)
                if extra and turn is None and t == 0:
                    extra[0](dve, None)

            def add(c, terms, terms_ready, done):
                dve.wait_ge(terms_ready, c + 1)
                if c > 1:
                    dve.wait_ge(done, c - 1)
                nc.vector.tensor_tensor(total, terms[:, 0, :] if c == 1 else total, terms[:, c, :], ALU.add).then_inc(done, 1)
            low(0, None)
            loop_tiles(dve, ntile, 1, tile)
            if ln:
                for c in range(CH):
                    wait_bank(dve, c)
                    nc.vector.scalar_tensor_tensor(out=g.x[:, c, :], in0=g.x[:, c, :], scalar=ALPHA, in1=ps[:, c, :],
                                                   op0=ALU.mult, op1=ALU.add).then_inc(kept, 1)
                    if c:
                        add(c, g.x, kept, added)
                dve.wait_ge(sums_done, 1)
                step(nc.vector.tensor_scalar(shift, ps[:, 0, :], 1.0 / D, None, ALU.mult))
                for c in range(CH):
                    nc.vector.tensor_tensor(g.x[:, c, :], g.x[:, c, :], shift, ALU.subtract).then_inc(centred, 1)
                for c in (4, 6):
                    dve.wait_ge(squared, c + 2)
                    nc.vector.tensor_tensor(sq[:, c, :], sq[:, c, :], sq[:, c + 1, :], ALU.add).then_inc(paired, 1)
                dve.wait_ge(sums_done, 2)
                step(nc.vector.tensor_scalar(total, ps[:, 1, :], 1.0 / D, LN_EPS, ALU.mult, ALU.add))
            else:
                dve.wait_ge(squared, 1)
                nc.vector.tensor_copy(shift, ps[:, 0, :]).then_inc(kept, 1)
                for c in range(1, CH):
                    add(c, sq, squared, added)
                dve.wait_ge(sums_done, 1)
                step(nc.vector.tensor_scalar(total, ps[:, 0, :], 1.0 / D, RMS_EPS_2, ALU.mult, ALU.add))
            nc.vector.reciprocal(inv, total).then_inc(inverse, 1)
            if ln and then == "split":
                return
            dve.wait_ge(root, 1)
            if ln:
                for c in range(CH):
                    nc.vector.scalar_tensor_tensor(out=g.x[:, c, :], in0=g.x[:, c, :], scalar=g.ln_g[:, l, c:c + 1], in1=rstd[:],
                                                   op0=ALU.mult, op1=ALU.mult).then_inc(scaled, 1)
            else:
                def residual(c):
                    dve.wait_ge(scaled, c + 1)
                    nc.vector.tensor_tensor(g.x[:, c, :], g.x[:, c, :], sq[:, c, :], ALU.add).then_inc(x_done, 1)
                for c in range(CH):
                    bank = ps[:, c, :] if c else shift
                    nc.vector.scalar_tensor_tensor(out=sq[:, c, :], in0=bank, scalar=g.norm_post[:, l, c:c + 1], in1=rstd[:],
                                                   op0=ALU.mult, op1=ALU.mult).then_inc(scaled, 1)
                    if c:
                        residual(c - 1)
                residual(CH - 1)
            if then == "pre":
                dve.wait_ge(pre_summed, 1)
                step(nc.vector.tensor_scalar(total, ps[:, 0, :], 1.0 / D, RMS_EPS_2, ALU.mult, ALU.add))
                nc.vector.reciprocal(inv, total).then_inc(inverse, 1)

        @block.scalar
        def _(act):
            def high(t, turn):
                if turn is not None or t >= 2:
                    act.wait_ge(st.used, at(turn, 1, t) + (seg["start"] - 1))
                lo = 2 * (t % 2)
                nc.scalar.copy(sh[0:kp, lo:lo + 2, :], pair(t, turn)).then_inc(src_high, 1)

            def tile(t, turn):
                st.next(st.take_high, act, seg, t, turn)
                if turn is not None or t + 1 < ntile:
                    high(t + 1, turn)
                if extra and turn is None and t == 0:
                    extra[1](act, None)
            high(0, None)
            loop_tiles(act, ntile, 1, tile)
            for c in range(CH):
                if ln:
                    act.wait_ge(centred, c + 1)
                else:
                    wait_bank(act, c)
                nc.scalar.activation(sq[:, c, :], g.x[:, c, :] if ln else ps[:, c, :], ACT.Square).then_inc(squared, 1)
            act.wait_ge(inverse, 1)
            nc.scalar.activation(rstd[:], inv, ACT.Sqrt).then_inc(root, 1)
            if then == "pre":
                for c in range(CH):
                    if ln:
                        act.wait_ge(scaled, c + 1)
                        nc.scalar.activation(g.x[:, c, :], g.x[:, c, :], ACT.Identity, bias=g.ln_b[:, l, c:c + 1], scale=1.0).then_inc(x_done, 1)
                    act.wait_ge(x_done, c + 1)
                    nc.scalar.activation(sq[:, c, :], g.x[:, c, :], ACT.Square).then_inc(pre_squared, 1)
                act.wait_ge(inverse, 2)
                nc.scalar.activation(rstd[:], inv, ACT.Sqrt).then_inc(root, 1)
            if then == "out":
                for c in range(CH):
                    act.wait_ge(turned, c + 1)
                    nc.scalar.copy(tokens_out[:, :, c * P:(c + 1) * P], ps[:, c, :].rearrange("p (t n) -> p t n", t=NT)).then_inc(out_kept, 1)


def split_normed(g, name, src, dst, gain, bias=None):
    nc = g.nc
    scaled, high_done, ready = (nc.alloc_semaphore(f"{name}_{n}") for n in ("scaled", "high_done", "parts_ready"))
    g.open_parts(name)
    high, low = g.parts

    def vector(dve):
        def take_low(c):
            dve.wait_ge(high_done, c + 1)
            if bias is None:
                last = nc.vector.tensor_tensor(low[:, c, :], dst[:, c, :], high[:, c, :].bitcast(F32), ALU.subtract)
            else:
                last = nc.vector.scalar_tensor_tensor(out=low[:, c, :], in0=dst[:, c, :], scalar=bias[:, c:c + 1],
                                                      in1=high[:, c, :].bitcast(F32), op0=ALU.add, op1=ALU.subtract)
            last.then_inc(ready, 1)
        for c in range(CH):
            nc.vector.scalar_tensor_tensor(out=dst[:, c, :], in0=src[:, c, :], scalar=gain[:, c:c + 1], in1=g.rstd[:],
                                           op0=ALU.mult, op1=ALU.mult).then_inc(scaled, 1)
            if c:
                take_low(c - 1)
        take_low(CH - 1)

    def scalar(act):
        def add_bias(c):
            act.wait_ge(ready, c + 1)
            nc.scalar.activation(dst[:, c, :], dst[:, c, :], ACT.Identity, bias=bias[:, c:c + 1], scale=1.0)
        for c in range(CH):
            act.wait_ge(scaled, c + 1)
            if bias is None:
                nc.scalar.copy(high[:, c, :], dst[:, c, :]).then_inc(high_done, 1)
            else:
                nc.scalar.activation(high[:, c, :], dst[:, c, :], ACT.Identity, bias=bias[:, c:c + 1], scale=1.0).then_inc(high_done, 1)
                if c:
                    add_bias(c - 1)
        if bias is not None:
            add_bias(CH - 1)
    return vector, scalar, ready, CH


def split_only(g, name, pairs):
    nc = g.nc
    high_done, ready = (nc.alloc_semaphore(f"{name}_{n}") for n in ("high_done", "parts_ready"))

    def vector(dve):
        for n, (x, (high, low)) in enumerate(pairs):
            dve.wait_ge(high_done, n + 1)
            nc.vector.tensor_tensor(low, x, high.bitcast(F32), ALU.subtract).then_inc(ready, 1)

    def scalar(act):
        for x, (high, low) in pairs:
            nc.scalar.copy(high, x).then_inc(high_done, 1)
    return vector, scalar, ready, len(pairs)


def layer_normed(g, l):
    return split_normed(g, f"ln{l}", g.x, g.x, g.ln_g[:, l, :], g.ln_b[:, l, :])


def pre_normed(g, l):
    return split_normed(g, f"pre{l}", g.x, g.h, g.norm_pre[:, l, :])


def ffn_up(g, l, act_t, cw, normed):
    nc, ps, st, seg = g.nc, g.ps, g.st, g.seg_up[l]
    with ExitStack() as ctx:
        sb = lambda n, s: ctx.enter_context(nc.sbuf_tensor(n, s, F32))
        sem = lambda n: nc.alloc_semaphore(n)
        conv = sb(f"ffn{l}_conv", [P, RING, S + 2])
        gel = sb(f"ffn{l}_gelu", [P, RING, S])
        n_ = f"ffn{l}_"
        par_in, done, zeroed, g_kept, t1, t2, t3, gelu_done, act_done = (sem(n_ + n) for n in
            ("params_in", "tile_done", "margins_zero", "gate_copied", "tap_1", "tap_2", "tap_3", "gelu_done", "act_done"))
        block = ctx.enter_context(nc.Block())

        @block.sync
        def _(sp):
            sp.dma_start(cw[:], g.a["f_ffn_conv"][l]).then_inc(par_in, 16)
            st.feed(sp, seg)

        @block.tensor
        def _(pe):
            def tile(t, turn):
                both = [part.rearrange("p (c s n) -> p c s n", c=CH, s=2) for part in st.wait(pe, seg, t, turn)]
                if turn is not None or t >= RING:
                    pe.wait_ge(act_done, at(turn, 1, t) - (RING - 1))

                def product(s, c):
                    for k, (w, x) in enumerate(passes(both, g.parts)):
                        last = nc.tensor.matmul(ps[:, 2 * (t % RING) + s, :], w[:, c, s, :], x[:, c, :],
                                                start=(c == 0 and k == 0), stop=(c == CH - 1 and k == 2))
                    if c == CH - 1:
                        last.then_inc(done if s else st.used, 1)
                if turn is None and t == 0:
                    for c in range(CH):
                        pe.wait_ge(normed[2], c + 1)
                        product(1, c)
                        product(0, c)
                else:
                    for s in (1, 0):
                        for c in range(CH):
                            product(s, c)
            loop_tiles(pe, FF_CH, RING, tile)

        @block.gpsimd
        def _(pool):
            pool.memset(conv[:, :, 0:2], 0.0).then_inc(zeroed, 1)

        @block.scalar
        def _(act):
            normed[1](act)
            act.wait_ge(par_in, 16)

            def tile(t, turn):
                st.next(st.take_high, act, seg, t, turn)
                act.wait_ge(done, at(turn, 1, t) + 1)
                if turn is not None or t >= RING:
                    act.wait_ge(t3, at(turn, 1, t) - (RING - 1))
                nc.scalar.copy(conv[:, t % RING, 2:S + 2], ps[:, 2 * (t % RING) + 1, :]).then_inc(g_kept, 1)
                act.wait_ge(t3, at(turn, 1, t) + 1)
                nc.scalar.activation(gel[:, t % RING, :], gel[:, t % RING, :], ACT.Gelu_apprx_tanh).then_inc(gelu_done, 1)
            loop_tiles(act, FF_CH, RING, tile)

        @block.vector
        def _(dve):
            normed[0](dve)
            dve.wait_ge(par_in, 16)
            dve.wait_ge(zeroed, 1)

            def tile(t, turn):
                f = bass.ds(at(turn, 1, t), 1)
                r = t % RING
                st.next(st.take_low, dve, seg, t, turn)
                tap = lambda k: cw[:, k, f]
                dve.wait_ge(g_kept, at(turn, 1, t) + 1)
                nc.vector.tensor_scalar(gel[:, r, :], conv[:, r, 2:S + 2], tap(2), tap(3), ALU.mult, ALU.add).then_inc(t1, 1)
                dve.wait_ge(t1, at(turn, 1, t) + 1)
                nc.vector.scalar_tensor_tensor(out=gel[:, r, :], in0=conv[:, r, 1:S + 1], scalar=tap(1), in1=gel[:, r, :],
                                               op0=ALU.mult, op1=ALU.add).then_inc(t2, 1)
                dve.wait_ge(t2, at(turn, 1, t) + 1)
                nc.vector.scalar_tensor_tensor(out=gel[:, r, :], in0=conv[:, r, 0:S], scalar=tap(0), in1=gel[:, r, :],
                                               op0=ALU.mult, op1=ALU.add).then_inc(t3, 1)
                dve.wait_ge(gelu_done, at(turn, 1, t) + 1)
                dve.wait_ge(st.used, at(turn, 1, t) + (seg["start"] + 1))
                dst = act_t[:, t, :] if turn is None else act_t[:, f, :].rearrange("p c n -> p (c n)")
                nc.vector.tensor_tensor(dst, gel[:, r, :], ps[:, 2 * r, :], ALU.mult).then_inc(act_done, 1)
            loop_tiles(dve, FF_CH, RING, tile)


def toeplitz(g, kind, col):
    base = g.rev[kind, col, :]
    return bass.AP(tensor=base.tensor, offset=base.offset, ap=[[1, P], [1, S]])


def biases(table, i, first_block=0):
    top = P * (i - first_block + 1) - 1
    return table[:, top::-1]


def causal(i):
    return list(range(i + 1))


def banded(i):
    return list(range(max(0, i - 1), i + 1))


def lambda_steps(g, neg_lam, buffers):
    nc, a = g.nc, g.a
    sb = lambda n, s: buffers.enter_context(nc.sbuf_tensor(f"lambda_{n}", s, F32))
    lp, prod = sb("params", [P, 4, A_QK]), sb("products", [P, 2, A_QK])
    dots, ex = sb("dots", [P, 2]), sb("exps", [P, 2])
    lp_in, v, e = (nc.alloc_semaphore(f"lambda_{n}") for n in ("in", "vector_step", "exp_done"))

    def vector(dve, kept):
        dve.wait_ge(lp_in, 16)
        pairs = lp[:].rearrange("p (k two) d -> p two k d", two=2)
        nc.vector.tensor_tensor(prod[:], pairs[:, 0], pairs[:, 1], ALU.mult).then_inc(v, 1)
        dve.wait_ge(v, 1)
        nc.vector.tensor_reduce(dots[:], prod[:], AX_X, ALU.add).then_inc(v, 1)
        dve.wait_ge(e, 1)
        nc.vector.tensor_tensor(dots[:, 0:1], ex[:, 1:2], ex[:, 0:1], ALU.subtract).then_inc(v, 1)
        dve.wait_ge(v, 3)
        for i in range(NT):
            nc.vector.tensor_scalar(neg_lam[:, i:i + 1], dots[:, 0:1], -LAM_INIT, None, ALU.add)

    def scalar(act, kept):
        act.wait_ge(v, 2)
        nc.scalar.activation(ex[:], dots[:], ACT.Exp).then_inc(e, 1)
    return vector, scalar, [(lp[:], a["ev_lambda"][0].partition_broadcast(P), lp_in)]


def even_mixer(g, o):
    nc, a = g.nc, g.a
    with ExitStack() as ctx:
        sb = lambda n, s: ctx.enter_context(nc.sbuf_tensor(n, s, F32))
        neg_lam, sub_g = sb("neg_lambda", [P, NT]), sb("subln_gain", [P, 1])
        with ExitStack() as inner:
            sbi = lambda n, s: inner.enter_context(nc.sbuf_tensor(n, s, F32))
            q, k, v = sbi("a_q", [P, 4, S]), sbi("a_k", [P, 4, S]), sbi("a_v", [P, NT, S])
            toe = sbi("a_tables", [P, 2, S])
            two = lambda dst, t, scale: [features(128 * j, P, 256, g.parts, [(dst[:, 2 * t + j, :], 0, P, scale, 0)]) for j in range(2)]
            plan = [two(q, t, A_QK ** -0.5) for t in range(2)] + [two(k, t, 1.0) for t in range(2)]
            plan += [[tokens(0, 256, 256, g.parts, lambda i, t=t: v[:, i, 256 * t:256 * (t + 1)])] for t in range(2)]
            tables = lambda h, s: [(toe[:, s, :], toeplitz(g, STD, h))]
            with ExitStack() as buffers:
                lam_vector, lam_scalar, load = lambda_steps(g, neg_lam, buffers)
                project(g, "a_proj", g.seg_a, plan, [(1, lam_vector)], [(1, lam_scalar)], small=load + first_tables(tables))

            def unit(h, m):
                n = m * A_HEADS + h
                lo = 64 * (n % 2)
                return {"q": q[lo:lo + 64, n // 2, :], "k": lambda kb, w: k[lo:lo + 64, n // 2, kb * P:kb * P + w],
                        "v": lambda kb: v[:, kb, h * A_V:(h + 1) * A_V], "blocks": causal, "klen": P,
                        "bias": lambda i: biases(toe[:, h % 2, :], i)}
            attention(g, "a_attn", [[unit(h, 0), unit(h, 1)] for h in range(A_HEADS)], False,
                      tables,
                      lambda h: (o[:, h, :], 0, P), gate_of=lambda h, u: neg_lam[:] if u else None)
        with ExitStack() as inner:
            sbi = lambda n, s: inner.enter_context(nc.sbuf_tensor(n, s, F32))
            q, k, v = sbi("b_q", [P, 3, 2, S]), sbi("b_k", [P, 3, 2, S]), sbi("b_v", [P, 3, NT, 256])
            toe = sbi("b_tables", [P, 2, 3, S])
            plan = []
            for i in range(N_PAIRS):
                for dst, scale in ((q, B_DIM ** -0.5), (k, 1.0)):
                    plan.append([features(128 * j, P, 256, g.parts, [(dst[:, i, j, :], 0, P, scale, 0)]) for j in range(2)])
                plan.append([tokens(0, 256, 256, g.parts, lambda t, i=i: v[:, i, t, :])])
            tables = lambda h, s: [(toe[:, s, i, :], toeplitz(g, (WIN, DIL4, DIL16)[i], A_HEADS + i * B_HEADS + h)) for i in range(N_PAIRS)]
            with nc.sbuf_tensor("subln_rows", [P, 2, A_HEADS, S], F32, side="right") as rows:
                vector_extra, scalar_extra = sub_norm(g, o, sub_g, rows)
                project(g, "b_proj", g.seg_b, plan, vector_extra, scalar_extra, small=first_tables(tables))
            g.close_parts()

            def unit(h, i):
                lo = 64 * (h % 2)
                return {"q": q[lo:lo + 64, i, h // 2, :], "k": lambda kb, w: k[lo:lo + 64, i, h // 2, kb * P:kb * P + w],
                        "v": lambda kb: v[:, i, kb, h * B_DIM:(h + 1) * B_DIM], "blocks": causal if i else banded, "klen": P,
                        "bias": lambda t: biases(toe[:, h % 2, i, :], t, 0 if i else max(0, t - 1))}
            attention(g, "b_attn", [[unit(h, i) for i in range(N_PAIRS)] for h in range(B_HEADS)], True,
                      tables,
                      lambda h: (o[64 * (h % 2):64 * (h % 2) + 64, 4 + h // 2, :], 64 * (h % 2), 64))


def sub_norm(g, o, sub_g, rows):
    nc, ps = g.nc, g.ps
    sem = lambda n: nc.alloc_semaphore(f"subln_{n}")
    gain_in, squared, summed, inverse, root = (sem(n) for n in ("gain_in", "squared", "squares_summed", "inverse_ready", "root_ready"))
    mult = 1.0 - LAM_INIT
    with ExitStack() as ctx:
        sq = ctx.enter_context(nc.sbuf_tensor("subln_squares", [P, A_HEADS, S], F32))
        block = ctx.enter_context(nc.Block())

        @block.sync
        def _(sp):
            sp.dma_start(sub_g[:, 0:1], g.a["f_subln"]).then_inc(gain_in, 16)

        @block.scalar
        def _(act):
            for h in range(A_HEADS):
                nc.scalar.activation(sq[:, h, :], o[:, h, :], ACT.Square).then_inc(squared, 1)

        @block.tensor
        def _(pe):
            for h in range(A_HEADS):
                pe.wait_ge(squared, h + 1)
                nc.tensor.matmul(ps[:, h, :], g.mean_w[:], sq[:, h, :], start=True, stop=True).then_inc(summed, 1)

        @block.vector
        def _(dve):
            for h in range(A_HEADS):
                dve.wait_ge(summed, h + 1)
                nc.vector.tensor_scalar(rows[:, 0, h, :], ps[:, h, :], 1.0 / (A_V * mult ** 2), RMS_EPS / mult ** 2, ALU.mult, ALU.add)
            dve.wait_ge(gain_in, 16)

    def scale(dve, h):
        dve.wait_ge(root, h + 1)
        nc.vector.scalar_tensor_tensor(out=o[:, h, :], in0=o[:, h, :], scalar=sub_g[:, 0:1], in1=rows[:, 0, h, :],
                                       op0=ALU.mult, op1=ALU.mult)

    def vector_step(h):
        def run(dve, kept):
            if h < A_HEADS:
                nc.vector.reciprocal(rows[:, 1, h, :], rows[:, 0, h, :]).then_inc(inverse, 1)
            if h:
                scale(dve, h - 1)
        return run

    def scalar_step(h):
        def run(act, kept):
            act.wait_ge(inverse, h + 1)
            nc.scalar.activation(rows[:, 0, h, :], rows[:, 1, h, :], ACT.Sqrt).then_inc(root, 1)
        return run
    return [(h, vector_step(h)) for h in range(A_HEADS + 1)], [(h, scalar_step(h)) for h in range(A_HEADS)]


def odd_mixer(g, o):
    normed = layer_normed(g, 1)
    nc, a, ps, st = g.nc, g.a, g.ps, g.st
    with ExitStack() as ctx:
        sb = lambda n, s, c=ctx: c.enter_context(nc.sbuf_tensor(n, s, F32))
        lora = ctx.enter_context(ExitStack())
        far = lambda n, s, dt=F32: lora.enter_context(nc.sbuf_tensor(n, s, dt))
        cq, ckv = far("cq", [P, 3, S]), far("ckv", [P, 2, S])
        raw_k = far("k_rope_raw", [96, S])
        qg, kvg = far("q_norm_gain", [P, 3]), far("kv_norm_gain", [P, 2])
        with ExitStack() as inner:
            sbi = lambda n, s: sb(n, s, inner)
            qc = sbi("c_q", [P, 4, S])
            kd = sbi("c_k", [P, 2, C_GROUPS, S])
            vd = sbi("c_v", [P, 2, NT, P])
            gate = sbi("gates", [P, NT, 24])
            w2 = sbi("cmp_w2", [P, 2, 2, C_DIM])
            kc = sbi("cmp_k", [P, C_GROUPS, CMP_BLOCKS])
            vc = sbi("cmp_v", [CMP_BLOCKS, C_GROUPS, C_DIM])
            AHEAD = 3 * P
            toe_all = sbi("c_tables", [P, 2, AHEAD + S])
            toe = toe_all[:, :, AHEAD:AHEAD + S]
            cmp_scope = inner.enter_context(ExitStack())
            kk = sb("cmp_in", [P, 2, C_GROUPS, S], cmp_scope)
            pe_t = sb("cmp_pos", [P, 2, 16], cmp_scope)

            def both_halves(dst, gr):
                return [(dst[64 * half:64 * half + 64, gr, :], 64 * gr, 64 * gr + 64, 1.0, 0) for half in range(2)]

            def shifted(s):
                return [(kk[64 * half:64 * half + 64, s, gr, 0:S - half], 64 * gr, 64 * gr + 64, 1.0, half)
                        for gr in range(2) for half in range(2)]
            plan = [[features(128 * j, P, 256, g.parts, [(qc[:, 2 * t + j, :], 0, P, C_DIM ** -0.5, 0)]) for j in range(2)] for t in range(2)]
            plan.append([features(128 * s, P, 256, g.parts, shifted(s)) for s in range(2)])
            for b in range(2):
                plan.append([features(0, P, 256, g.parts, both_halves(kd[:, b], 0) + both_halves(kd[:, b], 1)),
                             tokens(128, P, 256, g.parts, lambda i, b=b: vd[:, b, i, :])])
            plan.append([tokens(0, 24, 24, g.parts, lambda i: gate[:, i, :])])
            plan.append([features(0, P, P, g.parts, [(raw_k[64:96, :], 96, P, 1.0, 0)])])
            plan.append([features(128 * j, P, 256, g.parts, [(cq[:, j, :], 0, P, 1.0, 0)]) for j in range(2)])
            plan.append([features(0, P, 256, g.parts, [(cq[:, 2, :], 0, P, 1.0, 0)]), features(128, P, 256, g.parts, [(ckv[:, 0, :], 0, P, 1.0, 0)])])
            plan.append([features(0, P, 128, g.parts, [(ckv[:, 1, :], 0, P, 1.0, 0)])])
            tables = lambda h, s: [(toe[:, s, :], toeplitz(g, STD, h))]
            project(g, "od_proj", g.seg_od, plan, normed=normed, small=[
                (w2[:], a["od_cmp_w2"][0].rearrange("s (j p) n -> p s j n", p=P), None),
                (pe_t[:], a["f_cmp_pe"], None),
                (qg[:], a["f_q_norm"], None),
                (kvg[:], a["f_kv_norm"], None)] + first_tables(tables))
            g.close_parts()
            compress(g, kk, w2, pe_t, kc, vc, toe_all, gate, [(cq, qg), (ckv, kvg)])
            cmp_scope.close()

            def cmp_bias(i, h):
                lo = AHEAD + P * i + (P - 1) - (CMP_LEN - 1)
                stop = lo - CMP_STRIDE * CMP_BLOCKS
                return toe_all[:, h % 2, lo:(stop if stop >= 0 else None):-CMP_STRIDE]

            def units(h):
                lo, gr = 64 * (h % 2), h // 4
                q = qc[lo:lo + 64, h // 2, :]
                full = [{"q": q, "k": lambda kb, w, b=b: kd[lo:lo + 64, b, gr, kb * P:kb * P + w],
                         "v": lambda kb, b=b: vd[:, b, kb, 64 * gr:64 * gr + 64], "blocks": causal, "klen": P,
                         "bias": lambda i: biases(toe[:, h % 2, :], i)} for b in range(2)]
                cmp_ = {"q": q, "k": lambda kb, w: kc[lo:lo + 64, gr, :], "v": lambda kb: vc[:, gr, :], "blocks": lambda i: [0],
                        "klen": CMP_BLOCKS, "guard": True, "bias": lambda i: cmp_bias(i, h)}
                return [cmp_] + full
            attention(g, "c_attn", [units(h) for h in range(C_HEADS)], False,
                      tables,
                      lambda h: (o[64 * (h % 2):64 * (h % 2) + 64, h // 2, :], 64 * (h % 2), 64),
                      gate_of=lambda h, u: gate[:, :, 8 * u + h])
        cqp = [far(f"cq_{n}", [P, 3, S], F32R) for n in ("high", "low")]
        ckvp = [far(f"ckv_{n}", [P, 2, S], F32R) for n in ("high", "low")]
        qm, km, vm = (ctx.enter_context(nc.sbuf_tensor(n, shape, F32, side="right")) for n, shape in
                      (("m_q", [96, D_HEADS, S]), ("m_k", [96, D_HEADS, S]), ("m_v", [P, NT, S])))
        qr = far("q_rope", [P, 2, S])
        rot = far("rope_swap", [P, P])
        trig = far("rope_trig", [P, 4, S])
        scale = (D_NOPE + D_ROPE) ** -0.5
        plan = [[features(128 * j, P, 384, cqp, [(qm[0:64, 4 * t + 2 * j + e, :], 64 * e, 64 * e + 64, scale, 0) for e in range(2)])
                 for j in range(2)] + [features(256, P, 384, cqp, [(qr[:, t, :], 0, P, 1.0, 0)])] for t in range(2)]
        plan.append([features(128 * j, P, 512, ckvp, [(km[0:64, 2 * j + e, :], 64 * e, 64 * e + 64, 1.0, 0) for e in range(2)])
                     for j in range(4)])
        plan.append([tokens(0, 512, 512, ckvp, lambda i: vm[:, i, :])])
        mask = ctx.enter_context(nc.sbuf_tensor("m_mask", [P, 2, S], F32, side="right"))
        tables = lambda h, s: [(mask[:, s, :], toeplitz(g, STD, 16))]
        pairs = [(x[:, c, :], [p[:, c, :] for p in parts]) for x, parts in ((cq, cqp), (ckv, ckvp)) for c in range(x.shape[1])]
        project(g, "m_proj", g.seg_mla, plan, normed=split_only(g, "lora", pairs), small=[
            (rot[:], a["c_rope_swap"], None),
            (trig[:], a["c_rope_trig"].rearrange("k p t -> p k t"), None)] + first_tables(tables))
        rope(g, qm, km, raw_k, qr, rot, trig)
        lora.close()

        def unit(h):
            return {"q": qm[:, h, :], "k": lambda kb, w: km[:, h, kb * P:kb * P + w], "v": lambda kb: vm[:, kb, 64 * h:64 * h + 64],
                    "blocks": causal, "klen": P, "bias": lambda i: biases(mask[:, h % 2, :], i)}
        attention(g, "m_attn", [[unit(h)] for h in range(D_HEADS)], False,
                  tables,
                  lambda h: (o[64 * (h % 2):64 * (h % 2) + 64, 4 + h // 2, :], 64 * (h % 2), 64))


def rope(g, qm, km, raw_k, qr, rot, trig):
    nc, ps = g.nc, g.ps
    with ExitStack() as ctx:
        tmp = ctx.enter_context(nc.sbuf_tensor("rope_tmp", [P, 3, 2, S], F32))
        swapped, part, summed = (nc.alloc_semaphore(f"rope_{n}") for n in ("swapped", "part", "summed"))
        src = [(raw_k[64:96, :], km[64:96, 0, :], slice(64, 96), 0)] + [(qr[:, t, :], qr[:, t, :], slice(0, P), 2) for t in range(2)]
        block = ctx.enter_context(nc.Block())

        @block.tensor
        def _(pe):
            for n, (x, dst, rows, k) in enumerate(src):
                nc.tensor.matmul(ps[rows, n, :], rot[rows, rows], x, start=True, stop=True).then_inc(swapped, 1)

        @block.vector
        def _(dve):
            for n, (x, dst, rows, k) in enumerate(src):
                nc.vector.tensor_tensor(tmp[rows, n, 1, :], x, trig[rows, k, :], ALU.mult).then_inc(part, 1)
                dve.wait_ge(swapped, n + 1)
                nc.vector.tensor_tensor(tmp[rows, n, 0, :], ps[rows, n, :], trig[rows, k + 1, :], ALU.mult).then_inc(part, 1)
                dve.wait_ge(part, 2 * (n + 1))
                nc.vector.tensor_tensor(dst, tmp[rows, n, 0, :], tmp[rows, n, 1, :], ALU.add).then_inc(summed, 1)
            dve.wait_ge(summed, 3)
            for j in range(4):
                nc.vector.tensor_copy(qm[64:96, 4 + j, :], qr[32 * j:32 * j + 32, 1, :])

        @block.scalar
        def _(act):
            act.wait_ge(summed, 1)
            for h in range(1, D_HEADS):
                nc.scalar.copy(km[64:96, h, :], km[64:96, 0, :])
            act.wait_ge(summed, 2)
            for j in range(4):
                nc.scalar.copy(qm[64:96, j, :], qr[32 * j:32 * j + 32, 0, :])


def compress(g, kk, w2, pos, kc, vc, toe_all, gate, lora):
    nc, ps, st, seg = g.nc, g.ps, g.st, g.seg_cmp
    NB = C_GROUPS * CMP_BLOCKS
    PAIRS = CMP_LEN // 2
    with ExitStack() as ctx:
        sb = lambda n, s, dt=F32: ctx.enter_context(nc.sbuf_tensor(n, s, dt))
        sem = lambda n: nc.alloc_semaphore(n)
        zeroed, blocked, high, low, hid_done, hid_turned, turned_kept, kv_done = (sem(f"cmp_{n}") for n in
            ("zeroed", "blocks_ready", "blocks_high", "blocks_low", "hidden_ready", "hidden_turned", "turned_kept", "kv_done"))
        xb = sb("cmp_blocks", [P, PAIRS, 2, 64])
        parts = [sb(f"cmp_blocks_{n}", [P, PAIRS, 2, 64], F32R) for n in ("high", "low")]
        hid = sb("cmp_hidden", [P, CMP_HIDDEN])
        hid_t = sb("cmp_hidden_t", [P, 2, P])
        squared, summed, lora_ms, inverse, root = (sem(f"lora_{n}") for n in
            ("squared", "squares_summed", "mean_square", "inverse_ready", "root_ready"))
        sq = sb("lora_squares", [P, sum(x.shape[1] for x, _ in lora), S])
        rows = sb("lora_rows", [P, len(lora), 2, S])
        block = ctx.enter_context(nc.Block())
        QUARTER = PAIRS // 4

        @block.sync
        def _(sp):
            st.feed(sp, seg)

        @block.gpsimd
        def _(pool):
            pool.memset(xb[:, :, :, NB:64], 0.0).then_inc(zeroed, 1)
            pool.memset(toe_all[:, :, 0:toe_all.shape[2] - S], NEG)

        @block.vector
        def _(dve):
            for s in range(2):
                for gr in range(C_GROUPS):
                    for part in range(CMP_LEN // CMP_STRIDE):
                        first, n = CMP_STRIDE * part, CMP_STRIDE // 2
                        src = kk[:, s, gr, first:first + CMP_STRIDE * CMP_BLOCKS].rearrange("p (b c two) -> p c b two", c=n, two=2)
                        at_pair = pos[:, s, n * part:n * (part + 1)].unsqueeze(2).broadcast_to([P, n, CMP_BLOCKS])
                        last = nc.vector.tensor_tensor(xb[:, n * part:n * (part + 1), s, gr * CMP_BLOCKS:(gr + 1) * CMP_BLOCKS],
                                                       src[:, :, :, 0], at_pair, ALU.add)
            last.then_inc(blocked, 1)
            for q in range(4):
                dve.wait_ge(high, q + 1)
                cs = slice(QUARTER * q, QUARTER * (q + 1))
                nc.vector.tensor_tensor(parts[1][:, cs], xb[:, cs], parts[0][:, cs].bitcast(F32), ALU.subtract).then_inc(low, 1)
            for t in range(4):
                st.next(st.take_low, dve, seg, t)
            for k, (x, gain) in enumerate(lora):
                dve.wait_ge(summed, k + 1)
                nc.vector.tensor_scalar(rows[:, k, 0, :], ps[:, 4 + k, :], 1.0 / (P * x.shape[1]), RMS_EPS, ALU.mult, ALU.add).then_inc(lora_ms, 1)
                dve.wait_ge(lora_ms, k + 1)
                nc.vector.reciprocal(rows[:, k, 1, :], rows[:, k, 0, :]).then_inc(inverse, 1)
            dve.wait_ge(hid_turned, 1)
            nc.vector.tensor_copy(hid_t[:].rearrange("p j n -> p (j n)"), ps[:, 1, 0:2 * P]).then_inc(turned_kept, 1)
            for k, (x, gain) in enumerate(lora):
                dve.wait_ge(root, k + 1)
                for c in range(x.shape[1]):
                    nc.vector.scalar_tensor_tensor(out=x[:, c, :], in0=x[:, c, :], scalar=gain[:, c:c + 1], in1=rows[:, k, 0, :],
                                                   op0=ALU.mult, op1=ALU.mult)
            dve.wait_ge(kv_done, 1)
            for half in range(2):
                nc.vector.tensor_copy(kc[64 * half:64 * half + 64].rearrange("p g c -> p (g c)"), ps[0:64, 2, 0:NB])
            nc.vector.tensor_copy(vc[:].rearrange("p g c -> p (g c)"), ps[0:CMP_BLOCKS, 3, 0:P])

        @block.scalar
        def _(act):
            nc.scalar.activation(gate[:].rearrange("p i k -> p (i k)"), gate[:].rearrange("p i k -> p (i k)"), ACT.Sigmoid)
            for n, chunk in enumerate([x[:, c, :] for x, _ in lora for c in range(x.shape[1])]):
                nc.scalar.activation(sq[:, n, :], chunk, ACT.Square).then_inc(squared, 1)
            act.wait_ge(zeroed, 1)
            act.wait_ge(blocked, 1)
            for q in range(4):
                cs = slice(QUARTER * q, QUARTER * (q + 1))
                nc.scalar.copy(parts[0][:, cs], xb[:, cs]).then_inc(high, 1)
            for t in range(4):
                st.next(st.take_high, act, seg, t)
            act.wait_ge(st.used, seg["start"] + 4)
            for s in range(2):
                nc.scalar.activation(hid[64 * s:64 * s + 64, :], ps[64 * s:64 * s + 64, 0, CMP_HIDDEN * s:CMP_HIDDEN * (s + 1)],
                                     ACT.Gelu_apprx_tanh).then_inc(hid_done, 1)
            for k in range(len(lora)):
                act.wait_ge(inverse, k + 1)
                nc.scalar.activation(rows[:, k, 0, :], rows[:, k, 1, :], ACT.Sqrt).then_inc(root, 1)

        @block.tensor
        def _(pe):
            n = 0
            for k, (x, gain) in enumerate(lora):
                for c in range(x.shape[1]):
                    n += 1
                    pe.wait_ge(squared, n)
                    last = nc.tensor.matmul(ps[:, 4 + k, :], g.mean_w[:], sq[:, n - 1, :], start=(c == 0), stop=(c == x.shape[1] - 1))
                last.then_inc(summed, 1)
            for t in range(4):
                both = [part.rearrange("p (c n) -> p c n", c=QUARTER) for part in st.wait(pe, seg, t)]
                pe.wait_ge(low, t + 1)
                for cc in range(QUARTER):
                    c = QUARTER * t + cc
                    for n, (w, x) in enumerate(passes(both, parts)):
                        last = nc.tensor.matmul(ps[:, 0, :], x[:, c].rearrange("p s n -> p (s n)"), w[:, cc, :],
                                                start=(c == 0 and n == 0), stop=(c == PAIRS - 1 and n == 2))
                last.then_inc(st.used, 1)
            pe.wait_ge(hid_done, 2)
            for j in range(2):
                last = nc.tensor.transpose(ps[:, 1, j * P:(j + 1) * P], hid[:, j * P:(j + 1) * P], g.ident[:])
            last.then_inc(hid_turned, 1)
            pe.wait_ge(turned_kept, 1)
            for j in range(2):
                nc.tensor.matmul(ps[0:64, 2, 0:NB], w2[:, 0, j, :], hid_t[:, j, 0:NB], start=(j == 0), stop=(j == 1))
            for gr in range(C_GROUPS):
                for j in range(2):
                    last = nc.tensor.matmul(ps[0:CMP_BLOCKS, 3, 64 * gr:64 * gr + 64],
                                            hid_t[:, j, 64 + gr * CMP_BLOCKS:64 + (gr + 1) * CMP_BLOCKS],
                                            w2[:, 1, j, :], start=(j == 0), stop=(j == 1), skip_group_check=True)
            last.then_inc(kv_done, 1)


def decay_steps(g, par, decay, buffers):
    nc = g.nc
    sb = lambda n: buffers.enter_context(nc.sbuf_tensor(f"decay_{n}", [BW, GATES], F32))
    par_in, step_done, exp_done = (nc.alloc_semaphore(f"decay_{n}") for n in ("params_in", "step", "exp_done"))
    neg, low, u, den, inv, z, z2, series = (sb(n) for n in ("neg", "low", "u", "den", "inv", "z", "z2", "series"))
    lam = par[:, 7, :]

    def scalar(act, kept):
        act.wait_ge(step_done, 2)
        nc.scalar.activation(u[:], low[:], ACT.Exp).then_inc(exp_done, 1)

    def vector(dve, kept):
        steps = [0]

        def step(ins):
            steps[0] += 1
            ins.then_inc(step_done, 1)
            dve.wait_ge(step_done, steps[0])

        dve.wait_ge(par_in, 16)
        step(nc.vector.tensor_scalar(neg[:], lam, -1.0, None, ALU.mult))
        step(nc.vector.tensor_tensor(low[:], lam, neg[:], ALU.min))
        dve.wait_ge(exp_done, 1)
        step(nc.vector.tensor_scalar(den[:], u[:], 2.0, None, ALU.add))
        step(nc.vector.reciprocal(inv[:], den[:]))
        step(nc.vector.tensor_tensor(z[:], u[:], inv[:], ALU.mult))
        step(nc.vector.tensor_tensor(z2[:], z[:], z[:], ALU.mult))
        step(nc.vector.tensor_scalar(series[:], z2[:], 1.0 / 19, None, ALU.mult))
        for k in (17, 15, 13, 11, 9, 7, 5, 3):
            step(nc.vector.scalar_tensor_tensor(out=series[:], in0=series[:], scalar=1.0 / k, in1=z2[:], op0=ALU.add, op1=ALU.mult))
        step(nc.vector.scalar_tensor_tensor(out=series[:], in0=series[:], scalar=1.0, in1=z[:], op0=ALU.add, op1=ALU.mult))
        step(nc.vector.tensor_scalar(neg[:], neg[:], 0.0, -C_RG, ALU.max, ALU.mult))
        step(nc.vector.scalar_tensor_tensor(out=decay[:], in0=series[:], scalar=-2.0 * C_RG, in1=neg[:], op0=ALU.mult, op1=ALU.add))
    return vector, scalar, [(par[:], g.a["f_lru"], par_in)]


def rglru(g, y, par, decay, normed, buffers):
    nc, ps, st, seg, a = g.nc, g.ps, g.st, g.seg_lru, g.a
    with ExitStack() as ctx:
        sb = lambda n, s: buffers.enter_context(nc.sbuf_tensor(n, s, F32))
        sem = lambda n: nc.alloc_semaphore(n)
        pad = sb("lru_pad", [BW, 2, S + 3])
        xb = sb("lru_xb", [BW, 2, S])
        w = sb("lru_work", [BW, 2, 7, S])
        R, I, SG, A, TH, E2, GT = range(7)
        LA, IX = R, I
        zeroed = sem("lru_zeroed")
        gw = sb("lru_gate_weights", [BW, 2, 2, BW])
        gate_in = [sem(f"lru_gate_weights_in_{s}") for s in range(2)]
        pad_kept, gate_kept, xb_ready, ri_done, sig_done, la_done, exp_done = (sem(f"lru_{n}") for n in
            ("x_kept", "gate_kept", "conv_ready", "gates_done", "sigmoids_done", "log_decay_ready", "exps_done"))
        em_done, sq_done, y_done, vstep, ystep = (sem(f"lru_{n}") for n in
            ("expm1_ready", "root_done", "y_done", "conv_step", "recurrence_step"))
        block = ctx.enter_context(nc.Block())
        last_t = GATES - 1

        def powers(t, turn, act=nc.scalar):
            r = t % 2
            n = at(turn, 1, t)
            act.wait_ge(la_done, n + 1)
            nc.scalar.activation(w[:, r, A, :], w[:, r, LA, :], ACT.Exp)
            nc.scalar.activation(w[:, r, TH, :], w[:, r, LA, :], ACT.Tanh).then_inc(exp_done, 1)
            act.wait_ge(em_done, n + 1)
            nc.scalar.activation(w[:, r, E2, :], w[:, r, E2, :], ACT.Sqrt, bias=0.0, scale=-1.0).then_inc(sq_done, 1)

        def recur(t, turn, dve=nc.vector):
            r = t % 2
            n = at(turn, 1, t)
            m = at(turn, 4, t)
            dve.wait_ge(sig_done, n + 1)
            nc.vector.tensor_scalar(w[:, r, LA, :], w[:, r, R, :], decay[:, bass.ds(n, 1)], None, ALU.mult).then_inc(la_done, 1)
            nc.vector.tensor_tensor(w[:, r, IX, :], w[:, r, I, :], xb[:, r, :], ALU.mult).then_inc(ystep, 1)
            dve.wait_ge(exp_done, n + 1)
            nc.vector.tensor_tensor(w[:, r, E2, :], w[:, r, A, :], w[:, r, A, :], ALU.mult).then_inc(ystep, 1)
            dve.wait_ge(ystep, m + 2)
            nc.vector.scalar_tensor_tensor(out=w[:, r, E2, :], in0=w[:, r, E2, :], scalar=1.0, in1=w[:, r, TH, :],
                                           op0=ALU.add, op1=ALU.mult).then_inc(em_done, 1)
            dve.wait_ge(sq_done, n + 1)
            nc.vector.tensor_tensor(w[:, r, IX, :], w[:, r, IX, :], w[:, r, E2, :], ALU.mult).then_inc(ystep, 1)
            nc.vector.tensor_tensor(w[:, r, SG, :], w[:, r, SG, :], w[:, r, GT, :], ALU.mult)
            dve.wait_ge(ystep, m + 3)
            nc.vector.tensor_tensor_scan(w[:, r, TH, :], w[:, r, A, :], w[:, r, IX, :], 0.0, ALU.mult, ALU.add).then_inc(ystep, 1)
            dve.wait_ge(ystep, m + 4)
            dst = y[:, t, :] if turn is None else y[:, bass.ds(n, 1), :].rearrange("p c n -> p (c n)")
            nc.vector.tensor_tensor(dst, w[:, r, TH, :], w[:, r, SG, :], ALU.mult).then_inc(y_done, 1)

        @block.sync
        def _(sp):
            st.feed(sp, seg)

        @block.gpsimd
        def _(pool):
            pool.memset(pad[:, :, 0:3], 0.0).then_inc(zeroed, 1)

            def tile(t, turn):
                if turn is not None or t >= 2:
                    pool.wait_ge(ri_done, at(turn, 1, t) - 1)
                for s, name in enumerate(("lru_w_a_2", "lru_w_x_2")):
                    block_w = a[name][0, bass.ds(at(turn, 1, t), 1)].rearrange("t p n -> p (t n)")
                    pool.dma_start(gw[:, t % 2, s, :], block_w).then_inc(gate_in[t % 2], 16)
            loop_tiles(pool, GATES, RING, tile)

        @block.tensor
        def _(pe):
            def inputs(t, turn):
                both = [part[:, 0:CH * 2 * BW].rearrange("p (c s n) -> p c s n", c=CH, s=2) for part in st.wait(pe, seg, t, turn)]
                if turn is not None or t >= 2:
                    pe.wait_ge(gate_kept, at(turn, 1, t) - 1)

                def product(s, c):
                    for k, (wp, x) in enumerate(passes(both, g.parts)):
                        last = nc.tensor.matmul(ps[0:BW, 2 * (t % 2) + s, :], wp[:, c, s, :], x[:, c, :],
                                                start=(c == 0 and k == 0), stop=(c == CH - 1 and k == 2))
                    return last
                if turn is None and t == 0:
                    for c in range(CH):
                        pe.wait_ge(normed[2], c + 1)
                        for s in range(2):
                            last = product(s, c)
                else:
                    for s in range(2):
                        for c in range(CH):
                            last = product(s, c)
                last.then_inc(st.used, 1)

            def gates(t, turn):
                pe.wait_ge(gate_in[t % 2], 32 * (t // 2 + 1) if turn is None else turn * (16 * RING) + 32 * (t // 2 + 1))
                pe.wait_ge(xb_ready, at(turn, 1, t) + 1)
                if turn is not None or t >= 2:
                    pe.wait_ge(sig_done, at(turn, 1, t) - 1)
                for s in range(2):
                    last = nc.tensor.matmul(ps[0:BW, 4 + 2 * (t % 2) + s, :], gw[:, t % 2, s, :],
                                            xb[:, t % 2, :], start=True, stop=True)
                last.then_inc(ri_done, 1)

            def tile(t, turn):
                inputs(t, turn)
                if turn is not None or t:
                    gates(t - 1, turn)
            loop_tiles(pe, GATES, RING, tile)
            gates(last_t, None)

        @block.scalar
        def _(act):
            normed[1](act)
            act.wait_ge(zeroed, 1)

            def move(t, turn):
                act.wait_ge(st.used, at(turn, 1, t) + (seg["start"] + 1))
                if turn is not None or t >= 2:
                    act.wait_ge(xb_ready, at(turn, 1, t) - 1)
                nc.scalar.copy(pad[:, t % 2, 3:S + 3], ps[0:BW, 2 * (t % 2), :]).then_inc(pad_kept, 1)
                if turn is not None or t >= 2:
                    act.wait_ge(y_done, at(turn, 1, t) - 1)
                nc.scalar.copy(w[:, t % 2, GT, :], ps[0:BW, 2 * (t % 2) + 1, :]).then_inc(gate_kept, 1)

            def gate(t, turn):
                r = t % 2
                n = at(turn, 1, t)
                act.wait_ge(ri_done, n + 1)
                col = lambda k: par[:, k, bass.ds(n, 1)]
                nc.scalar.activation(w[:, r, R, :], ps[0:BW, 4 + 2 * r, :], ACT.Sigmoid, bias=col(5), scale=1.0)
                nc.scalar.activation(w[:, r, I, :], ps[0:BW, 5 + 2 * r, :], ACT.Sigmoid, bias=col(6), scale=1.0)
                act.wait_ge(gate_kept, n + 1)
                nc.scalar.activation(w[:, r, SG, :], w[:, r, GT, :], ACT.Sigmoid).then_inc(sig_done, 1)
                if turn is not None or t < last_t:
                    powers(t, turn)

            def tile(t, turn):
                st.next(st.take_high, act, seg, t, turn)
                move(t, turn)
                if turn is not None or t:
                    gate(t - 1, turn)
            loop_tiles(act, GATES, RING, tile)
            gate(last_t, None)

        @block.vector
        def _(dve):
            normed[0](dve)
            dve.wait_ge(zeroed, 1)

            def conv(t, turn):
                r = t % 2
                n = at(turn, 1, t)
                m = at(turn, 3, t)
                col = lambda k: par[:, k, bass.ds(n, 1)]
                dve.wait_ge(pad_kept, n + 1)
                if turn is not None or t >= 2:
                    dve.wait_ge(em_done, n - 1)
                    dve.wait_ge(ri_done, n - 1)
                nc.vector.tensor_scalar(xb[:, r, :], pad[:, r, 3:S + 3], col(3), col(4), ALU.mult, ALU.add).then_inc(vstep, 1)
                for k in (2, 1):
                    dve.wait_ge(vstep, m + (3 - k))
                    nc.vector.scalar_tensor_tensor(out=xb[:, r, :], in0=pad[:, r, k:S + k], scalar=col(k), in1=xb[:, r, :],
                                                   op0=ALU.mult, op1=ALU.add).then_inc(vstep, 1)
                dve.wait_ge(vstep, m + 3)
                nc.vector.scalar_tensor_tensor(out=xb[:, r, :], in0=pad[:, r, 0:S], scalar=col(0), in1=xb[:, r, :],
                                               op0=ALU.mult, op1=ALU.add).then_inc(xb_ready, 1)

            def tile(t, turn):
                st.next(st.take_low, dve, seg, t, turn)
                conv(t, turn)
                if turn is not None or t:
                    recur(t - 1, turn)
            loop_tiles(dve, GATES, RING, tile)

    return lambda dve, kept: recur(last_t, None, dve), lambda act, kept: powers(last_t, None, act), []


def retention(g, y, normed, buffers):
    nc, a = g.nc, g.a
    sb = lambda n, s: buffers.enter_context(nc.sbuf_tensor(n, s, F32))
    qk, v = sb("r_qk", [P, 4, S]), sb("r_v", [P, NT, R_V])
    q, k = qk[:, 0:2, :], qk[:, 2:4, :]
    gate = sb("r_gate", [P, 4, S])
    cs = sb("r_trig", [P, 2, S])
    dec = sb("r_decay", [P, S])
    tmp = sb("r_tmp", [P, 4, S])
    rotary_in = nc.alloc_semaphore("rotary_in")
    finish_head = None
    for h in range(R_HEADS):
        plan = [[features(128 * j, P, 256, g.parts, [(q[:, j, :], 0, P, 1.0, 0)]) for j in range(2)],
                [features(128 * j, P, 256, g.parts, [(k[:, j, :], 0, P, R_QK ** -0.5, 0)]) for j in range(2)]]
        plan += [[tokens(0, 256, 256, g.parts, lambda i, t=t: v[:, i, 256 * t:256 * (t + 1)])] for t in range(2)]
        plan += [[features(128 * j, P, 256, g.parts, [(gate[:, 2 * t + j, :], 0, P, 1.0, 0)]) for j in range(2)] for t in range(2)]
        turn = rotation(g, h, qk, cs, tmp, rotary_in)
        vector_extra, scalar_extra = [(2, turn)], []
        if finish_head:
            vector_extra.append((0, finish_head[0]))
            scalar_extra.append((0, finish_head[1]))
        project(g, f"ret{h}_proj", g.seg_ret[h], plan, vector_extra, scalar_extra, None if h else normed,
                [] if h else [(cs[:], a["c_rotary"].rearrange("k p t -> p k t"), rotary_in)])
        finish_head = retain(g, h, qk, v, gate, dec, tmp, y)
    return finish_head


def rotation(g, h, qk, cs, tmp, rotary_in):
    nc = g.nc
    part, turned = nc.alloc_semaphore(f"ret{h}_products"), nc.alloc_semaphore(f"ret{h}_turned")
    cos, sin = cs[:, 0, :], cs[:, 1, :]

    def turn(dve, kept):
        dve.wait_ge(rotary_in, 16)
        for by in kept:
            dve.wait_ge(by, 2)
        for n in range(2):
            x1, x2 = qk[:, 2 * n, :], qk[:, 2 * n + 1, :]
            if n:
                dve.wait_ge(turned, 2)
            for m, (x, f) in enumerate(((x1, cos), (x2, sin), (x2, cos), (x1, sin))):
                nc.vector.tensor_tensor(tmp[:, m, :], x, f, ALU.mult).then_inc(part, 1)
            dve.wait_ge(part, 4 * (n + 1))
            nc.vector.tensor_tensor(x1, tmp[:, 0, :], tmp[:, 1, :], ALU.subtract).then_inc(turned, 1)
            nc.vector.tensor_tensor(x2, tmp[:, 2, :], tmp[:, 3, :], ALU.add).then_inc(turned, 1)
    return turn


def retain(g, h, qk, v, gate, dec, tmp, y):
    nc, ps = g.nc, g.ps
    with ExitStack() as ctx:
        sem = lambda n: nc.alloc_semaphore(f"ret{h}_" + n)
        s_t, o = g.h[:, 0:NT, :], g.h[:, NT:2 * NT, :]
        sq = qk
        rs = tmp
        total = rs[:, 1, :]
        decay_in = sem("decay_in")
        added, s_done, s_kept, o_done, o_kept, mean_done, centred, squared, sq_done, vs, inverse, root, silu, normed = (sem(n) for n in
            ("added", "scores_done", "scores_kept", "values_done", "out_kept", "mean_done", "centred", "squared",
             "squares_summed", "vector_step", "inverse_ready", "root_ready", "silu_done", "normed"))
        block = ctx.enter_context(nc.Block())

        @block.sync
        def _(sp):
            sp.dma_start(dec[:], g.a["c_decay"][h]).then_inc(decay_in, 16)

        @block.vector
        def _(dve):
            dve.wait_ge(decay_in, 16)
            for kb in range(NT):
                w = S - kb * P
                dve.wait_ge(s_done, kb + 1)
                nc.vector.tensor_tensor(s_t[:, kb, 0:w], ps[:, kb, 0:w], dec[:, 0:w], ALU.mult).then_inc(s_kept, 1)
            for c in range(4):
                dve.wait_ge(o_done, c + 1)
                nc.vector.tensor_copy(o[:, c, :], ps[:, 4 + c, :]).then_inc(o_kept, 1)
                if c:
                    dve.wait_ge(o_kept, c + 1)
                    if c > 1:
                        dve.wait_ge(added, c - 1)
                    nc.vector.tensor_tensor(total, o[:, 0, :] if c == 1 else total, o[:, c, :], ALU.add).then_inc(added, 1)
            dve.wait_ge(mean_done, 1)
            nc.vector.tensor_scalar(rs[:, 0, :], ps[:, 0, :], 1.0 / R_V, None, ALU.mult).then_inc(vs, 1)
            dve.wait_ge(vs, 1)
            for c in range(4):
                nc.vector.tensor_tensor(o[:, c, :], o[:, c, :], rs[:, 0, :], ALU.subtract).then_inc(centred, 1)
            dve.wait_ge(squared, 4)
            nc.vector.tensor_tensor(sq[:, 2, :], sq[:, 2, :], sq[:, 3, :], ALU.add).then_inc(added, 1)
            dve.wait_ge(sq_done, 1)
            nc.vector.tensor_scalar(rs[:, 1, :], ps[:, 1, :], 1.0 / R_V, GN_EPS, ALU.mult, ALU.add).then_inc(vs, 1)

        @block.tensor
        def _(pe):
            for kb in range(NT):
                for c in range(2):
                    last = nc.tensor.matmul(ps[:, kb, 0:S - kb * P], qk[:, 2 + c, kb * P:(kb + 1) * P], qk[:, c, kb * P:S],
                                            start=(c == 0), stop=(c == 1))
                last.then_inc(s_done, 1)
            for c in range(4):
                for kb in range(NT):
                    pe.wait_ge(s_kept, kb + 1)
                    last = nc.tensor.matmul(ps[:, 4 + c, kb * P:S], v[:, kb, c * P:(c + 1) * P], s_t[:, kb, 0:S - kb * P],
                                            start=(kb == 0), stop=(kb == NT - 1), skip_group_check=True)
                last.then_inc(o_done, 1)
            pe.wait_ge(added, 3)
            nc.tensor.matmul(ps[:, 0, :], g.mean_w[:], total, start=True, stop=True).then_inc(mean_done, 1)
            for c in range(2):
                pe.wait_ge(squared, c + 1)
                nc.tensor.matmul(ps[:, 1, :], g.mean_w[:], sq[:, c, :], start=(c == 0), stop=False)
            pe.wait_ge(added, 4)
            nc.tensor.matmul(ps[:, 1, :], g.mean_w[:], sq[:, 2, :], start=False, stop=True).then_inc(sq_done, 1)

        @block.scalar
        def _(act):
            for c in range(4):
                nc.scalar.activation(gate[:, c, :], gate[:, c, :], ACT.Silu).then_inc(silu, 1)
            for c in range(4):
                act.wait_ge(centred, c + 1)
                nc.scalar.activation(sq[:, c, :], o[:, c, :], ACT.Square).then_inc(squared, 1)

    def finish_vector(dve, kept):
        dve.wait_ge(vs, 2)
        nc.vector.reciprocal(rs[:, 2, :], rs[:, 1, :]).then_inc(inverse, 1)
        dve.wait_ge(root, 1)
        for c in range(4):
            nc.vector.tensor_tensor(o[:, c, :], o[:, c, :], rs[:, 3, :], ALU.mult).then_inc(normed, 1)
        for c in range(4):
            dve.wait_ge(normed, c + 1)
            dve.wait_ge(silu, c + 1)
            nc.vector.tensor_tensor(y[:, 4 * h + c, :], o[:, c, :], gate[:, c, :], ALU.mult)

    def finish_scalar(act, kept):
        act.wait_ge(inverse, 1)
        nc.scalar.activation(rs[:, 3, :], rs[:, 2, :], ACT.Sqrt).then_inc(root, 1)
    return finish_vector, finish_scalar, []


def program(nc, a, out):
    with ExitStack() as ctx:
        g = Program(nc, ctx, a)
        g.plan()

        def begin():
            g.open_parts("x_tokens_in")
            start(g)

        def even():
            even_mixer(g, g.h)

        def odd():
            odd_mixer(g, g.h)

        def ffn(l, then):
            normed = layer_normed(g, 2 * l)
            with nc.sbuf_tensor(f"ffn{l}_act", [P, FF_CH, S], F32) as act_t:
                with nc.sbuf_tensor(f"ffn{l}_taps", [P, 4, FF_CH], F32) as cw:
                    ffn_up(g, l, act_t, cw, normed)
                g.close_parts()
                with ExitStack() as buffers:
                    extra = decay_steps(g, g.lru_par, g.lru_decay, buffers) if then == "pre" else None
                    down(g, f"ffn{l}_down", g.seg_down[l], act_t, P, "ln", 2 * l + 1, FF_CH, then, extra)

        def lru():
            normed = pre_normed(g, 0)
            with nc.sbuf_tensor("lru_y", [BW, GATES, S], F32) as y:
                with ExitStack() as buffers:
                    extra = rglru(g, y, g.lru_par, g.lru_decay, normed, buffers)
                    g.close_parts()
                    down(g, "lru_down", g.seg_lru_out, y, BW, "rms", 0, GATES, "pre", extra)

        def ret():
            normed = pre_normed(g, 1)
            with nc.sbuf_tensor("ret_y", [P, 16, S], F32) as y:
                with ExitStack() as buffers:
                    extra = retention(g, y, normed, buffers)
                    g.close_parts()
                    down(g, "ret_down", g.seg_ret_out, y, P, "rms", 1, 16, "out", extra, out)

        stages = [begin, even, lambda: down(g, "ev_down", g.seg_ev_out, g.h, P, "ln", 0, 6, "split"), lambda: ffn(0, "split"),
                  odd, lambda: down(g, "od_down", g.seg_od_out, g.h, P, "ln", 2, 8, "split"), lambda: ffn(1, "pre"), lru, ret]
        held = nc.snapshot_sems()
        for stage in stages:
            stage()
            nc.clear_and_free_semaphores(nc.allocated_since(held))
            nc.all_engine_barrier()


def shape_tables():
    import numpy as np
    f32 = np.float32

    def bucket(dist):
        n = np.maximum(dist, 0)
        nf = np.maximum(n, 1).astype(f32)
        large = 16 + (np.log(nf / f32(16)) / f32(math.log(2048 / 16)) * f32(16)).astype(np.int32)
        return np.where(n < 16, n, np.minimum(large, 31))

    def onehot(dist, valid):
        t = np.zeros((33, dist.size), f32)
        t[bucket(dist), np.arange(dist.size)] = 1.0
        t[:, ~valid] = 0.0
        t[32] = ~valid
        return t

    dist = np.arange(TOE) - (P - 1)
    kinds = [dist >= 0, (dist >= 0) & (dist <= 128), (dist >= 0) & (dist % 4 == 0), (dist >= 0) & (dist % 16 == 0)]
    out = {"c_ident": np.eye(P, dtype=f32),
           "c_onehot": np.stack([onehot(dist, v) for v in kinds])}
    half = D_ROPE // 2
    swap = np.zeros((D_ROPE, D_ROPE), f32)
    for i in range(half):
        swap[half + i, i] = -1.0
        swap[i, half + i] = 1.0
    pos = np.arange(S, dtype=f32)
    ang = pos[None, :] * (f32(10000.0) ** (-np.arange(half, dtype=f32) / f32(half)))[:, None]
    c, s = np.tile(np.cos(ang), (2, 1)), np.tile(np.sin(ang), (2, 1))
    sc = f32((D_NOPE + D_ROPE) ** -0.5)
    out["c_rope_swap"] = np.kron(np.eye(P // D_ROPE, dtype=f32), swap)
    out["c_rope_trig"] = np.tile(np.stack([c, s, c * sc, s * sc]), (1, P // D_ROPE, 1)).astype(f32)
    ang = pos[None, :] * (f32(10000.0) ** (-np.arange(0, R_QK, 2, dtype=f32) / f32(R_QK)))[:, None]
    out["c_rotary"] = np.stack([np.cos(ang), np.sin(ang)]).astype(f32)
    log_g = np.log(1.0 - np.exp2(-5.0 - np.arange(R_HEADS, dtype=np.float64)))
    diff = np.arange(S)[None, :] - np.arange(P)[:, None]
    out["c_decay"] = np.where(diff[None] >= 0, np.exp(np.maximum(diff, 0)[None] * log_g[:, None, None]), 0.0).astype(f32)
    return out


def arranged(inputs):
    import numpy as np
    v = {n: np.asarray(x) for n, x in inputs.items()}
    small = ("ln_g", "ln_b", "norm_pre_2", "norm_post_2", "ffn_conv_w", "ffn_conv_b", "ev_subln", "od_cmp_pe", "od_q_norm",
             "od_kv_norm", "lru_conv_w_2", "lru_conv_b_2", "lru_b_a_2", "lru_b_x_2", "lru_lambda_2")
    out = {n: x for n, x in v.items() if n not in small}

    def columns(x, p=P):
        x = x.reshape(x.shape[:-1] + (x.shape[-1] // p, p))
        return np.moveaxis(x, -1, 0)

    uq = v["od_w_uq"].reshape(1, D_Q_LORA, 2, 4, D_NOPE + D_ROPE)
    out["od_w_uq"] = np.concatenate([uq[..., :D_NOPE].reshape(1, D_Q_LORA, 2, 4 * D_NOPE),
                                     uq[..., D_NOPE:].reshape(1, D_Q_LORA, 2, 4 * D_ROPE)], axis=3).reshape(1, D_Q_LORA, -1)
    out["f_ln_g"] = columns(v["ln_g"].reshape(2 * DEPTH, D))
    out["f_ln_b"] = columns(v["ln_b"].reshape(2 * DEPTH, D))
    out["f_norm_pre"], out["f_norm_post"] = columns(v["norm_pre_2"]), columns(v["norm_post_2"])
    taps = np.concatenate([v["ffn_conv_w"], v["ffn_conv_b"][:, None]], axis=1)
    out["f_ffn_conv"] = np.stack([columns(t) for t in taps])
    out["f_subln"] = v["ev_subln"].reshape(P, 1)
    out["f_cmp_pe"] = columns(v["od_cmp_pe"][0].reshape(2, CMP_LEN * C_DIM))
    out["f_q_norm"], out["f_kv_norm"] = columns(v["od_q_norm"][0]), columns(v["od_kv_norm"][0])
    out["f_lru"] = columns(np.concatenate([v["lru_conv_w_2"][0]] + [v[n] for n in
                           ("lru_conv_b_2", "lru_b_a_2", "lru_b_x_2", "lru_lambda_2")]), BW)
    return out


def kernel(**inputs):
    import numpy as _np
    import concourse.bacc as _bacc
    from concourse import mybir as _mybir
    from concourse.bass_utils import run_bass_kernel_spmd as _run

    nc = _bacc.Bacc("TRN2", target_bir_lowering=False, num_devices=1)
    arrays, args = {}, {}
    for name, value in {**arranged(inputs), **shape_tables()}.items():
        a = _np.ascontiguousarray(value)
        arrays[f"in_{name}_dram"] = a
        args[name] = nc.dram_tensor(f"in_{name}_dram", a.shape, _mybir.dt.from_np(a.dtype), kind="ExternalInput").ap()
    out = nc.dram_tensor("out_0_dram", (1, S, D), F32, kind="ExternalOutput").ap()
    program(nc, args, out)
    r = _run(nc, [arrays], core_ids=[0])
    return r.results[0]["out_0_dram"]
```
